# Optimizing a Trainium2 kernel written in Bass

```python
import math
import jax, jax.numpy as jnp
from jax import lax
import numpy as np
import jax
import jax.numpy as jnp

D_MODEL = 1024
BATCH = 1
SEQ = 512
DEPTH = 1

CHUNK = 64
N_HEADS_A = 4
HEAD_DIM_A = 64
WIDTH_A = N_HEADS_A * 2 * HEAD_DIM_A
Q_BLOCK = 128
N_HEADS_B = 8
HEAD_DIM_B = 64
WIDTH_B = N_HEADS_B * HEAD_DIM_B
N_PREV_CHUNKS = 8
REL_CLIP = 128
IN_COLS = 3 * WIDTH_A + 3 * WIDTH_B + 2 * D_MODEL
N_EXPERTS = 32
TOP_K = 4
D_FF = 1024
SWIGLU_ALPHA = 1.702
SWIGLU_LIMIT = 7.0
EXPERT_BLOCK = 128
DEEPNORM_ALPHA = (2 * DEPTH) ** 0.25
DEEPNORM_BETA = (8 * DEPTH) ** -0.25
LN_EPS = 1e-5


def layer_norm(x, g, b):
    xf = x.astype(jnp.float32)
    mu = jnp.mean(xf, axis=-1, keepdims=True)
    var = jnp.mean(jnp.square(xf - mu), axis=-1, keepdims=True)
    y = (xf - mu) * lax.rsqrt(var + LN_EPS) * g.astype(jnp.float32) + b.astype(jnp.float32)
    return y.astype(x.dtype)

def rms_norm(x, w):
    xf = x.astype(jnp.float32)
    y = xf * lax.rsqrt(jnp.mean(jnp.square(xf), axis=-1, keepdims=True) + LN_EPS) * w.astype(jnp.float32)
    return y.astype(x.dtype)

def alibi_slopes(n):
    return jnp.asarray(np.array([2.0 ** (-8.0 * (i + 1) / n) for i in range(n)], dtype=np.float32))

def diff_attention(q, k, v, lam, lam_init, subln_w):
    B, S = q.shape[0], q.shape[1]
    scale = HEAD_DIM_A ** -0.5
    q = q.transpose(0, 2, 1, 3, 4) * scale
    k = k.transpose(0, 2, 1, 3, 4)
    v = v.transpose(0, 2, 1, 3)
    n_qb = S // Q_BLOCK
    qb = q.reshape(B, N_HEADS_A, n_qb, Q_BLOCK, 2, HEAD_DIM_A).transpose(2, 0, 1, 3, 4, 5)
    kpos = jnp.arange(S, dtype=jnp.int32)
    kchunk = kpos // CHUNK
    slopes = alibi_slopes(N_HEADS_A)

    def one_block(args):
        q_blk, i = args
        qpos = i * Q_BLOCK + jnp.arange(Q_BLOCK, dtype=jnp.int32)
        s = jnp.einsum('bhqcd,bhkcd->cbhqk', q_blk, k).astype(jnp.float32)
        dist = jnp.abs(qpos[:, None] - kpos[None, :]).astype(jnp.float32)
        bias = -slopes[:, None, None] * dist
        allowed = kchunk[None, :] <= (qpos // CHUNK)[:, None]
        p = jax.nn.softmax(jnp.where(allowed, s + bias, -jnp.inf), axis=-1)
        a = p[0] - lam * p[1]
        return jnp.einsum('bhqk,bhkd->bhqd', a.astype(v.dtype), v)

    o = lax.map(one_block, (qb, jnp.arange(n_qb, dtype=jnp.int32)))
    o = o.transpose(1, 0, 3, 2, 4).reshape(B, S, N_HEADS_A, 2 * HEAD_DIM_A)
    o = rms_norm(o, subln_w) * (1.0 - lam_init)
    return o.reshape(B, S, WIDTH_A)

def chunk_band_attention(q, k, v, rel_bias):
    B, S = q.shape[0], q.shape[1]
    n_chunks = S // CHUNK
    pad_len = N_PREV_CHUNKS * CHUNK
    band = (N_PREV_CHUNKS + 1) * CHUNK
    scale = HEAD_DIM_B ** -0.5
    q = q.transpose(0, 2, 1, 3) * scale
    kp = jnp.pad(k.transpose(0, 2, 1, 3), ((0, 0), (0, 0), (pad_len, 0), (0, 0)))
    vp = jnp.pad(v.transpose(0, 2, 1, 3), ((0, 0), (0, 0), (pad_len, 0), (0, 0)))
    qc = q.reshape(B, N_HEADS_B, n_chunks, CHUNK, HEAD_DIM_B).transpose(2, 0, 1, 3, 4)
    qi = jnp.arange(CHUNK, dtype=jnp.int32)
    kj = jnp.arange(band, dtype=jnp.int32)
    rel = (kj[None, :] - pad_len) - qi[:, None]
    bias = rel_bias.astype(jnp.float32)[:, jnp.clip(rel, -REL_CLIP, REL_CLIP) + REL_CLIP]

    def one_chunk(args):
        q_blk, c = args
        start = c * CHUNK
        kb = lax.dynamic_slice_in_dim(kp, start, band, axis=2)
        vb = lax.dynamic_slice_in_dim(vp, start, band, axis=2)
        s = jnp.einsum('bhqd,bhkd->bhqk', q_blk, kb).astype(jnp.float32) + bias
        valid = (start - pad_len + kj) >= 0
        p = jax.nn.softmax(jnp.where(valid, s, -jnp.inf), axis=-1)
        return jnp.einsum('bhqk,bhkd->bhqd', p.astype(vb.dtype), vb)

    o = lax.map(one_chunk, (qc, jnp.arange(n_chunks, dtype=jnp.int32)))
    return o.transpose(1, 0, 3, 2, 4).reshape(B, S, WIDTH_B)

def gated_mixer(h, w_in, b_gate, lam_q1, lam_k1, lam_q2, lam_k2, subln_w, rel_bias,
                w_branch_a, w_branch_b, w_out, lam_init):
    B, S, D = h.shape
    proj = h @ w_in
    o0 = 0
    qa = proj[..., o0:o0 + WIDTH_A].reshape(B, S, N_HEADS_A, 2, HEAD_DIM_A); o0 += WIDTH_A
    ka = proj[..., o0:o0 + WIDTH_A].reshape(B, S, N_HEADS_A, 2, HEAD_DIM_A); o0 += WIDTH_A
    va = proj[..., o0:o0 + WIDTH_A].reshape(B, S, N_HEADS_A, 2 * HEAD_DIM_A); o0 += WIDTH_A
    qb = proj[..., o0:o0 + WIDTH_B].reshape(B, S, N_HEADS_B, HEAD_DIM_B); o0 += WIDTH_B
    kb = proj[..., o0:o0 + WIDTH_B].reshape(B, S, N_HEADS_B, HEAD_DIM_B); o0 += WIDTH_B
    vb = proj[..., o0:o0 + WIDTH_B].reshape(B, S, N_HEADS_B, HEAD_DIM_B); o0 += WIDTH_B
    gates = jax.nn.sigmoid(proj[..., o0:] + b_gate).reshape(B, S, 2, D)

    lam = (jnp.exp(jnp.sum(lam_q1.astype(jnp.float32) * lam_k1.astype(jnp.float32)))
           - jnp.exp(jnp.sum(lam_q2.astype(jnp.float32) * lam_k2.astype(jnp.float32))) + lam_init)
    out_a = diff_attention(qa, ka, va, lam, lam_init, subln_w)
    out_b = chunk_band_attention(qb, kb, vb, rel_bias)
    merged = gates[:, :, 0] * (out_a @ w_branch_a) + gates[:, :, 1] * (out_b @ w_branch_b)
    return merged @ w_out

def moe_ffn(h, w_router, b_router, w_exp_in, b_exp_in, w_exp_out, b_exp_out):
    B, S, D = h.shape
    t = h.reshape(-1, D)
    n_tok = t.shape[0]
    logits = (t @ w_router + b_router).astype(jnp.float32)
    top_val, top_idx = lax.top_k(logits, TOP_K)
    gate_w = jax.nn.softmax(top_val, axis=-1).astype(h.dtype)

    n_slots = n_tok * TOP_K
    e_flat = top_idx.reshape(-1).astype(jnp.int32)
    tok_flat = jnp.arange(n_slots, dtype=jnp.int32) // TOP_K
    order = jnp.argsort(e_flat)
    e_sorted = e_flat[order]
    counts = jnp.bincount(e_flat, length=N_EXPERTS).astype(jnp.int32)
    padded = (counts + EXPERT_BLOCK - 1) // EXPERT_BLOCK * EXPERT_BLOCK
    start = jnp.cumsum(counts) - counts
    pend = jnp.cumsum(padded)
    pstart = pend - padded
    rank = jnp.arange(n_slots, dtype=jnp.int32) - start[e_sorted]
    dest_sorted = pstart[e_sorted] + rank
    buf_len = (-(-n_slots // EXPERT_BLOCK)) * EXPERT_BLOCK + N_EXPERTS * EXPERT_BLOCK
    n_blocks = buf_len // EXPERT_BLOCK
    buf_tok = jnp.full((buf_len,), n_tok, jnp.int32).at[dest_sorted].set(tok_flat[order])
    dest = jnp.zeros((n_slots,), jnp.int32).at[order].set(dest_sorted)
    block_start = jnp.arange(n_blocks, dtype=jnp.int32) * EXPERT_BLOCK
    block_exp = jnp.minimum(jnp.searchsorted(pend, block_start, side='right'), N_EXPERTS - 1).astype(jnp.int32)
    t_pad = jnp.concatenate([t, jnp.zeros((1, D), t.dtype)], axis=0)

    def expert_block(args):
        tok_idx, e = args
        xb = t_pad[tok_idx]
        hb = xb @ w_exp_in[e] + b_exp_in[e]
        g = jnp.minimum(hb[:, :D_FF], SWIGLU_LIMIT)
        u = jnp.clip(hb[:, D_FF:], -SWIGLU_LIMIT, SWIGLU_LIMIT)
        a = g * jax.nn.sigmoid(SWIGLU_ALPHA * g) * (u + 1.0)
        return a @ w_exp_out[e] + b_exp_out[e]

    y_buf = lax.map(expert_block, (buf_tok.reshape(n_blocks, EXPERT_BLOCK), block_exp)).reshape(buf_len, D)
    y_slot = y_buf[dest].reshape(n_tok, TOP_K, D)
    y = jnp.einsum('nk,nkd->nd', gate_w, y_slot)
    return y.reshape(B, S, D)

def first_inputs(seed: int = 0) -> dict:
    key = jax.random.key(seed)
    ks = jax.random.split(key, 24)
    L, D, E, F = DEPTH, D_MODEL, N_EXPERTS, D_FF
    nrm = lambda k, shape: jax.random.normal(k, shape, jnp.float32)
    col_scale = np.ones((IN_COLS,), np.float32)
    col_scale[2 * WIDTH_A:3 * WIDTH_A] = DEEPNORM_BETA
    col_scale[3 * WIDTH_A + 2 * WIDTH_B:3 * WIDTH_A + 3 * WIDTH_B] = DEEPNORM_BETA
    return {
        "x": nrm(ks[0], (BATCH, SEQ, D)),
        "ln_in_g": 1.0 + 0.05 * nrm(ks[1], (D,)),
        "ln_in_b": 0.02 * nrm(ks[2], (D,)),
        "w_in": nrm(ks[3], (L, D, IN_COLS)) * (D ** -0.5) * jnp.asarray(col_scale),
        "b_gate": 0.02 * nrm(ks[4], (L, 2 * D)),
        "lambda_q1": 0.1 * nrm(ks[5], (L, HEAD_DIM_A)),
        "lambda_k1": 0.1 * nrm(ks[6], (L, HEAD_DIM_A)),
        "lambda_q2": 0.1 * nrm(ks[7], (L, HEAD_DIM_A)),
        "lambda_k2": 0.1 * nrm(ks[8], (L, HEAD_DIM_A)),
        "subln_w": 1.0 + 0.05 * nrm(ks[9], (L, 2 * HEAD_DIM_A)),
        "rel_bias": 0.1 * nrm(ks[10], (L, N_HEADS_B, 2 * REL_CLIP + 1)),
        "w_branch_a": nrm(ks[11], (L, WIDTH_A, D)) * (WIDTH_A ** -0.5) * DEEPNORM_BETA,
        "w_branch_b": nrm(ks[12], (L, WIDTH_B, D)) * (WIDTH_B ** -0.5) * DEEPNORM_BETA,
        "w_out": nrm(ks[13], (L, D, D)) * (D ** -0.5) * DEEPNORM_BETA,
        "ln1_g": 1.0 + 0.05 * nrm(ks[14], (L, D)),
        "ln1_b": 0.02 * nrm(ks[15], (L, D)),
        "w_router": nrm(ks[16], (L, D, E)) * (D ** -0.5),
        "b_router": 0.01 * nrm(ks[17], (L, E)),
        "w_exp_in": nrm(ks[18], (L, E, D, 2 * F)) * (D ** -0.5) * DEEPNORM_BETA,
        "b_exp_in": 0.01 * nrm(ks[19], (L, E, 2 * F)),
        "w_exp_out": nrm(ks[20], (L, E, F, D)) * (F ** -0.5) * DEEPNORM_BETA,
        "b_exp_out": 0.01 * nrm(ks[21], (L, E, D)),
        "ln2_g": 1.0 + 0.05 * nrm(ks[22], (L, D)),
        "ln2_b": 0.02 * nrm(ks[23], (L, D)),
    }

def first_block(x, ln_in_g, ln_in_b, w_in, b_gate, lambda_q1, lambda_k1, lambda_q2, lambda_k2,
              subln_w, rel_bias, w_branch_a, w_branch_b, w_out, ln1_g, ln1_b,
              w_router, b_router, w_exp_in, b_exp_in, w_exp_out, b_exp_out, ln2_g, ln2_b):
    h = layer_norm(x, ln_in_g, ln_in_b)
    for l in range(DEPTH):
        lam_init = 0.8 - 0.6 * math.exp(-0.3 * l)
        m = gated_mixer(h, w_in[l], b_gate[l], lambda_q1[l], lambda_k1[l], lambda_q2[l], lambda_k2[l],
                        subln_w[l], rel_bias[l], w_branch_a[l], w_branch_b[l], w_out[l], lam_init)
        h = layer_norm(DEEPNORM_ALPHA * h + m, ln1_g[l], ln1_b[l])
        f = moe_ffn(h, w_router[l], b_router[l], w_exp_in[l], b_exp_in[l], w_exp_out[l], b_exp_out[l])
        h = layer_norm(DEEPNORM_ALPHA * h + f, ln2_g[l], ln2_b[l])
    return h


HEAD_DIM = D_MODEL // 16
NSA_HEADS = 6
NSA_KV_GROUPS = 2
NSA_HPG = NSA_HEADS // NSA_KV_GROUPS
CMP_BLOCK = 32
CMP_STRIDE = 16
CMP_HIDDEN = 2 * HEAD_DIM
SLC_BLOCK = 64
SLC_TOPN = 16
WINDOW = 512
NSA_QBLOCK = 64
FORCE_BONUS = 1000.0
NEG_BIG = -1e30
LB_FLOOR = 1e-30
SB_HEADS = 4
SB_QBLOCK = 128
HG_HEADS = 6
HG_KDIM = HEAD_DIM
HG_VDIM = HEAD_DIM
HG_CHUNK = 64
NUM_BUCKETS = 32
MAX_DISTANCE = 128
D_NSA = NSA_HEADS * HEAD_DIM
D_KV = NSA_KV_GROUPS * HEAD_DIM
D_SB = SB_HEADS * HEAD_DIM
D_HG = HG_HEADS * HG_VDIM
D_MIX = D_NSA + D_SB + D_HG
N_GATES = NSA_HEADS * 3
SPLIT_SIZES = (D_NSA, D_KV, D_KV, D_KV, D_KV, D_KV, D_KV, N_GATES, D_NSA,
               D_SB, D_SB, D_SB, D_SB,
               HG_HEADS * HG_KDIM, HG_HEADS * HG_KDIM, D_HG, D_HG)
D_IN = sum(SPLIT_SIZES)
ALPHA = (2 * DEPTH) ** 0.25
OUT_INIT_SCALE = (8 * DEPTH) ** -0.25
RMS_EPS = 1e-6


def t5_bucket(rel):
    n = jnp.maximum(rel, 0)
    max_exact = NUM_BUCKETS // 2
    large = max_exact + (jnp.log(jnp.maximum(n, 1).astype(jnp.float32) / max_exact)
                         / math.log(MAX_DISTANCE / max_exact)
                         * (NUM_BUCKETS - max_exact)).astype(jnp.int32)
    large = jnp.clip(large, 0, NUM_BUCKETS - 1)
    return jnp.where(n < max_exact, n, large)

def masked_softmax(s, mask):
    s = jnp.where(mask, s.astype(jnp.float32), NEG_BIG)
    p = jax.nn.softmax(s, axis=-1)
    return jnp.where(mask, p, 0.0)

def layer_norm_2(v, g, b):
    v32 = v.astype(jnp.float32)
    mu = jnp.mean(v32, axis=-1, keepdims=True)
    var = jnp.mean(jnp.square(v32 - mu), axis=-1, keepdims=True)
    return ((v32 - mu) * lax.rsqrt(var + LN_EPS) * g + b).astype(v.dtype)

def nsa_mixer(q, kc_src, vc_src, ks_src, vs_src, kw_src, vw_src, gate_logits,
              cmp_pos, w_ck1, w_ck2, w_cv1, w_cv2, rel_bias):
    B, S = q.shape[:2]
    G, HPG, dk, QB = NSA_KV_GROUPS, NSA_HPG, HEAD_DIM, NSA_QBLOCK
    scale = 1.0 / math.sqrt(dk)
    q = q.reshape(B, S, G, HPG, dk).transpose(0, 2, 3, 1, 4)
    gates = jax.nn.sigmoid(gate_logits.reshape(B, S, G, HPG, 3).transpose(0, 2, 3, 1, 4))

    n_cmp = (S - CMP_BLOCK) // CMP_STRIDE + 1
    blk_idx = np.arange(n_cmp)[:, None] * CMP_STRIDE + np.arange(CMP_BLOCK)[None, :]

    def compress(src, w1, w2):
        blocks = src.reshape(B, S, G, dk)[:, blk_idx] + cmp_pos[None, None, :, None, :]
        blocks = blocks.transpose(0, 3, 1, 2, 4).reshape(B, G, n_cmp, CMP_BLOCK * dk)
        return jax.nn.gelu(blocks @ w1) @ w2

    kc = compress(kc_src, w_ck1, w_ck2)
    vc = compress(vc_src, w_cv1, w_cv2)
    cmp_start = np.arange(n_cmp) * CMP_STRIDE
    cmp_end = jnp.asarray(cmp_start + CMP_BLOCK - 1, dtype=jnp.int32)

    n_slc = S // SLC_BLOCK
    topn = min(SLC_TOPN, n_slc)
    slc_start = np.arange(n_slc) * SLC_BLOCK
    overlap = jnp.asarray(((cmp_start[:, None] < slc_start[None, :] + SLC_BLOCK)
                           & (cmp_start[:, None] + CMP_BLOCK > slc_start[None, :])).astype(np.float32))
    ks = ks_src.reshape(B, S, G, dk).transpose(0, 2, 1, 3).reshape(B, G, n_slc, SLC_BLOCK, dk)
    vs = vs_src.reshape(B, S, G, dk).transpose(0, 2, 1, 3).reshape(B, G, n_slc, SLC_BLOCK, dk)

    pad = ((0, 0), (0, 0), (WINDOW, 0), (0, 0))
    kw = jnp.pad(kw_src.reshape(B, S, G, dk).transpose(0, 2, 1, 3), pad)
    vw = jnp.pad(vw_src.reshape(B, S, G, dk).transpose(0, 2, 1, 3), pad)

    tbl = rel_bias.reshape(NUM_BUCKETS, G, HPG)
    tbl_g = tbl.transpose(1, 0, 2)
    b_ix = jnp.arange(B)[:, None, None, None]
    g_ix = jnp.arange(G)[None, :, None, None]
    blk = jnp.arange(n_slc)

    def block(i):
        t0 = i * QB
        t = t0 + jnp.arange(QB)
        qb = lax.dynamic_slice_in_dim(q, t0, QB, axis=3)
        gb = lax.dynamic_slice_in_dim(gates, t0, QB, axis=3)

        rel_c = t[:, None] - cmp_end[None, :]
        bias_c = tbl[t5_bucket(rel_c)].transpose(2, 3, 0, 1)
        s_c = jnp.einsum('bghtd,bgnd->bghtn', qb, kc) * scale + bias_c
        p_c = masked_softmax(s_c, rel_c >= 0)
        o_c = jnp.einsum('bghtn,bgnd->bghtd', p_c.astype(vc.dtype), vc)

        imp = jnp.einsum('bghtn,nj->bgtj', p_c, overlap)
        cur = t // SLC_BLOCK
        forced = (blk[None, :] == 0) | (blk[None, :] == cur[:, None]) | (blk[None, :] == cur[:, None] - 1)
        valid = blk[None, :] * SLC_BLOCK <= t[:, None]
        score = jnp.where(valid, imp + FORCE_BONUS * forced.astype(jnp.float32), NEG_BIG)
        _, idx = lax.top_k(score, topn)
        k_sel = ks[b_ix, g_ix, idx].reshape(B, G, QB, topn * SLC_BLOCK, dk)
        v_sel = vs[b_ix, g_ix, idx].reshape(B, G, QB, topn * SLC_BLOCK, dk)
        pos = (idx[..., None] * SLC_BLOCK + jnp.arange(SLC_BLOCK)).reshape(B, G, QB, topn * SLC_BLOCK)
        rel_s = t[:, None] - pos
        bias_s = jnp.moveaxis(tbl_g[g_ix, t5_bucket(rel_s)], -1, 2)
        s_s = jnp.einsum('bghtd,bgtkd->bghtk', qb, k_sel) * scale + bias_s
        p_s = masked_softmax(s_s, (rel_s >= 0)[:, :, None])
        o_s = jnp.einsum('bghtk,bgtkd->bghtd', p_s.astype(v_sel.dtype), v_sel)

        kwb = lax.dynamic_slice_in_dim(kw, t0, WINDOW + QB, axis=2)
        vwb = lax.dynamic_slice_in_dim(vw, t0, WINDOW + QB, axis=2)
        pos_w = t0 - WINDOW + jnp.arange(WINDOW + QB)
        rel_w = t[:, None] - pos_w[None, :]
        mask_w = (rel_w >= 0) & (rel_w < WINDOW) & (pos_w[None, :] >= 0)
        bias_w = tbl[t5_bucket(rel_w)].transpose(2, 3, 0, 1)
        s_w = jnp.einsum('bghtd,bgkd->bghtk', qb, kwb) * scale + bias_w
        p_w = masked_softmax(s_w, mask_w)
        o_w = jnp.einsum('bghtk,bgkd->bghtd', p_w.astype(vwb.dtype), vwb)

        return gb[..., 0:1] * o_c + gb[..., 1:2] * o_s + gb[..., 2:3] * o_w

    o = lax.map(block, jnp.arange(S // QB))
    return o.transpose(1, 0, 4, 2, 3, 5).reshape(B, S, D_NSA)

def stick_breaking_mixer(q, k, v):
    B, S = q.shape[:2]
    H, dk, QB = SB_HEADS, HEAD_DIM, SB_QBLOCK
    scale = 1.0 / math.sqrt(dk)
    q = q.reshape(B, S, H, dk).transpose(0, 2, 1, 3)
    k = k.reshape(B, S, H, dk).transpose(0, 2, 1, 3)
    v = v.reshape(B, S, H, dk).transpose(0, 2, 1, 3)
    s_idx = jnp.arange(S)

    def block(i):
        t0 = i * QB
        t = t0 + jnp.arange(QB)
        qb = lax.dynamic_slice_in_dim(q, t0, QB, axis=2)
        z = jnp.einsum('bhtd,bhsd->bhts', qb, k).astype(jnp.float32) * scale
        mask = s_idx[None, :] < t[:, None]
        log_rest = jnp.where(mask, jax.nn.log_sigmoid(-z), 0.0)
        rcs = lax.cumsum(log_rest, axis=3, reverse=True)
        between = jnp.pad(rcs[..., 1:], ((0, 0), (0, 0), (0, 0), (0, 1)))
        log_a = jnp.where(mask, jax.nn.log_sigmoid(z) + between, 0.0)
        a = jnp.where(mask, jnp.exp(log_a), 0.0)
        return jnp.einsum('bhts,bhsd->bhtd', a.astype(v.dtype), v)

    o = lax.map(block, jnp.arange(S // QB))
    return o.transpose(1, 0, 3, 2, 4).reshape(B, S, D_SB)

def hgrn2_mixer(q, f_logit, i_val, lb):
    B, S = q.shape[:2]
    H, dk, dv, C = HG_HEADS, HG_KDIM, HG_VDIM, HG_CHUNK
    n_c = S // C
    f32 = f_logit.astype(jnp.float32)
    log_f = jnp.logaddexp(jnp.log(jnp.maximum(lb, LB_FLOOR)), jnp.log1p(-lb) + jax.nn.log_sigmoid(f32))
    key = (1.0 - lb) * jax.nn.sigmoid(-f32)

    def heads(a, d):
        return a.astype(jnp.float32).reshape(B, n_c, C, H, d).transpose(1, 0, 3, 2, 4)

    qc, kc, lfc, vc = heads(q, dk), heads(key, dk), heads(log_f, dk), heads(i_val, dv)
    causal = jnp.asarray(np.tril(np.ones((C, C), dtype=bool)))[None, None, :, :, None]

    def step(state, inp):
        qx, kx, lf, vx = inp
        b = jnp.cumsum(lf, axis=2)
        diff = b[:, :, :, None, :] - b[:, :, None, :, :]
        decay = jnp.where(causal, jnp.exp(jnp.where(causal, diff, 0.0)), 0.0)
        att = jnp.einsum('bhtd,bhsd,bhtsd->bhts', qx, kx, decay)
        o = att @ vx + jnp.einsum('bhtd,bhde->bhte', qx * jnp.exp(b), state)
        b_last = b[:, :, -1:, :]
        state = (jnp.exp(b_last[:, :, 0, :])[..., None] * state
                 + jnp.einsum('bhsd,bhse->bhde', kx * jnp.exp(b_last - b), vx))
        return state, o

    s0 = jnp.zeros((B, H, dk, dv), jnp.float32)
    _, o = lax.scan(step, s0, (qc, kc, lfc, vc))
    return o.transpose(1, 0, 3, 2, 4).reshape(B, S, H, dv)

def second_inputs(seed: int = 0) -> dict:
    key = jax.random.key(seed)
    ks = jax.random.split(key, 13)

    def nrm(k, shape, scale):
        return jax.random.normal(k, shape, jnp.float32) * scale

    x = nrm(ks[0], (BATCH, SEQ, D_MODEL), 1.0)
    w_in = nrm(ks[1], (DEPTH, D_MODEL, D_IN), D_MODEL ** -0.5)
    cmp_pos = nrm(ks[2], (DEPTH, CMP_BLOCK, HEAD_DIM), 0.1)
    w_ck1 = nrm(ks[3], (DEPTH, CMP_BLOCK * HEAD_DIM, CMP_HIDDEN), (CMP_BLOCK * HEAD_DIM) ** -0.5)
    w_ck2 = nrm(ks[4], (DEPTH, CMP_HIDDEN, HEAD_DIM), CMP_HIDDEN ** -0.5)
    w_cv1 = nrm(ks[5], (DEPTH, CMP_BLOCK * HEAD_DIM, CMP_HIDDEN), (CMP_BLOCK * HEAD_DIM) ** -0.5)
    w_cv2 = nrm(ks[6], (DEPTH, CMP_HIDDEN, HEAD_DIM), CMP_HIDDEN ** -0.5)
    hg_lb = nrm(ks[7], (DEPTH, HG_HEADS * HG_KDIM), 0.5)
    hg_norm_w = 1.0 + nrm(ks[8], (DEPTH, D_HG), 0.05)
    w_out = nrm(ks[9], (DEPTH, D_MIX, D_MODEL), D_MIX ** -0.5 * OUT_INIT_SCALE)
    ln_g = 1.0 + nrm(ks[10], (DEPTH, D_MODEL), 0.05)
    ln_b = nrm(ks[11], (DEPTH, D_MODEL), 0.02)
    rel_bias = nrm(ks[12], (NUM_BUCKETS, NSA_HEADS), 0.5)
    return {'x': x, 'w_in': w_in, 'cmp_pos': cmp_pos, 'w_ck1': w_ck1, 'w_ck2': w_ck2,
            'w_cv1': w_cv1, 'w_cv2': w_cv2, 'hg_lb': hg_lb, 'hg_norm_w': hg_norm_w,
            'w_out': w_out, 'ln_g': ln_g, 'ln_b': ln_b, 'rel_bias': rel_bias}

def second_block(x, w_in, cmp_pos, w_ck1, w_ck2, w_cv1, w_cv2, hg_lb, hg_norm_w,
              w_out, ln_g, ln_b, rel_bias):
    lb_w = jax.nn.softmax(hg_lb.astype(jnp.float32), axis=0)
    lb_all = jnp.cumsum(lb_w, axis=0) - lb_w[0]
    offsets = np.cumsum(SPLIT_SIZES)[:-1].tolist()
    for l in range(DEPTH):
        h = x @ w_in[l]
        (nsa_q, nsa_kc, nsa_vc, nsa_ks, nsa_vs, nsa_kw, nsa_vw, nsa_g, nsa_z,
         sb_q, sb_k, sb_v, sb_z, hg_q, hg_f, hg_i, hg_z) = jnp.split(h, offsets, axis=-1)
        o_nsa = nsa_mixer(nsa_q, nsa_kc, nsa_vc, nsa_ks, nsa_vs, nsa_kw, nsa_vw, nsa_g,
                          cmp_pos[l], w_ck1[l], w_ck2[l], w_cv1[l], w_cv2[l], rel_bias)
        o_sb = stick_breaking_mixer(sb_q, sb_k, sb_v)
        o_hg = hgrn2_mixer(hg_q, hg_f, hg_i, lb_all[l])
        o_hg = o_hg * lax.rsqrt(jnp.mean(jnp.square(o_hg), axis=-1, keepdims=True) + RMS_EPS)
        o_hg = (o_hg * hg_norm_w[l].reshape(HG_HEADS, HG_VDIM)).reshape(o_hg.shape[0], o_hg.shape[1], D_HG)
        mixed = jnp.concatenate([o_nsa * jax.nn.silu(nsa_z),
                                 o_sb * jax.nn.silu(sb_z),
                                 o_hg.astype(x.dtype) * jax.nn.silu(hg_z)], axis=-1)
        x = layer_norm_2(ALPHA * x + (mixed @ w_out[l]).astype(x.dtype), ln_g[l], ln_b[l])
    return x


def setup_inputs(seed=0):
    out = dict(first_inputs(seed))
    for name, value in second_inputs(seed + 1).items():
        if name != "x":
            out[name + "_2"] = value
    return out


def reference(
    x, ln_in_g, ln_in_b, w_in, b_gate, lambda_q1, lambda_k1, lambda_q2, lambda_k2, subln_w,
    rel_bias, w_branch_a, w_branch_b, w_out, ln1_g, ln1_b, w_router, b_router, w_exp_in,
    b_exp_in, w_exp_out, b_exp_out, ln2_g, ln2_b, w_in_2, cmp_pos_2, w_ck1_2, w_ck2_2, w_cv1_2,
    w_cv2_2, hg_lb_2, hg_norm_w_2, w_out_2, ln_g_2, ln_b_2, rel_bias_2,
):
    x = first_block(
        x, ln_in_g, ln_in_b, w_in, b_gate, lambda_q1, lambda_k1, lambda_q2, lambda_k2, subln_w,
        rel_bias, w_branch_a, w_branch_b, w_out, ln1_g, ln1_b, w_router, b_router, w_exp_in,
        b_exp_in, w_exp_out, b_exp_out, ln2_g, ln2_b,
    )
    return second_block(
        x, w_in_2, cmp_pos_2, w_ck1_2, w_ck2_2, w_cv1_2, w_cv2_2, hg_lb_2, hg_norm_w_2, w_out_2,
        ln_g_2, ln_b_2, rel_bias_2,
    )


_drawn_inputs = setup_inputs


def setup_inputs(seed=0):
    import zlib

    import numpy as np

    out = dict(_drawn_inputs(seed))
    spreads = {}
    factors = {'b_gate': 8.0,
     'lambda_q1': 24.477,
     'lambda_k1': 3.869,
     'lambda_q2': 4.906,
     'lambda_k2': 6.718,
     'subln_w': 5.452,
     'rel_bias': 8.0,
     'w_branch_b': 3.459,
     'b_router': 8.0,
     'b_exp_in': 8.0,
     'b_exp_out': 8.0,
     'cmp_pos_2': 8.0,
     'w_ck1_2': 5.547,
     'w_ck2_2': 5.529,
     'hg_norm_w_2': 5.943,
     'rel_bias_2': 5.089,
     'ln_b_2': 2.667}
    for name, (base, spread) in spreads.items():
        noise = np.random.default_rng([zlib.crc32(name.encode()), seed]).standard_normal(out[name].shape)
        drawn = base * np.exp(spread * noise) if base else spread * noise
        out[name] = jnp.asarray(drawn.astype(out[name].dtype))
    for name, factor in factors.items():
        out[name] = (out[name] * factor).astype(out[name].dtype)
    return out
```

```python
import concourse.bass as bass
from concourse import mybir
from contextlib import ExitStack

F32 = mybir.dt.float32
BF16 = mybir.dt.bfloat16
I32 = mybir.dt.int32
U32 = mybir.dt.uint32
ALU = mybir.AluOpType
ACT = mybir.ActivationFunctionType
AX = mybir.AxisListType
ds = bass.ds

P = 128
D = 1024
S = 512
NT = S // P
NK = D // P
NEG = -1e30
LN_EPS = 1e-5
RMS_EPS = 1e-6
ALPHA = 2.0 ** 0.25
LAM_INIT = 0.8 - 0.6
HD = 64
WA = 512
NE, TOPK, FF = 32, 4, 1024
BLOCK = 128
MAX_BLOCKS = 48
SLOTS = S * TOPK
LIMIT, SWI = 7.0, 1.702
LOG_FLOOR = -69.07755278982137

C_ID, C_GT, C_LT, C_ONE, C_IOTA, C_DIST, C_P, C_END = 0, 128, 256, 384, 512, 640, 1152, 1160
Q2, KC2, VC2, KS2, VS2, KW2, VW2, G2, Z2 = 0, 384, 512, 640, 768, 896, 1024, 1152, 1170
SBQ, SBK, SBV, SBZ = 1554, 1810, 2066, 2322
HGQ, HGF, HGI, HGZ = 2578, 2962, 3346, 3730
NSA_J = 3
N_CMP = 31
BW = 896


def column_tiles(w, first, width=P):
    return w[:, ds(first, width)].rearrange("(k p) n -> p k n", p=P)


def row_broadcast(v):
    return v.partition_broadcast(P)


class Stage:

    def __init__(self, nc, name):
        self.nc, self.name, self.stack = nc, name, ExitStack()

    def __enter__(self):
        self.stack.__enter__()
        return self

    def __exit__(self, *e):
        return self.stack.__exit__(*e)

    def sb(self, name, shape, dt=F32):
        return self.stack.enter_context(self.nc.sbuf_tensor(f"{self.name}_{name}", shape, dt))

    def sem(self, name):
        return self.stack.enter_context(self.nc.semaphore(f"{self.name}_{name}"))

    def block(self):
        return self.stack.enter_context(self.nc.Block())


class SharedSemaphores:

    def __init__(self, nc, stack, kind, names):
        self.sems = {n: stack.enter_context(nc.semaphore(f"{kind}_{n}")) for n in names}
        self.done = {n: 0 for n in names}

    def __getitem__(self, name):
        return self.sems[name]

    def counted(self, **counts):
        for name, count in counts.items():
            self.done[name] += count


NORM_SEMS = ("gain_in", "shift_in", "var_ready", "std_ready", "normed", "transposed", "copied")


def layer_norm_stage(nc, name, k, x, g_dram, b_dram, x_t=None, save=None):
    n = k.norm.done["var_ready"]
    with Stage(nc, name) as st:
        gain, shift = st.sb("gain", [P, D]), st.sb("shift", [P, D])
        stats, mv = st.sb("stats", [P, NT, 12]), st.sb("mv", [P, NT, 2])
        ve, std, r, t = (st.sb(a, [P, NT]) for a in ("ve", "std", "r", "t"))
        gain_in, shift_in, var_ready, std_ready, normed, transposed, copied = (k.norm[x] for x in NORM_SEMS)
        if save is not None:
            saved = st.sem("saved")
        block = st.block()

        @block.sync
        def _(sp):
            sp.dma_start(gain[:, :], row_broadcast(g_dram)).then_inc(gain_in, 16)
            sp.dma_start(shift[:, :], row_broadcast(b_dram)).then_inc(shift_in, 16)
            if save is not None:
                for i in range(NT):
                    sp.wait_ge(normed, n * NT + i + 1)
                    sp.dma_start(save[i * P:(i + 1) * P, :], x[:, i, :]).then_inc(saved, 16)
                sp.wait_ge(saved, 16 * NT)

        @block.vector
        def _(dve):
            for i in range(NT):
                for c in range(2):
                    nc.vector.bn_stats(stats[:, i, 6 * c:6 * c + 6], x[:, i, 512 * c:512 * c + 512])
            dve.drain()
            for i in range(NT):
                nc.vector.bn_aggr(mv[:, i, :], stats[:, i, :])
            dve.drain()
            nc.vector.tensor_scalar(ve[:, :], mv[:, :, 1], LN_EPS, None, ALU.add).then_inc(var_ready, 1)
            dve.wait_ge(std_ready, n + 1)
            nc.vector.reciprocal(r[:, :], std[:, :])
            dve.drain()
            nc.vector.tensor_tensor(t[:, :], r[:, :], r[:, :], ALU.mult)
            dve.drain()
            nc.vector.tensor_tensor(t[:, :], t[:, :], ve[:, :], ALU.mult)
            dve.drain()
            nc.vector.tensor_scalar(t[:, :], t[:, :], -0.5, 1.5, ALU.mult, ALU.add)
            dve.drain()
            nc.vector.tensor_tensor(r[:, :], r[:, :], t[:, :], ALU.mult)
            dve.drain()
            dve.wait_ge(gain_in, 16 * n + 16)
            dve.wait_ge(shift_in, 16 * n + 16)
            for i in range(NT):
                nc.vector.scalar_tensor_tensor(out=x[:, i, :], in0=x[:, i, :], scalar=mv[:, i, 0:1],
                                               in1=gain[:, :], op0=ALU.subtract, op1=ALU.mult)
                dve.drain()
                nc.vector.scalar_tensor_tensor(out=x[:, i, :], in0=x[:, i, :], scalar=r[:, i:i + 1],
                                               in1=shift[:, :], op0=ALU.mult, op1=ALU.add).then_inc(normed, 1)

        @block.scalar
        def _(act):
            act.wait_ge(var_ready, n + 1)
            nc.scalar.activation(std[:, :], ve[:, :], ACT.Sqrt).then_inc(std_ready, 1)
            if x_t is not None:
                for c in range(NK):
                    act.wait_ge(transposed, n * NK + c + 1)
                    nc.scalar.activation(x_t[:, c, :], k.bank[c % 2][:, :], ACT.Copy).then_inc(copied, 1)

        if x_t is not None:
            @block.tensor
            def _(pe):
                for c in range(NK):
                    if c >= 2:
                        pe.wait_ge(copied, n * NK + c - 1)
                    for i in range(NT):
                        if c == 0:
                            pe.wait_ge(normed, n * NT + i + 1)
                        last = nc.tensor.transpose(k.bank[c % 2][:, i * P:(i + 1) * P],
                                                   x[:, i, c * P:(c + 1) * P], k.ident)
                    last.then_inc(transposed, 1)

    k.norm.counted(var_ready=1)


def setup_stage(nc, k, A):
    with Stage(nc, "setup") as st:
        rb, wb = st.sb("rb", [8, 257]), st.sb("wb", [8, 640])
        onehot, table, wt = st.sb("onehot", [32, 512]), st.sb("table", [32, 6]), st.sb("wt", [6, 1024])
        lv, lp, lsum, lexp = (st.sb("lv", [P, 4, HD]), st.sb("lp", [P, 2, HD]), st.sb("lsum", [P, 2]),
                              st.sb("lexp", [P, 2]))
        x_in, const_in, small_in, lam_in = st.sem("x_in"), st.sem("const_in"), st.sem("small_in"), st.sem("lam_in")
        band_row, t5_ps, t5_row, stored = st.sem("band_row"), st.sem("t5_ps"), st.sem("t5_row"), st.sem("stored")
        lam_sum, lam_exp = st.sem("lam_sum"), st.sem("lam_exp")
        block = st.block()

        @block.sync
        def _(sp):
            sp.dma_start(rb[:, :], A["rel_bias"][0]).then_inc(small_in, 16)
            sp.dma_start(onehot[:, :], A["c_onehot"]).then_inc(small_in, 16)
            sp.dma_start(table[:, :], A["rel_bias_2"]).then_inc(small_in, 16)
            sp.dma_start(k.x[:, :, :], A["x"][0].rearrange("(i p) n -> p i n", p=P)).then_inc(x_in, 16)
            sp.wait_ge(band_row, 1)
            sp.dma_start(k.z_band[:, :, :], wb[:, :].unsqueeze(1).to_broadcast([8, P, 640])).then_inc(stored, 16)
            sp.wait_ge(t5_row, 1)
            sp.dma_start(k.z_t5[:, :, :], wt[:, :].unsqueeze(1).to_broadcast([6, P, 1024])).then_inc(stored, 16)
            sp.wait_ge(x_in, 16)
            sp.wait_ge(stored, 32)

        @block.scalar
        def _(act):
            act.dma_start(k.const[:, :], A["c_f32"]).then_inc(const_in, 16)
            act.dma_start(k.hg_mask[:, :], A["c_mask"]).then_inc(const_in, 16)
            for n, v in enumerate(("lambda_q1", "lambda_k1", "lambda_q2", "lambda_k2")):
                act.dma_start(lv[:, n, :], row_broadcast(A[v][0])).then_inc(lam_in, 16)
            act.wait_ge(lam_sum, 1)
            nc.scalar.activation(lexp[:, :], lsum[:, :], ACT.Exp).then_inc(lam_exp, 1)
            act.wait_ge(const_in, 32)

        @block.vector
        def _(dve):
            dve.wait_ge(small_in, 48)
            nc.vector.tensor_copy(wb[:, 0:383], rb[:, 0:1].to_broadcast([8, 383]))
            nc.vector.memset(wb[:, 639:640], 0.0)
            nc.vector.tensor_copy(wb[:, 383:639], rb[:, 0:256]).then_inc(band_row, 1)
            nc.vector.memset(wt[:, 512:1024], NEG)
            dve.wait_ge(t5_ps, 1)
            nc.vector.tensor_copy(wt[:, 0:512], k.bank[0][0:6, :]).then_inc(t5_row, 1)
            dve.wait_ge(lam_in, 64)
            nc.vector.tensor_tensor(lp[:, 0, :], lv[:, 0, :], lv[:, 1, :], ALU.mult)
            nc.vector.tensor_tensor(lp[:, 1, :], lv[:, 2, :], lv[:, 3, :], ALU.mult)
            dve.drain()
            nc.vector.tensor_reduce(lsum[:, :], lp[:, :, :], AX.X, ALU.add).then_inc(lam_sum, 1)
            dve.wait_ge(lam_exp, 1)
            nc.vector.tensor_tensor(k.neg_lam[:, :], lexp[:, 1:2], lexp[:, 0:1], ALU.subtract)
            dve.drain()
            nc.vector.tensor_scalar(k.neg_lam[:, :], k.neg_lam[:, :], -LAM_INIT, None, ALU.add)

        @block.tensor
        def _(pe):
            pe.wait_ge(small_in, 48)
            nc.tensor.matmul(k.bank[0][0:6, :], table[:, :], onehot[:, :], start=True, stop=True).then_inc(t5_ps, 1)


LOOK, NORM_LAG, COPY_LAG, PV_LAG = 3, 2, 3, 4


class Items:

    def __init__(self, tiles):
        self.tiles, self.n = tiles, len(tiles)

    def blocks(self, n):
        keys = self.tiles[n]["keys"]
        return [(j, min(P, keys - j * P)) for j in range((keys + P - 1) // P)]


ATTENTION_SEMS = ("scored", "biased", "exped", "normed", "transposed", "copied", "weighed", "out_copied")


def attention_buffers(k, st):
    b = dict(scores=st.sb("scores", [P, 4, S]), pt=st.sb("pt", [P, 3, S]), nm=st.sb("nm", [P, 4]),
             l=st.sb("l", [P, 4]), tiles_done=k.attention.done["scored"], out_done=k.attention.done["out_copied"])
    b.update((name, k.attention[name]) for name in ATTENTION_SEMS)
    return b


def attention_pe(nc, pe, k, items, b, u):
    N = items.n
    at = b["tiles_done"] + u * N
    for t in range(N + PV_LAG):
        if t < N:
            it = items.tiles[t]
            if t >= LOOK:
                pe.wait_ge(b["biased"], at + t - LOOK + 1)
            nc.tensor.matmul(k.bank[t % 3][:, 0:it["keys"]], it["q"], it["kt"], start=True, stop=True)\
                .then_inc(b["scored"], 1)
        n = t - COPY_LAG
        if 0 <= n < N:
            pe.wait_ge(b["normed"], at + n + 1)
            if n >= 2:
                pe.wait_ge(b["copied"], at + n - 1)
            for j, rows in items.blocks(n):
                last = nc.tensor.transpose(k.bank[3 + n % 2][0:rows, j * P:(j + 1) * P],
                                           b["scores"][:, n % 4, j * P:j * P + rows], k.ident)
            last.then_inc(b["transposed"], 1)
        n = t - PV_LAG
        if 0 <= n < N:
            it = items.tiles[n]
            pe.wait_ge(b["copied"], at + n + 1)
            if it["first"] and (n == 0 or items.tiles[n - 1]["i"] != it["i"]):
                pe.wait_ge(b["out_copied"], b["out_done"] + u * NT + it["i"] + 1)
            col, width = it["out"]
            blocks = items.blocks(n)
            for j, rows in blocks:
                last = nc.tensor.matmul(k.bank[5 + it["i"] % 2][:, col:col + width],
                                        b["pt"][0:rows, n % 3, j * P:(j + 1) * P], it["v"](j),
                                        start=it["first"] and j == 0, stop=it["last"] and j == len(blocks) - 1)
            last.then_inc(b["weighed"], 1)


def attention_dve(nc, dve, k, items, b, u, copy_out):
    N = items.n
    at = b["tiles_done"] + u * N
    for t in range(N + PV_LAG + 1):
        if t < N:
            it = items.tiles[t]
            s = b["scores"][:, t % 4, 0:it["keys"]]
            dve.wait_ge(b["scored"], at + t + 1)
            if t >= 4:
                dve.wait_ge(b["transposed"], at + t - 3)
            nc.vector.tensor_tensor(s, k.bank[t % 3][:, 0:it["keys"]], it["bias"](u), ALU.add)
            dve.drain()
            nc.vector.tensor_reduce(b["nm"][:, t % 4:t % 4 + 1], s, AX.X, ALU.max, negate=True)\
                .then_inc(b["biased"], 1)
        n = t - NORM_LAG
        if 0 <= n < N:
            it = items.tiles[n]
            e, l = b["scores"][:, n % 4, 0:it["keys"]], b["l"][:, n % 4:n % 4 + 1]
            dve.wait_ge(b["exped"], at + n + 1)
            nc.vector.reciprocal(l, l)
            if it["masked"]:
                nc.vector.scalar_tensor_tensor(out=e, in0=it["bias"](u), scalar=0.1 * NEG, in1=e,
                                               op0=ALU.is_gt, op1=ALU.mult)
            dve.drain()
            extra = it["scale"](u)
            if extra is None:
                nc.vector.tensor_scalar(e, e, l, None, ALU.mult).then_inc(b["normed"], 1)
            else:
                nc.vector.tensor_scalar(e, e, l, extra, ALU.mult, ALU.mult).then_inc(b["normed"], 1)
        n = t - PV_LAG - 1
        if 0 <= n < N and (n == N - 1 or items.tiles[n + 1]["i"] != items.tiles[n]["i"]):
            dve.wait_ge(b["weighed"], at + n + 1)
            copy_out(u, items.tiles[n]["i"]).then_inc(b["out_copied"], 1)


def attention_act(nc, act, k, items, b, u):
    N = items.n
    at = b["tiles_done"] + u * N
    for t in range(N + COPY_LAG):
        if t < N:
            s = b["scores"][:, t % 4, 0:items.tiles[t]["keys"]]
            act.wait_ge(b["biased"], at + t + 1)
            nc.scalar.activation(s, s, ACT.Exp, bias=b["nm"][:, t % 4:t % 4 + 1],
                                 accum_out=b["l"][:, t % 4:t % 4 + 1]).then_inc(b["exped"], 1)
        n = t - COPY_LAG
        if 0 <= n < N:
            blocks = items.blocks(n)
            rows, cols = blocks[0][1], len(blocks) * P
            act.wait_ge(b["transposed"], at + n + 1)
            if n >= 3:
                act.wait_ge(b["weighed"], at + n - 2)
            nc.scalar.activation(b["pt"][0:rows, n % 3, 0:cols], k.bank[3 + n % 2][0:rows, 0:cols],
                                 ACT.Copy).then_inc(b["copied"], 1)


def alibi_stage(nc, k, table):
    with Stage(nc, "alibi") as st:
        block = st.block()

        @block.vector
        def _(dve):
            for h in range(4):
                nc.vector.tensor_scalar(table[:, h, :], k.const[:, C_DIST:C_DIST + S], 2.0 ** (-2 * (h + 1)),
                                        None, ALU.mult)
            dve.drain()
            nc.vector.memset(table[0:HD, :, S - HD:S], NEG)


def band_bias_stage(nc, k, table):
    with Stage(nc, "bandbias") as st:
        table_in = st.sem("table_in")
        block = st.block()

        @block.sync
        def _(sp):
            skewed = bass.AP(k.z_band_handle, P - 1, [[639, P], [P * 640, 8], [1, S]])
            sp.dma_start(table[:, :, :], skewed).then_inc(table_in, 16)

        @block.vector
        def _(dve):
            dve.wait_ge(table_in, 16)
            nc.vector.memset(table[0:HD, :, S - HD:S], NEG)


def project_heads_stage(nc, name, k, w, first_q, first_k, first_v, units, bias, shared_v, scale, out):
    with Stage(nc, name) as st:
        wq, wk, wv = (st.sb(n, [P, NK, P]) for n in ("wq", "wk", "wv"))
        qt, kt, v = st.sb("qt", [P, S]), st.sb("kt", [P, S]), st.sb("v", [P, NT, P])
        b = attention_buffers(k, st)
        w_in, projected, evacuated = st.sem("w_in"), st.sem("projected"), st.sem("evacuated")
        width = P if shared_v else HD
        tiles = []
        for i in range(NT):
            for m in range(2):
                col = 0 if shared_v else HD * m
                tiles.append(dict(
                    i=i, keys=(i + 1) * P, q=qt[HD * m:HD * m + HD, i * P:(i + 1) * P],
                    kt=kt[HD * m:HD * m + HD, 0:(i + 1) * P],
                    bias=lambda u, i=i, m=m: bias(u, m, (NT - 1 - i) * P, (i + 1) * P),
                    v=lambda j, col=col: v[:, j, col:col + width], out=(col, width),
                    first=m == 0 or not shared_v, last=m == 1 or not shared_v, masked=False,
                    scale=lambda u, m=m: scale(m)))
        items = Items(tiles)
        block = st.block()

        @block.sync
        def _(sp):
            def load(u):
                for dst, first in ((wq, first_q), (wk, first_k), (wv, first_v)):
                    sp.dma_start(dst[:, :, :], column_tiles(w, first + u * P)).then_inc(w_in, 16)

            load(0)
            with sp.Fori(1, units) as u:
                sp.wait_ge(projected, u * 3)
                load(u)

        @block.tensor
        def _(pe):
            with pe.Fori(0, units) as u:
                pe.wait_ge(w_in, u * 48 + 48)
                for weights, bank in ((wq, 7), (wk, 0)):
                    for c in range(NK):
                        last = nc.tensor.matmul(k.bank[bank][:, :], weights[:, c, :], k.x_t[:, c, :],
                                                start=c == 0, stop=c == NK - 1)
                    last.then_inc(projected, 1)
                for i in range(NT):
                    for c in range(NK):
                        last = nc.tensor.matmul(k.bank[1][:, i * P:(i + 1) * P], k.x_t[:, c, i * P:(i + 1) * P],
                                                wv[:, c, :], start=c == 0, stop=c == NK - 1)
                last.then_inc(projected, 1)
                pe.wait_ge(evacuated, u * 3 + 3)
                attention_pe(nc, pe, k, items, b, u)

        @block.vector
        def _(dve):
            if b["out_done"] == 0:
                dve.drain().then_inc(b["out_copied"], 2)
            with dve.Fori(0, units) as u:
                def copy_out(u, i):
                    return nc.vector.tensor_copy(out[:, i, ds(u * P, P)], k.bank[5 + i % 2][:, 0:P])

                attention_dve(nc, dve, k, items, b, u, copy_out)

        @block.scalar
        def _(act):
            with act.Fori(0, units) as u:
                act.wait_ge(projected, u * 3 + 1)
                nc.scalar.activation(qt[:, :], k.bank[7][:, :], ACT.Copy, scale=HD ** -0.5).then_inc(evacuated, 1)
                act.wait_ge(projected, u * 3 + 2)
                nc.scalar.activation(kt[:, :], k.bank[0][:, :], ACT.Copy).then_inc(evacuated, 1)
                act.wait_ge(projected, u * 3 + 3)
                nc.scalar.activation(v[:, :, :], k.bank[1][:, :], ACT.Copy).then_inc(evacuated, 1)
                attention_act(nc, act, k, items, b, u)

    k.attention.counted(scored=units * items.n, out_copied=units * NT)


HEADS_SEMS = ("ready", "transposed", "sum_ready", "std_ready", "weight_in", "weight_ready")


def transpose_heads_stage(nc, name, k, o, o_t, heads=0, weight=None, eps=LN_EPS, factor=1.0):
    width = o.shape[2]
    tiles = width // P
    n, t0 = k.heads.done["ready"], k.heads.done["transposed"]
    with Stage(nc, name) as st:
        ready, transposed, sum_ready, std_ready, weight_in, weight_ready = (k.heads[x] for x in HEADS_SEMS)
        sq = sums = wcol = None
        if heads:
            hw = width // heads
            sq, sums, std = st.sb("sq", [P, NT, width]), st.sb("sums", [P, NT * heads]), st.sb("std", [P, NT * heads])
            wcol = st.sb("wcol", [P, weight.shape[1]])
        block = st.block()

        if heads:
            @block.sync
            def _(sp):
                with nc.allow_non_contiguous_dma(reason="a column of weights"):
                    sp.dma_start(wcol[:, :], weight).then_inc(weight_in, 16)

            @block.vector
            def _(dve):
                dve.wait_ge(weight_in, 16 * n + 16)
                nc.vector.tensor_scalar(wcol[:, :], wcol[:, :], factor, None, ALU.mult).then_inc(weight_ready, 1)
                nc.vector.tensor_tensor(sq[:, :, :], o, o, ALU.mult)
                dve.drain()
                nc.vector.tensor_reduce(sums[:, :], sq[:, :, :].rearrange("p i (h e) -> p (i h) e", e=hw),
                                        AX.X, ALU.add)
                dve.drain()
                nc.vector.tensor_scalar(sums[:, :], sums[:, :], 1.0 / hw, eps, ALU.mult, ALU.add)\
                    .then_inc(sum_ready, 1)
                dve.wait_ge(std_ready, n + 1)
                nc.vector.reciprocal(sums[:, :], std[:, :])
                dve.drain()
                o3 = o.rearrange("p i (h e) -> p (i h) e", e=hw)
                r3 = sums[:, :].unsqueeze(2).to_broadcast([P, NT * heads, hw])
                nc.vector.tensor_tensor(o3, o3, r3, ALU.mult).then_inc(ready, 1)

        @block.scalar
        def _(act):
            if heads:
                act.wait_ge(sum_ready, n + 1)
                nc.scalar.activation(std[:, :], sums[:, :], ACT.Sqrt).then_inc(std_ready, 1)
                act.wait_ge(weight_ready, n + 1)
            for c in range(tiles):
                act.wait_ge(transposed, t0 + c + 1)
                if heads:
                    w1 = wcol[:, c % wcol.shape[1]:c % wcol.shape[1] + 1]
                    nc.scalar.activation(o_t[:, c, :], k.bank[c][:, :], ACT.Copy, scale=w1)
                else:
                    nc.scalar.activation(o_t[:, c, :], k.bank[c][:, :], ACT.Copy)

        @block.tensor
        def _(pe):
            if heads:
                pe.wait_ge(ready, n + 1)
            for c in range(tiles):
                for i in range(NT):
                    last = nc.tensor.transpose(k.bank[c][:, i * P:(i + 1) * P], o[:, i, c * P:(c + 1) * P], k.ident)
                last.then_inc(transposed, 1)

    k.heads.counted(transposed=tiles, ready=1 if heads else 0)


def merge_stage(nc, k, A, oa_t, ob_t, m_t):
    with Stage(nc, "merge") as st:
        wg = st.sb("wg", [P, 2, NK, P])
        wab = st.sb("wab", [P, 2, 4, P])
        bg, bcol, sig = st.sb("bg", [P, 2, NK + 1]), st.sb("bcol", [P, 2]), st.sb("sig", [P, 2, S])
        bg_in, w_in, gates_ps, branches_ps = (st.sem(n) for n in ("bg_in", "w_in", "gates_ps", "branches_ps"))
        gates, merged, tmp = st.sem("gates"), st.sem("merged"), st.sb("tmp", [P, S])
        block = st.block()
        w_in_all = A["w_in"][0]

        @block.sync
        def _(sp):
            with nc.allow_non_contiguous_dma(reason="a column of biases"):
                for g in range(2):
                    sp.dma_start(bg[:, g, 0:NK], A["b_gate"][0][g * D:(g + 1) * D].rearrange("(k p) -> p k", p=P))\
                        .then_inc(bg_in, 16)

            def load(f):
                for g in range(2):
                    sp.dma_start(wg[:, g, :, :], column_tiles(w_in_all, 3072 + D * g + f * P)).then_inc(w_in, 16)
                    sp.dma_start(wab[:, g, :, :], column_tiles(A[("w_branch_a", "w_branch_b")[g]][0], f * P))\
                        .then_inc(w_in, 16)

            load(0)
            with sp.Fori(1, NK) as f:
                sp.wait_ge(branches_ps, f)
                load(f)

        @block.tensor
        def _(pe):
            with pe.Fori(0, NK) as f:
                pe.wait_ge(w_in, f * 64 + 64)
                pe.wait_ge(gates, f * 2 + 1)
                for g in range(2):
                    for c in range(NK):
                        last = nc.tensor.matmul(k.bank[g][:, :], wg[:, g, c, :], k.x_t[:, c, :],
                                                start=c == 0, stop=c == NK - 1)
                    last.then_inc(gates_ps, 1)
                pe.wait_ge(merged, f + 1)
                for g, o_t in enumerate((oa_t, ob_t)):
                    for c in range(4):
                        last = nc.tensor.matmul(k.bank[2 + g][:, :], wab[:, g, c, :], o_t[:, c, :],
                                                start=c == 0, stop=c == 3)
                last.then_inc(branches_ps, 1)

        @block.scalar
        def _(act):
            act.drain().then_inc(gates, 1)
            with act.Fori(0, NK) as f:
                act.wait_ge(merged, f + 1)
                for g in range(2):
                    act.wait_ge(gates_ps, f * 2 + g + 1)
                    nc.scalar.activation(sig[:, g, :], k.bank[g][:, :], ACT.Sigmoid, bias=bcol[:, g:g + 1])\
                        .then_inc(gates, 1)

        @block.vector
        def _(dve):
            nc.vector.memset(bg[:, :, NK:NK + 1], 0.0)
            dve.wait_ge(bg_in, 32)
            nc.vector.tensor_copy(bcol[:, :], bg[:, :, 0])
            dve.drain().then_inc(merged, 1)
            with dve.Fori(0, NK) as f:
                dve.wait_ge(branches_ps, f + 1)
                dve.wait_ge(gates, f * 2 + 3)
                nc.vector.tensor_tensor(tmp[:, :], sig[:, 0, :], k.bank[2][:, :], ALU.mult)
                nc.vector.tensor_tensor(sig[:, 1, :], sig[:, 1, :], k.bank[3][:, :], ALU.mult)
                dve.drain()
                nc.vector.tensor_tensor(m_t[:, ds(f, 1), :], tmp[:, :].unsqueeze(1), sig[:, 1, :].unsqueeze(1),
                                        ALU.add)
                nc.vector.tensor_copy(bcol[:, :].unsqueeze(2), bg[:, :, ds(f + 1, 1)])
                dve.drain().then_inc(merged, 1)


def output_stage(nc, name, k, w_dram, m_t, x):
    o = k.output.done["w0_in"]
    with Stage(nc, name) as st:
        w = st.sb("w", [P, 2, NK, 512])
        w_in = [k.output["w0_in"], k.output["w1_in"]]
        product, added = k.output["product"], k.output["added"]
        block = st.block()

        @block.sync
        def _(sp):
            for c in range(2):
                sp.dma_start(w[:, c, :, :], column_tiles(w_dram, 512 * c, 512)).then_inc(w_in[c], 16)

        @block.tensor
        def _(pe):
            for c in range(2):
                pe.wait_ge(w_in[c], 16 * o + 16)
                for i in range(NT):
                    n = c * NT + i
                    if n >= 4:
                        pe.wait_ge(added, 2 * NT * o + n - 3)
                    for t in range(NK):
                        last = nc.tensor.matmul(k.bank[n % 4][:, :], m_t[:, t, i * P:(i + 1) * P], w[:, c, t, :],
                                                start=t == 0, stop=t == NK - 1)
                    last.then_inc(product, 1)

        @block.vector
        def _(dve):
            for c in range(2):
                for i in range(NT):
                    n = c * NT + i
                    xs = x[:, i, 512 * c:512 * c + 512]
                    dve.wait_ge(product, 2 * NT * o + n + 1)
                    nc.vector.scalar_tensor_tensor(out=xs, in0=xs, scalar=ALPHA, in1=k.bank[n % 4][:, :],
                                                   op0=ALU.mult, op1=ALU.add).then_inc(added, 1)

    k.output.counted(w0_in=1)


def route_stage(nc, k, A, r):
    with Stage(nc, "route") as st:
        wr, br = st.sb("wr", [P, NK, NE]), st.sb("br", [P, NE])
        logits, top, idx = st.sb("logits", [P, NT, NE]), st.sb("top", [P, NT, 8]), st.sb("idx", [P, NT, 8], U32)
        idxf, nmax, wsum = st.sb("idxf", [P, NT, 8]), st.sb("nmax", [P, NT]), st.sb("wsum", [P, NT])
        pick = st.sb("pick", [P, NT, TOPK, NE])
        chosen = st.sb("chosen", [P, NT, NE])
        counts, nb, ends = st.sb("counts", [P, NE]), st.sb("nb", [P, NE]), st.sb("ends", [P, NE])
        step, starts, zero = st.sb("step", [P, NE]), st.sb("starts", [P, NE]), st.sb("zero", [P, NE])
        dest, picked = st.sb("dest", [P, NT, NE]), st.sb("picked", [P, NT, TOPK, NE])
        destk = st.sb("destk", [P, NT * TOPK])
        desti, lane_i, blk_i = (st.sb(n, [P, NT * TOPK], I32) for n in ("desti", "lane_i", "blk_i"))
        lane_f, blk_f = st.sb("lane_f", [P, NT * TOPK]), st.sb("blk_f", [P, NT * TOPK])
        slot_no = st.sb("slot_no", [P, NT * TOPK])
        lane_hot, blk_hot = st.sb("lane_hot", [P, 16, P]), st.sb("blk_hot", [P, 16, MAX_BLOCKS])
        before = st.sb("before", [P, MAX_BLOCKS, NE])
        slots, token, row, isnone = (st.sb(n, [P, MAX_BLOCKS]) for n in ("slots", "token", "row", "isnone"))
        token_i = st.sb("token_i", [P, MAX_BLOCKS], I32)
        w_in, logits_ps, logits_sb = st.sem("w_in"), st.sem("logits_ps"), st.sem("logits_sb")
        exped, weights, chosen_ready, counted = (st.sem(n) for n in ("exped", "weights", "chosen_ready", "counted"))
        slot_ready, hot, listed = st.sem("slot_ready"), st.sem("hot"), st.sem("listed")
        top_ready = st.sem("top_ready")
        block = st.block()

        @block.sync
        def _(sp):
            sp.dma_start(wr[:, :, :], A["w_router"][0].rearrange("(k p) n -> p k n", p=P)).then_inc(w_in, 16)
            sp.dma_start(br[:, :], row_broadcast(A["b_router"][0])).then_inc(w_in, 16)

        @block.gpsimd
        def _(pool):
            nc.gpsimd.iota(slot_no[:, :], pattern=[[P * TOPK, NT], [1, TOPK]], base=1, channel_multiplier=TOPK,
                           allow_small_or_imprecise_dtypes=True).then_inc(slot_ready, 1)

        @block.tensor
        def _(pe):
            pe.wait_ge(w_in, 32)
            for i in range(NT):
                for c in range(NK):
                    last = nc.tensor.matmul(k.bank[i][:, 0:NE], k.x_t[:, c, i * P:(i + 1) * P], wr[:, c, :],
                                            start=c == 0, stop=c == NK - 1)
                last.then_inc(logits_ps, 1)
            pe.wait_ge(chosen_ready, 1)
            for i in range(NT):
                nc.tensor.matmul(k.bank[4][:, 0:NE], k.const[:, C_ONE:C_ONE + P], chosen[:, i, :],
                                 start=i == 0, stop=i == NT - 1)
            for i in range(NT):
                for h in range(i + 1):
                    earlier = C_LT if h == i else C_ONE
                    last = nc.tensor.matmul(k.bank[i][:, 0:NE], k.const[:, earlier:earlier + P], chosen[:, h, :],
                                            start=h == 0, stop=h == i)
            last.then_inc(counted, 1)
            pe.wait_ge(hot, 1)
            for n in range(16):
                last = nc.tensor.matmul(k.bank[5][:, 0:MAX_BLOCKS], lane_hot[:, n, :], blk_hot[:, n, :],
                                        start=n == 0, stop=n == 15)
            last.then_inc(listed, 1)

        @block.scalar
        def _(act):
            act.wait_ge(top_ready, 1)
            for i in range(NT):
                last = nc.scalar.activation(r.weight[:, i, :], top[:, i, 0:TOPK], ACT.Exp, bias=nmax[:, i:i + 1],
                                            accum_out=wsum[:, i:i + 1])
            last.then_inc(exped, 1)

        @block.vector
        def _(dve):
            dve.wait_ge(w_in, 32)
            for i in range(NT):
                dve.wait_ge(logits_ps, i + 1)
                nc.vector.tensor_tensor(logits[:, i, :], k.bank[i][:, 0:NE], br[:, :], ALU.add)
            dve.drain()
            for i in range(NT):
                nc.vector.max(top[:, i, :], logits[:, i, :])
            dve.drain()
            for i in range(NT):
                nc.vector.max_index(idx[:, i, :], top[:, i, :], logits[:, i, :])
            nc.vector.tensor_scalar(nmax[:, :], top[:, :, 0], -1.0, None, ALU.mult).then_inc(top_ready, 1)
            dve.drain()
            nc.vector.tensor_copy(idxf[:, :, :], idx[:, :, :])
            dve.drain()
            for i in range(NT):
                for c in range(TOPK):
                    nc.vector.tensor_scalar(pick[:, i, c, :], k.const[:, C_IOTA:C_IOTA + NE], idxf[:, i, c:c + 1],
                                            None, ALU.is_equal)
            dve.drain()
            nc.vector.tensor_reduce(chosen[:, :, :], pick[:, :, :, :].rearrange("p i c e -> p i e c"), AX.X, ALU.add)\
                .then_inc(chosen_ready, 1)
            nc.vector.memset(zero[:, :], 0.0)
            dve.wait_ge(exped, 1)
            nc.vector.reciprocal(wsum[:, :], wsum[:, :])
            dve.drain()
            nc.vector.tensor_tensor(r.weight[:, :, :], r.weight[:, :, :],
                                    wsum[:, :].unsqueeze(2).to_broadcast([P, NT, TOPK]), ALU.mult)
            dve.wait_ge(counted, 1)
            nc.vector.tensor_copy(counts[:, :], k.bank[4][:, 0:NE])
            dve.drain()
            nc.vector.tensor_scalar(nb[:, :], counts[:, :], 0.0, None, ALU.is_gt)
            dve.drain()
            for n in range(1, S // BLOCK):
                nc.vector.scalar_tensor_tensor(out=nb[:, :], in0=counts[:, :], scalar=float(n * BLOCK), in1=nb[:, :],
                                               op0=ALU.is_gt, op1=ALU.add)
                dve.drain()
            nc.vector.tensor_tensor_scan(ends[:, :], nb[:, :], zero[:, :], 0.0, ALU.add, ALU.add)
            dve.drain()
            nc.vector.tensor_tensor(starts[:, :], ends[:, :], nb[:, :], ALU.subtract)
            nc.vector.tensor_tensor(before[:, :, :],
                                    k.const[:, C_IOTA:C_IOTA + MAX_BLOCKS].unsqueeze(2).to_broadcast([P, MAX_BLOCKS, NE]),
                                    ends[:, :].unsqueeze(1).to_broadcast([P, MAX_BLOCKS, NE]), ALU.is_ge)
            dve.drain()
            nc.vector.tensor_reduce(r.expert[:, :], before[:, :, :], AX.X, ALU.add)
            nc.vector.tensor_scalar(starts[:, :], starts[:, :], float(BLOCK), None, ALU.mult)
            dve.drain()
            nc.vector.tensor_copy(r.expert_i[:, 0:MAX_BLOCKS], r.expert[:, :])
            nc.vector.tensor_copy(r.expert_i[:, MAX_BLOCKS:MAX_BLOCKS + 1], ends[:, NE - 1:NE])
            for i in range(NT):
                nc.vector.tensor_tensor(dest[:, i, :], k.bank[i][:, 0:NE], starts[:, :], ALU.add)
            dve.drain()
            nc.vector.tensor_tensor(picked[:, :, :, :], pick[:, :, :, :],
                                    dest[:, :, :].unsqueeze(2).to_broadcast([P, NT, TOPK, NE]), ALU.mult)
            dve.drain()
            nc.vector.tensor_reduce(destk[:, :], picked[:, :, :, :].rearrange("p i c e -> p (i c) e"), AX.X, ALU.add)
            dve.drain()
            nc.vector.tensor_copy(desti[:, :], destk[:, :])
            dve.drain()
            nc.vector.tensor_scalar(lane_i[:, :], desti[:, :], BLOCK - 1, None, ALU.bitwise_and)
            nc.vector.tensor_scalar(blk_i[:, :], desti[:, :], 7, None, ALU.arith_shift_right)
            dve.drain()
            nc.vector.tensor_copy(lane_f[:, :], lane_i[:, :])
            nc.vector.tensor_copy(blk_f[:, :], blk_i[:, :])
            dve.drain()
            dve.wait_ge(slot_ready, 1)
            for n in range(16):
                nc.vector.tensor_scalar(lane_hot[:, n, :], k.const[:, C_IOTA:C_IOTA + P], lane_f[:, n:n + 1], None,
                                        ALU.is_equal)
                nc.vector.tensor_scalar(blk_hot[:, n, :], k.const[:, C_IOTA:C_IOTA + MAX_BLOCKS], blk_f[:, n:n + 1],
                                        slot_no[:, n:n + 1], ALU.is_equal, ALU.mult)
            dve.drain().then_inc(hot, 1)
            dve.wait_ge(listed, 1)
            nc.vector.tensor_scalar(slots[:, :], k.bank[5][:, 0:MAX_BLOCKS], 1.0, None, ALU.subtract)
            dve.drain()
            nc.vector.tensor_scalar(isnone[:, :], slots[:, :], 0.0, k.const[:, C_P + 2:C_P + 3], ALU.is_lt, ALU.mult)
            nc.vector.tensor_scalar(token[:, :], slots[:, :], 0.0, None, ALU.max)
            dve.drain()
            nc.vector.tensor_tensor(row[:, :], slots[:, :], isnone[:, :], ALU.add)
            nc.vector.tensor_copy(token_i[:, :], token[:, :])
            dve.drain()
            nc.vector.tensor_copy(r.row[:, :], row[:, :])
            nc.vector.tensor_scalar(r.token[:, 0:MAX_BLOCKS].bitcast(I32), token_i[:, :], 2, None, ALU.arith_shift_right)
            nc.vector.memset(r.token[:, MAX_BLOCKS:MAX_BLOCKS + 1], 0)


def bias_split_stage(nc, k, A, r):
    with Stage(nc, "bsplit") as st:
        full = st.sb("full", [96, 3 * FF])
        hi = st.sb("hi", [96, 3 * FF], BF16)
        bias_in = st.sem("bias_in")
        block = st.block()

        @block.sync
        def _(sp):
            for g in range(3):
                rows = full[32 * g:32 * g + 32, :]
                sp.dma_start(rows[:, 0:2 * FF], A["b_exp_in"][0]).then_inc(bias_in, 16)
                sp.dma_start(rows[:, 2 * FF:3 * FF], A["b_exp_out"][0]).then_inc(bias_in, 16)

        @block.vector
        def _(dve):
            dve.wait_ge(bias_in, 96)
            for g in range(3):
                nc.vector.tensor_copy(hi[:, :], full[:, :])
                dve.drain()
                nc.vector.tensor_copy(r.bias[32 * g:32 * g + 32, :], hi[32 * g:32 * g + 32, :])
                nc.vector.tensor_tensor(full[:, :], full[:, :], hi[:, :], ALU.subtract)
                dve.drain()


def experts_stage(nc, k, A, r):
    CH = 6
    with Stage(nc, "moe") as st:
        ring = [st.sb(f"w{c}", [P, NK, 512]) for c in range(CH)]
        rows_in = [st.sb(f"rows{p}", [P, D]) for p in range(2)]
        tok = [st.sb(f"tok{p}", [P, 1], U32) for p in range(2)]
        dst = [st.sb(f"dst{p}", [P, 1], U32) for p in range(2)]
        xt, at = st.sb("xt", [P, NK, P]), st.sb("at", [P, NK, P])
        sel = [st.sb(f"sel{p}", [96, P], BF16) for p in range(2)]
        g2, u2, sg2, a2 = ([st.sb(f"{n}{half}", [P, 512]) for half in range(2)] for n in ("g", "u", "sg", "a"))
        y = [st.sb(f"y{p}", [P, D]) for p in range(2)]
        chunk_in = [st.sem(f"chunk{c}_in") for c in range(CH)]
        rows_sem = [st.sem(f"rows{p}_in") for p in range(2)]
        stored = [st.sem(f"stored{p}") for p in range(2)]
        x_ps, sel_ready, y_free = (st.sem(n) for n in ("x_ps", "sel_ready", "y_free"))
        x_sb = [st.sem("x_sb0"), st.sem("x_sb1")]
        h_ps, g_ready, sg_ready, a_ready = (st.sem(n) for n in ("h_ps", "g_ready", "sg_ready", "a_ready"))
        a_ps, a_sb, y_ps, y_sb = (st.sem(n) for n in ("a_ps", "a_sb", "y_ps", "y_sb"))
        w_in = A["w_exp_in"][0].rearrange("e (k p) n -> e p k n", p=P)
        w_out = A["w_exp_out"][0].rearrange("e (k p) n -> e p k n", p=P)
        COLS = [0, FF, 512, FF + 512, 0, 512]
        block = st.block()

        def each_block(eng, body, before=None):
            count = eng.value_load(r.expert_i[0:1, MAX_BLOCKS:MAX_BLOCKS + 1], min_val=0, max_val=MAX_BLOCKS)
            if before:
                before()
            with eng.Fori(0, MAX_BLOCKS // 2) as q:
                for p in range(2):
                    with eng.If(q * 2 + p < count):
                        body(q, p, q * 2 + p)

        @block.sync
        def _(sp):
            def body(q, p, j):
                e = sp.value_load(r.expert_i[0:1, ds(j, 1)], min_val=0, max_val=NE - 1)
                for c in range(CH):
                    src = (w_in if c < 4 else w_out)[ds(e, 1), :, :, COLS[c]:COLS[c] + 512]
                    if c < 4:
                        sp.wait_ge(h_ps, j * 4 + c + 1)
                    else:
                        sp.wait_ge(y_ps, j * 2 + c - 3)
                    sp.dma_start(ring[c][:, :, :], src.rearrange("o p k n -> (o p) k n")).then_inc(chunk_in[c], 16)

            each_block(sp, body)

        @block.gpsimd
        def _(pool):
            def start():
                nc.gpsimd.tensor_copy(tok[0][:, :], r.token[:, 0:1])
                pool.drain()
                nc.gpsimd.indirect_dma_start(
                    out=rows_in[0][:, :], out_offset=None, in_=k.h1[:, :],
                    in_offset=bass.IndirectOffsetOnAxis(ap=tok[0][:, 0:1], axis=0)).then_inc(rows_sem[0], 16)

            def body(q, p, j):
                pool.wait_ge(x_ps, j * 2 + 1)
                nc.gpsimd.tensor_copy(tok[1 - p][:, :], r.token[:, ds(j + 1, 1)])
                pool.drain()
                nc.gpsimd.indirect_dma_start(
                    out=rows_in[1 - p][:, :], out_offset=None, in_=k.h1[:, :],
                    in_offset=bass.IndirectOffsetOnAxis(ap=tok[1 - p][:, 0:1], axis=0)).then_inc(rows_sem[1 - p], 16)
                pool.wait_ge(y_sb, j * 2 + 4)
                nc.gpsimd.tensor_copy(dst[p][:, :], r.row[:, ds(j, 1)])
                pool.drain()
                nc.gpsimd.indirect_dma_start(
                    out=k.y_slots[:, :], out_offset=bass.IndirectOffsetOnAxis(ap=dst[p][:, 0:1], axis=0),
                    in_=y[p][:, :], in_offset=None).then_inc(stored[p], 16)
                pool.wait_ge(stored[p], q * 16 + 16)
                pool.sem_inc(y_free, 1)

            each_block(pool, body, start)
            pool.drain()

        @block.tensor
        def _(pe):
            def start():
                pe.drain().then_inc(h_ps, 4)
                pe.drain().then_inc(y_ps, 2)
                pe.drain().then_inc(x_ps, 1)

            def body(q, p, j):
                pe.wait_ge(rows_sem[p], q * 16 + 16)
                for half in range(2):
                    pe.wait_ge(a_sb, j * 2 + half + 1)
                    for c in range(4):
                        t = half * 4 + c
                        last = nc.tensor.transpose(k.bank[6 + half][:, c * P:(c + 1) * P],
                                                   rows_in[p][:, t * P:(t + 1) * P], k.ident)
                    last.then_inc(x_ps, 1)
                pe.wait_ge(sel_ready, j + 1)
                for c in range(4):
                    pe.wait_ge(chunk_in[c], j * 16 + 16)
                    nc.tensor.matmul(k.bank[c][:, :], sel[p][:, :], r.bias[:, COLS[c]:COLS[c] + 512],
                                     start=True, stop=False)
                    for t in range(NK):
                        if c == 0 and t % 4 == 0:
                            pe.wait_ge(x_sb[t // 4], j + 1)
                        last = nc.tensor.matmul(k.bank[c][:, :], xt[:, t, :], ring[c][:, t, :],
                                                start=False, stop=t == NK - 1)
                    last.then_inc(h_ps, 1)
                pe.wait_ge(y_sb, j * 2 + 2)
                for half in range(2):
                    pe.wait_ge(a_ready, j * 2 + half + 1)
                    for c in range(4):
                        last = nc.tensor.transpose(k.bank[6 + half][:, c * P:(c + 1) * P],
                                                   a2[half][:, c * P:(c + 1) * P], k.ident)
                    last.then_inc(a_ps, 1)
                    pe.wait_ge(a_sb, j * 2 + half + 3)
                    for c in range(2):
                        if half == 0:
                            pe.wait_ge(chunk_in[4 + c], j * 16 + 16)
                            nc.tensor.matmul(k.bank[4 + c][:, :], sel[p][:, :],
                                             r.bias[:, 2 * FF + 512 * c:2 * FF + 512 * c + 512],
                                             start=True, stop=False)
                        for t in range(4 * half, 4 * half + 4):
                            last = nc.tensor.matmul(k.bank[4 + c][:, :], at[:, t, :], ring[4 + c][:, t, :],
                                                    start=False, stop=t == NK - 1)
                        if half:
                            last.then_inc(y_ps, 1)

            each_block(pe, body, start)

        @block.scalar
        def _(act):
            def start():
                act.drain().then_inc(a_sb, 2)

            def body(q, p, j):
                act.wait_ge(x_ps, j * 2 + 3)
                nc.scalar.activation(xt[:, 4:8, :], k.bank[7][:, :], ACT.Copy).then_inc(x_sb[1], 1)
                for half in range(2):
                    act.wait_ge(g_ready, j * 2 + half + 1)
                    nc.scalar.activation(sg2[half][:, :], g2[half][:, :], ACT.Sigmoid, scale=SWI).then_inc(sg_ready, 1)
                    act.wait_ge(a_ps, j * 2 + half + 1)
                    nc.scalar.activation(at[:, 4 * half:4 * half + 4, :], k.bank[6 + half][:, :], ACT.Copy)\
                        .then_inc(a_sb, 1)
                act.wait_ge(y_ps, j * 2 + 4)
                act.wait_ge(y_free, j + 1)
                nc.scalar.activation(y[p][:, 512:1024], k.bank[5][:, :], ACT.Copy).then_inc(y_sb, 1)

            each_block(act, body, start)

        @block.vector
        def _(dve):
            def start():
                dve.drain().then_inc(y_sb, 2)
                dve.drain().then_inc(y_free, 2)

            def body(q, p, j):
                nc.vector.tensor_scalar(sel[p][:, :], k.const[0:96, C_P + 1:C_P + 2].to_broadcast([96, P]),
                                        r.expert[0:96, ds(j, 1)], None, ALU.is_equal).then_inc(sel_ready, 1)
                dve.wait_ge(x_ps, j * 2 + 2)
                nc.vector.tensor_copy(xt[:, 0:4, :], k.bank[6][:, :]).then_inc(x_sb[0], 1)
                for half in range(2):
                    dve.wait_ge(h_ps, j * 4 + 2 * half + 5)
                    nc.vector.tensor_scalar(g2[half][:, :], k.bank[2 * half][:, :], LIMIT, None, ALU.min)\
                        .then_inc(g_ready, 1)
                    dve.wait_ge(h_ps, j * 4 + 2 * half + 6)
                    nc.vector.tensor_scalar(u2[half][:, :], k.bank[2 * half + 1][:, :], LIMIT, -LIMIT, ALU.min, ALU.max)
                    dve.drain()
                    nc.vector.scalar_tensor_tensor(out=u2[half][:, :], in0=u2[half][:, :], scalar=1.0, in1=g2[half][:, :],
                                                   op0=ALU.add, op1=ALU.mult)
                    dve.drain()
                    dve.wait_ge(sg_ready, j * 2 + half + 1)
                    nc.vector.tensor_tensor(a2[half][:, :], u2[half][:, :], sg2[half][:, :], ALU.mult).then_inc(a_ready, 1)
                dve.wait_ge(y_ps, j * 2 + 3)
                dve.wait_ge(y_free, j + 1)
                nc.vector.tensor_copy(y[p][:, 0:512], k.bank[4][:, :]).then_inc(y_sb, 1)

            each_block(dve, body, start)


def combine_stage(nc, k, r, x):
    with Stage(nc, "combine") as st:
        ys = [st.sb(f"ys{p}", [P, TOPK, D]) for p in range(2)]
        y_in = [st.sem("y0_in"), st.sem("y1_in")]
        added = st.sem("added")
        rows = k.y_slots[0:SLOTS, :].rearrange("(i p c) n -> i p c n", p=P, c=TOPK)
        block = st.block()

        @block.sync
        def _(sp):
            for i in range(NT):
                if i >= 2:
                    sp.wait_ge(added, i - 1)
                sp.dma_start(ys[i % 2][:, :, :], rows[i]).then_inc(y_in[i % 2], 16)

        @block.vector
        def _(dve):
            for i in range(NT):
                dve.wait_ge(y_in[i % 2], 16 * (i // 2 + 1))
                nc.vector.tensor_scalar(x[:, i, :], x[:, i, :], ALPHA, None, ALU.mult)
                for c in range(TOPK):
                    dve.drain()
                    last = nc.vector.scalar_tensor_tensor(out=x[:, i, :], in0=ys[i % 2][:, c, :],
                                                          scalar=r.weight[:, i, c:c + 1], in1=x[:, i, :],
                                                          op0=ALU.mult, op1=ALU.add)
                last.then_inc(added, 1)


def nsa_keys_stage(nc, k, A, n):
    w2 = A["w_in_2"][0]
    with Stage(nc, "nsakv") as st:
        FEATURE, NATURAL = (KC2, VC2, KS2, KW2), (VS2, VW2)
        w = [st.sb(f"w{c}", [P, NK, P]) for c in range(6)]
        wg = st.sb("wg", [P, NK, 18])
        w1 = [st.sb(f"wc1{c}", [P, 32, P]) for c in range(2)]
        wc2 = [st.sb(f"wc2{c}", [P, HD]) for c in range(2)]
        pos = st.sb("pos", [P, 32])
        src = [st.sb(f"src{c}", [P, S]) for c in range(2)]
        blk = [st.sb(f"blk{c}", [P, 32, N_CMP]) for c in range(2)]
        NH = 4 * N_CMP
        hid, t, th, act_h = (st.sb(x, [P, NH]) for x in ("hid", "t", "th", "act_h"))
        w_in = [st.sem(f"w{c}_in") for c in range(6)]
        wg_in, wc_in, table_in = st.sem("wg_in"), st.sem("wc_in"), st.sem("table_in")
        projected, evacuated, blocks = st.sem("projected"), st.sem("evacuated"), st.sem("blocks")
        hid_ps, arg_ready, tanh_ready, hid_ready = (st.sem(x) for x in ("hid_ps", "arg_ready", "tanh_ready", "hid_ready"))
        cmp_ps = st.sem("cmp_ps")
        block = st.block()

        @block.sync
        def _(sp):
            for c, first in enumerate(FEATURE + NATURAL):
                sp.dma_start(w[c][:, :, :], column_tiles(w2, first)).then_inc(w_in[c], 16)
            with nc.allow_non_contiguous_dma(reason="positions by feature; 18 gate columns"):
                for g in range(2):
                    sp.dma_start(pos[HD * g:HD * g + HD, :], A["cmp_pos_2"][0].rearrange("l d -> d l"))\
                        .then_inc(wc_in, 16)
                sp.dma_start(wg[:, :, :], column_tiles(w2, G2, 18)).then_inc(wg_in, 16)
            skewed = bass.AP(k.z_t5_handle, P - 1, [[1023, P], [P * 1024, 6], [1, BW]])
            sp.dma_start(n.table[:, :, :], skewed).then_inc(table_in, 16)
            sp.wait_ge(table_in, 16)

        @block.scalar
        def _(act):
            for c, names in enumerate((("w_ck1_2", "w_ck2_2"), ("w_cv1_2", "w_cv2_2"))):
                for g in range(2):
                    act.dma_start(w1[c][HD * g:HD * g + HD, :, :],
                                  A[names[0]][0].rearrange("(l d) h -> d l h", d=HD)).then_inc(wc_in, 16)
                act.dma_start(wc2[c][:, :], A[names[1]][0]).then_inc(wc_in, 16)
            for c, dst in enumerate((src[0], src[1], n.ks_t, n.kw_t)):
                act.wait_ge(projected, c + 1)
                nc.scalar.activation(dst[:, :], k.bank[c][:, :], ACT.Copy).then_inc(evacuated, 1)
            for c, dst in enumerate((n.vs, n.vw)):
                act.wait_ge(projected, c + 5)
                nc.scalar.activation(dst[:, :, :], k.bank[4 + c][:, :], ACT.Copy)
            act.wait_ge(projected, 7)
            nc.scalar.activation(n.gates[:, :, :], k.bank[6][:, 0:NT * 18], ACT.Sigmoid)
            act.wait_ge(arg_ready, 1)
            nc.scalar.activation(th[:, :], t[:, :], ACT.Tanh, scale=0.7978845608028654).then_inc(tanh_ready, 1)

        @block.tensor
        def _(pe):
            for c in range(4):
                pe.wait_ge(w_in[c], 16)
                for f in range(NK):
                    last = nc.tensor.matmul(k.bank[c][:, :], w[c][:, f, :], k.x_t[:, f, :],
                                            start=f == 0, stop=f == NK - 1)
                last.then_inc(projected, 1)
            for c in range(4, 6):
                pe.wait_ge(w_in[c], 16)
                for i in range(NT):
                    for f in range(NK):
                        last = nc.tensor.matmul(k.bank[c][:, i * P:(i + 1) * P], k.x_t[:, f, i * P:(i + 1) * P],
                                                w[c][:, f, :], start=f == 0, stop=f == NK - 1)
                last.then_inc(projected, 1)
            pe.wait_ge(wg_in, 16)
            for i in range(NT):
                for f in range(NK):
                    last = nc.tensor.matmul(k.bank[6][:, i * 18:(i + 1) * 18], k.x_t[:, f, i * P:(i + 1) * P],
                                            wg[:, f, :], start=f == 0, stop=f == NK - 1)
            last.then_inc(projected, 1)
            pe.wait_ge(wc_in, 128)
            for c in range(2):
                pe.wait_ge(blocks, c + 1)
                for g, bank in enumerate((7, 0)):
                    rows, cols = slice(HD * g, HD * g + HD), slice(c * N_CMP, (c + 1) * N_CMP)
                    for l in range(32):
                        last = nc.tensor.matmul(k.bank[bank][:, cols], w1[c][rows, l, :], blk[c][rows, l, :],
                                                start=l == 0, stop=l == 31)
            last.then_inc(hid_ps, 1)
            pe.wait_ge(evacuated, 2)
            pe.wait_ge(hid_ready, 1)
            for g in range(2):
                nc.tensor.matmul(k.bank[0][HD * g:HD * g + HD, 0:N_CMP], wc2[0][:, :],
                                 act_h[:, g * N_CMP:(g + 1) * N_CMP], start=True, stop=True)
                last = nc.tensor.matmul(k.bank[1][0:N_CMP, HD * g:HD * g + HD],
                                        act_h[:, (2 + g) * N_CMP:(3 + g) * N_CMP], wc2[1][:, :],
                                        start=True, stop=True)
            last.then_inc(cmp_ps, 1)

        @block.vector
        def _(dve):
            dve.wait_ge(wc_in, 128)
            for c in range(2):
                dve.wait_ge(evacuated, c + 1)
                by_block = src[c][:, :].rearrange("p (n b) -> p b n", b=16)
                for a in range(2):
                    last = nc.vector.tensor_tensor(
                        blk[c][:, 16 * a:16 * a + 16, :], by_block[:, :, a:a + N_CMP],
                        pos[:, 16 * a:16 * a + 16].unsqueeze(2).to_broadcast([P, 16, N_CMP]), ALU.add)
                last.then_inc(blocks, 1)
            dve.wait_ge(hid_ps, 1)
            for g, bank in enumerate((7, 0)):
                nc.vector.tensor_copy(hid[:, :].rearrange("p (c g n) -> p c g n", c=2, g=2)[:, :, g, :],
                                      k.bank[bank][:, 0:2 * N_CMP].rearrange("p (c n) -> p c n", c=2))
            dve.drain()
            nc.vector.tensor_tensor(t[:, :], hid[:, :], hid[:, :], ALU.mult)
            dve.drain()
            nc.vector.tensor_scalar(t[:, :], t[:, :], 0.044715, 1.0, ALU.mult, ALU.add)
            dve.drain()
            nc.vector.tensor_tensor(t[:, :], t[:, :], hid[:, :], ALU.mult).then_inc(arg_ready, 1)
            dve.wait_ge(tanh_ready, 1)
            nc.vector.tensor_scalar(th[:, :], th[:, :], 1.0, 0.5, ALU.add, ALU.mult)
            dve.drain()
            nc.vector.tensor_tensor(act_h[:, :], th[:, :], hid[:, :], ALU.mult).then_inc(hid_ready, 1)
            dve.wait_ge(cmp_ps, 1)
            nc.vector.tensor_copy(n.kc_t[:, :], k.bank[0][:, 0:N_CMP])
            nc.vector.tensor_copy(n.vc[:, :], k.bank[1][0:N_CMP, 0:P])


def nsa_attention_stage(nc, k, A, n, out):
    w2 = A["w_in_2"][0]
    with Stage(nc, "nsa") as st:
        wq, qt = st.sb("wq", [P, NK, P]), st.sb("qt", [P, S])
        b = attention_buffers(k, st)
        w_in, projected, evacuated = st.sem("w_in"), st.sem("projected"), st.sem("evacuated")
        tiles = []
        for i in range(NT):
            for g in range(2):
                rows = slice(HD * g, HD * g + HD)
                for br in range(3):
                    keys = N_CMP if br == 0 else (i + 1) * P
                    kt = (n.kc_t, n.ks_t, n.kw_t)[br]
                    if br == 0:
                        first = BW - 481 - P * i
                        cols = slice(first, first + 16 * (N_CMP - 1) + 1, 16)
                    else:
                        cols = slice((NT - 1 - i) * P, S)
                    if br == 0:
                        def value(j, g=g):
                            return n.vc[0:N_CMP, HD * g:HD * g + HD]
                    else:
                        def value(j, g=g, v=(None, n.vs, n.vw)[br]):
                            return v[:, j, HD * g:HD * g + HD]
                    tiles.append(dict(
                        i=i, keys=keys, q=qt[rows, i * P:(i + 1) * P], kt=kt[rows, 0:keys],
                        bias=lambda u, g=g, cols=cols: n.table[:, ds(u + 3 * g, 1), cols]
                            .rearrange("p o n -> p (o n)"),
                        v=value, out=(HD * g, HD), first=br == 0, last=br == 2, masked=br == 0 and i == 0,
                        scale=lambda u, i=i, c=9 * g + br: n.gates[:, i, ds(u * 3 + c, 1)]))
        items = Items(tiles)
        out4 = out.rearrange("p i (g d) -> p i g d", g=2)
        block = st.block()

        @block.sync
        def _(sp):
            def load(u):
                for g in range(2):
                    sp.dma_start(wq[:, :, HD * g:HD * g + HD], column_tiles(w2, Q2 + 192 * g + u * HD, HD))\
                        .then_inc(w_in, 16)

            load(0)
            with sp.Fori(1, NSA_J) as u:
                sp.wait_ge(projected, u)
                load(u)

        @block.tensor
        def _(pe):
            with pe.Fori(0, NSA_J) as u:
                pe.wait_ge(w_in, u * 32 + 32)
                for c in range(NK):
                    last = nc.tensor.matmul(k.bank[7][:, :], wq[:, c, :], k.x_t[:, c, :],
                                            start=c == 0, stop=c == NK - 1)
                last.then_inc(projected, 1)
                pe.wait_ge(evacuated, u + 1)
                attention_pe(nc, pe, k, items, b, u)

        @block.vector
        def _(dve):
            with dve.Fori(0, NSA_J) as u:
                def copy_out(u, i):
                    return nc.vector.tensor_copy(out4[:, i, :, ds(u * HD, HD)],
                                                 k.bank[5 + i % 2][:, 0:P].rearrange("p (g d) -> p g d", g=2))

                attention_dve(nc, dve, k, items, b, u, copy_out)

        @block.scalar
        def _(act):
            with act.Fori(0, NSA_J) as u:
                act.wait_ge(projected, u + 1)
                nc.scalar.activation(qt[:, :], k.bank[7][:, :], ACT.Copy, scale=HD ** -0.5).then_inc(evacuated, 1)
                attention_act(nc, act, k, items, b, u)

    k.attention.counted(scored=NSA_J * items.n, out_copied=NSA_J * NT)


def negative_abs(nc, out, x, floor):
    return nc.vector.scalar_tensor_tensor(out=out, in0=floor, scalar=2.0, in1=x, op0=ALU.mult, op1=ALU.subtract)


def load_three(sp, wts, w, firsts, u, w_in):
    for dst, first in zip(wts, firsts):
        sp.dma_start(dst[:, :, :], column_tiles(w, first + u * P)).then_inc(w_in, 16)


def project_three(nc, pe, k, wts, banks, projected):
    for weights, bank in zip(wts[:2], banks[:2]):
        for c in range(NK):
            last = nc.tensor.matmul(k.bank[bank][:, :], weights[:, c, :], k.x_t[:, c, :],
                                    start=c == 0, stop=c == NK - 1)
        last.then_inc(projected, 1)
    for i in range(NT):
        for c in range(NK):
            last = nc.tensor.matmul(k.bank[banks[2]][:, i * P:(i + 1) * P], k.x_t[:, c, i * P:(i + 1) * P],
                                    wts[2][:, c, :], start=c == 0, stop=c == NK - 1)
    last.then_inc(projected, 1)


def stick_breaking_stage(nc, k, A, out_t):
    w2 = A["w_in_2"][0]
    UNITS, WIDTHS = 2, [S - P * j for j in range(NT)]
    AT = [sum(WIDTHS[:j]) for j in range(NT)]
    W = sum(WIDTHS)
    with Stage(nc, "sb") as st:
        wts = [st.sb(f"w{c}", [P, NK, P]) for c in range(3)]
        qt, kt, v = st.sb("qt", [P, S]), st.sb("kt", [P, S]), st.sb("v", [P, NT, P])
        ex, ls, lr, a = (st.sb(x, [P, W]) for x in ("ex", "ls", "lr", "a"))
        w_in, projected, evacuated = st.sem("w_in"), st.sem("projected"), st.sem("evacuated")
        z_ps, abs_ready, log_ready, rest_ready = (st.sem(x) for x in ("z_ps", "abs_ready", "log_ready", "rest_ready"))
        between, sum_ready, a_exp, a_ready, o_ps, o_sb = (st.sem(x) for x in (
            "between", "sum_ready", "a_exp", "a_ready", "o_ps", "o_sb"))
        exp_done = st.sem("exp_done")
        below = k.const[:, C_LT:C_LT + P]
        block = st.block()

        @block.sync
        def _(sp):
            load_three(sp, wts, w2, (SBQ, SBK, SBV), 0, w_in)
            with sp.Fori(1, UNITS) as u:
                sp.wait_ge(projected, u * 3)
                load_three(sp, wts, w2, (SBQ, SBK, SBV), u, w_in)

        @block.tensor
        def _(pe):
            with pe.Fori(0, UNITS) as u:
                pe.wait_ge(w_in, u * 48 + 48)
                project_three(nc, pe, k, wts, (7, 6, 5), projected)
                pe.wait_ge(evacuated, u * 3 + 3)
                for m in range(2):
                    rows = slice(HD * m, HD * m + HD)
                    pe.wait_ge(o_sb, u * 2 + m + 1)
                    for j in range(NT):
                        nc.tensor.matmul(k.bank[j][:, 0:WIDTHS[j]], kt[rows, j * P:(j + 1) * P], qt[rows, j * P:S],
                                         start=True, stop=True).then_inc(z_ps, 1)
                    pe.wait_ge(rest_ready, u * 2 + m + 1)
                    for j in range(NT):
                        for h in range(j, NT):
                            later = C_GT if h == j else C_ONE
                            last = nc.tensor.matmul(k.bank[4 + j][:, (h - j) * P:WIDTHS[j]],
                                                    k.const[:, later:later + P], lr[:, AT[h]:AT[h] + WIDTHS[h]],
                                                    start=h == j, stop=h == NT - 1)
                        last.then_inc(between, 1)
                    pe.wait_ge(a_ready, u * 2 + m + 1)
                    for j in range(NT):
                        last = nc.tensor.matmul(k.bank[0][rows, j * P:S], v[:, j, rows], a[:, AT[j]:AT[j] + WIDTHS[j]],
                                                start=j == 0, stop=j == NT - 1)
                    last.then_inc(o_ps, 1)

        @block.scalar
        def _(act):
            with act.Fori(0, UNITS) as u:
                act.wait_ge(projected, u * 3 + 1)
                nc.scalar.activation(qt[:, :], k.bank[7][:, :], ACT.Copy, scale=HD ** -0.5).then_inc(evacuated, 1)
                act.wait_ge(projected, u * 3 + 2)
                nc.scalar.activation(kt[:, :], k.bank[6][:, :], ACT.Copy).then_inc(evacuated, 1)
                act.wait_ge(projected, u * 3 + 3)
                nc.scalar.activation(v[:, :, :], k.bank[5][:, :], ACT.Copy).then_inc(evacuated, 1)
                for m in range(2):
                    act.wait_ge(abs_ready, u * 2 + m + 1)
                    nc.scalar.activation(ex[:, :], ex[:, :], ACT.Exp)
                    act.drain()
                    nc.scalar.activation(ex[:, :], ex[:, :], ACT.Ln, bias=1.0).then_inc(log_ready, 1)
                    act.wait_ge(sum_ready, u * 2 + m + 1)
                    nc.scalar.activation(a[:, :], a[:, :], ACT.Exp).then_inc(a_exp, 1)

        @block.vector
        def _(dve):
            dve.drain().then_inc(o_sb, 1)
            with dve.Fori(0, UNITS) as u:
                for m in range(2):
                    for j in range(NT):
                        at = slice(AT[j], AT[j] + WIDTHS[j])
                        dve.wait_ge(z_ps, u * 8 + m * 4 + j + 1)
                        nc.vector.tensor_scalar(ls[:, at], k.bank[j][:, 0:WIDTHS[j]], 0.0, None, ALU.min)
                    dve.drain()
                    for j in range(NT):
                        at = slice(AT[j], AT[j] + WIDTHS[j])
                        negative_abs(nc, ex[:, at], k.bank[j][:, 0:WIDTHS[j]], ls[:, at])
                    dve.drain().then_inc(abs_ready, 1)
                    dve.wait_ge(log_ready, u * 2 + m + 1)
                    nc.vector.tensor_tensor(ls[:, :], ls[:, :], ex[:, :], ALU.subtract)
                    dve.drain()
                    for j in range(NT):
                        at = slice(AT[j], AT[j] + WIDTHS[j])
                        nc.vector.tensor_tensor(lr[:, at], ls[:, at], k.bank[j][:, 0:WIDTHS[j]], ALU.subtract)
                    dve.drain()
                    for j in range(NT):
                        diag = lr[:, AT[j]:AT[j] + P]
                        nc.vector.tensor_tensor(diag, diag, below, ALU.mult)
                    dve.drain().then_inc(rest_ready, 1)
                    for j in range(NT):
                        at = slice(AT[j], AT[j] + WIDTHS[j])
                        dve.wait_ge(between, u * 8 + m * 4 + j + 1)
                        nc.vector.tensor_tensor(a[:, at], ls[:, at], k.bank[4 + j][:, 0:WIDTHS[j]], ALU.add)
                    dve.drain().then_inc(sum_ready, 1)
                    dve.wait_ge(a_exp, u * 2 + m + 1)
                    for j in range(NT):
                        diag = a[:, AT[j]:AT[j] + P]
                        nc.vector.tensor_tensor(diag, diag, below, ALU.mult)
                    dve.drain().then_inc(a_ready, 1)
                    dve.wait_ge(o_ps, u * 2 + m + 1)
                    rows = slice(HD * m, HD * m + HD)
                    nc.vector.tensor_copy(out_t[rows, ds(u, 1), :], k.bank[0][rows, :].unsqueeze(1))
                    dve.drain().then_inc(o_sb, 1)


def hgrn_stage(nc, k, A, out):
    w2 = A["w_in_2"][0]
    UNITS, LEVELS = 3, 8
    with Stage(nc, "hg") as st:
        wts = [st.sb(f"w{c}", [P, NK, P]) for c in range(3)]
        q, v = st.sb("q", [P, S]), st.sb("v", [P, NT, P])
        t1, t2, ls, key, lf, b = (st.sb(x, [P, S]) for x in ("t1", "t2", "ls", "key", "lf", "b"))
        lev = [st.sb(f"lev{x}", [P, S]) for x in range(2)]
        eb, qe, kd, kd_t = (st.sb(x, [P, S]) for x in ("eb", "qe", "kd", "kd_t"))
        att = [st.sb(f"att{m}", [P, S]) for m in range(2)]
        zeros, state = st.sb("zeros", [P, P]), st.sb("state", [P, HD])
        w_in, projected, evacuated = st.sem("w_in"), st.sem("projected"), st.sem("evacuated")
        abs_ready, log_ready, floor_ready, floor_log = (st.sem(x) for x in (
            "abs_ready", "log_ready", "floor_ready", "floor_log"))
        key_ready, diff_ready, lev_exp, lev_ready, lev_ps, lev_done = (st.sem(x) for x in (
            "key_ready", "diff_ready", "lev_exp", "lev_ready", "lev_ps", "lev_done"))
        edge_ready, edge_exp, kd_ready, kd_ps, kd_sb = (st.sem(x) for x in (
            "edge_ready", "edge_exp", "kd_ready", "kd_ps", "kd_sb"))
        grown, state_ready, o_ps, o_sb = (st.sem(x) for x in ("grown", "state_ready", "o_ps", "o_sb"))
        block = st.block()

        @block.sync
        def _(sp):
            load_three(sp, wts, w2, (HGQ, HGF, HGI), 0, w_in)
            with sp.Fori(1, UNITS) as u:
                sp.wait_ge(projected, u * 3)
                load_three(sp, wts, w2, (HGQ, HGF, HGI), u, w_in)

        @block.tensor
        def _(pe):
            with pe.Fori(0, UNITS) as u:
                pe.wait_ge(w_in, u * 48 + 48)
                pe.wait_ge(o_sb, u + 1)
                project_three(nc, pe, k, wts, (7, 6, 4), projected)
                pe.wait_ge(evacuated, u * 3 + 3)
                for n in range(LEVELS):
                    pe.wait_ge(lev_ready, u * LEVELS + n + 1)
                    if n >= 2:
                        pe.wait_ge(lev_done, u * LEVELS + n - 1)
                    for m in range(2):
                        rows = slice(HD * m, HD * m + HD)
                        left, right = (lev[n % 2], lev[n % 2]) if n < 7 else (key, q)
                        for c in range(NT):
                            last = nc.tensor.matmul(k.bank[2 * (n % 2) + m][:, c * P:(c + 1) * P],
                                                    left[rows, c * P:(c + 1) * P], right[rows, c * P:(c + 1) * P],
                                                    start=True, stop=True)
                    last.then_inc(lev_ps, 1)
                pe.wait_ge(kd_ready, u + 1)
                for c in range(NT):
                    last = nc.tensor.transpose(k.bank[4][:, c * P:(c + 1) * P], kd[:, c * P:(c + 1) * P], k.ident)
                last.then_inc(kd_ps, 1)
                pe.wait_ge(kd_sb, u + 1)
                pe.wait_ge(lev_done, u * LEVELS + LEVELS)
                for c in range(NT):
                    chunk = slice(c * P, (c + 1) * P)
                    if c:
                        pe.wait_ge(state_ready, u * (NT - 1) + c)
                    for m in range(2):
                        rows = slice(HD * m, HD * m + HD)
                        bank, cols = k.bank[(5, 3)[m]], slice(c * HD, c * HD + HD)
                        last = nc.tensor.matmul(bank[:, cols], att[m][:, chunk], v[:, c, rows],
                                                start=True, stop=c == 0)
                        if c:
                            last = nc.tensor.matmul(bank[:, cols], qe[rows, chunk], state[rows, :],
                                                    start=False, stop=True)
                    if c == NT - 1:
                        last.then_inc(o_ps, 1)
                    else:
                        for m in range(2):
                            rows = slice(HD * m, HD * m + HD)
                            last = nc.tensor.matmul(k.bank[6 + c % 2][rows, 0:HD],
                                                    kd_t[:, c * P + HD * m:c * P + HD * m + HD], v[:, c, rows],
                                                    start=True, stop=True)
                        last.then_inc(grown, 1)

        @block.scalar
        def _(act):
            with act.Fori(0, UNITS) as u:
                act.wait_ge(projected, u * 3 + 1)
                nc.scalar.activation(q[:, :], k.bank[7][:, :], ACT.Copy).then_inc(evacuated, 1)
                act.wait_ge(projected, u * 3 + 3)
                nc.scalar.activation(v[:, :, :], k.bank[4][:, :], ACT.Copy).then_inc(evacuated, 1)
                act.wait_ge(abs_ready, u + 1)
                nc.scalar.activation(t1[:, :], t1[:, :], ACT.Exp)
                act.drain()
                nc.scalar.activation(t1[:, :], t1[:, :], ACT.Ln, bias=1.0).then_inc(log_ready, 1)
                act.wait_ge(floor_ready, u + 1)
                nc.scalar.activation(key[:, :], key[:, :], ACT.Exp)
                nc.scalar.activation(t2[:, :], t2[:, :], ACT.Exp)
                act.drain()
                nc.scalar.activation(t2[:, :], t2[:, :], ACT.Ln, bias=1.0).then_inc(floor_log, 1)
                for n in range(LEVELS - 1):
                    act.wait_ge(diff_ready, u * (LEVELS - 1) + n + 1)
                    nc.scalar.activation(lev[n % 2][:, :], lev[n % 2][:, :], ACT.Exp).then_inc(lev_exp, 1)
                act.wait_ge(edge_ready, u + 1)
                nc.scalar.activation(kd[:, :], kd[:, :], ACT.Exp)
                nc.scalar.activation(eb[:, :], b[:, :], ACT.Exp).then_inc(edge_exp, 1)
                act.wait_ge(kd_ps, u + 1)
                nc.scalar.activation(kd_t[:, :], k.bank[4][:, :], ACT.Copy).then_inc(kd_sb, 1)

        @block.vector
        def _(dve):
            nc.vector.memset(zeros[:, :], 0.0)
            for m in range(2):
                nc.vector.memset(att[m][:, :], 0.0)
            dve.drain().then_inc(o_sb, 1)
            with dve.Fori(0, UNITS) as u:
                dve.wait_ge(projected, u * 3 + 2)
                nc.vector.tensor_scalar(ls[:, :], k.bank[6][:, :], 0.0, None, ALU.min)
                dve.drain()
                negative_abs(nc, t1[:, :], k.bank[6][:, :], ls[:, :]).then_inc(abs_ready, 1)
                dve.wait_ge(log_ready, u + 1)
                nc.vector.tensor_tensor(ls[:, :], ls[:, :], t1[:, :], ALU.subtract)
                dve.drain()
                nc.vector.tensor_tensor(key[:, :], ls[:, :], k.bank[6][:, :], ALU.subtract).then_inc(evacuated, 1)
                nc.vector.tensor_scalar(t1[:, :], ls[:, :], LOG_FLOOR, None, ALU.subtract)
                nc.vector.tensor_scalar(t2[:, :], ls[:, :], LOG_FLOOR, 0.0, ALU.subtract, ALU.min)
                nc.vector.tensor_scalar(lf[:, :], ls[:, :], LOG_FLOOR, None, ALU.max)
                dve.drain()
                negative_abs(nc, t2[:, :], t1[:, :], t2[:, :]).then_inc(floor_ready, 1)
                dve.wait_ge(floor_log, u + 1)
                nc.vector.tensor_tensor(lf[:, :], lf[:, :], t2[:, :], ALU.add)
                dve.drain()
                for c in range(NT):
                    chunk = slice(c * P, (c + 1) * P)
                    nc.vector.tensor_tensor_scan(b[:, chunk], lf[:, chunk], zeros[:, :], 0.0, ALU.add, ALU.add)
                dve.drain()
                dve.wait_ge(evacuated, u * 3 + 3)
                chunks = [x[:, :].rearrange("p (c t) -> p c t", t=P) for x in (kd, b)]
                nc.vector.tensor_tensor(chunks[0], chunks[1][:, :, P - 1:P].to_broadcast([P, NT, P]), chunks[1],
                                        ALU.subtract).then_inc(edge_ready, 1)

                def halves(x, n):
                    v4 = x[:, :].rearrange("p (b s t) -> p b s t", s=2, t=1 << n)
                    return v4[:, :, 0, :], v4[:, :, 1, :]

                def exponents(n):
                    left, right = halves(b, n)
                    shape = [P, S >> (n + 1), 1 << n]
                    middle = left[:, :, (1 << n) - 1:1 << n].to_broadcast(shape)
                    to_left, to_right = halves(lev[n % 2], n)
                    if n >= 2:
                        dve.wait_ge(lev_ps, u * LEVELS + n - 1)
                    nc.vector.tensor_tensor(to_left, middle, left, ALU.subtract)
                    nc.vector.tensor_tensor(to_right, right, middle, ALU.subtract)
                    dve.drain().then_inc(diff_ready, 1)

                def factors(n):
                    dve.wait_ge(lev_exp, u * (LEVELS - 1) + n + 1)
                    to_left, to_right = halves(lev[n % 2], n)
                    nc.vector.tensor_tensor(to_left, to_left, halves(key, n)[0], ALU.mult)
                    nc.vector.tensor_tensor(to_right, to_right, halves(q, n)[1], ALU.mult)
                    dve.drain().then_inc(lev_ready, 1)

                def take(n):
                    dve.wait_ge(lev_ps, u * LEVELS + n + 1)
                    nc.vector.memset(zeros[:, 0:1], 0.0)
                    mask = k.hg_mask[:, n * P:(n + 1) * P].unsqueeze(1).to_broadcast([P, NT, P])
                    for m in range(2):
                        nc.vector.copy_predicated(att[m][:, :].rearrange("p (c t) -> p c t", t=P), mask,
                                                  k.bank[2 * (n % 2) + m][:, :].rearrange("p (c t) -> p c t", t=P))
                    dve.drain().then_inc(lev_done, 1)

                for n in range(LEVELS + 1):
                    if n < LEVELS - 1:
                        exponents(n)
                        if n:
                            factors(n - 1)
                    elif n == LEVELS - 1:
                        factors(n - 1)
                        dve.drain().then_inc(lev_ready, 1)
                    if n >= 1:
                        take(n - 1)
                dve.wait_ge(edge_exp, u + 1)
                nc.vector.tensor_tensor(kd[:, :], kd[:, :], key[:, :], ALU.mult).then_inc(kd_ready, 1)
                nc.vector.tensor_tensor(qe[:, :], eb[:, :], q[:, :], ALU.mult)
                for c in range(NT - 1):
                    dve.wait_ge(grown, u * (NT - 1) + c + 1)
                    if c == 0:
                        nc.vector.tensor_copy(state[:, :], k.bank[6][:, 0:HD])
                    else:
                        nc.vector.scalar_tensor_tensor(out=state[:, :], in0=state[:, :],
                                                       scalar=eb[:, c * P + P - 1:c * P + P],
                                                       in1=k.bank[6 + c % 2][:, 0:HD], op0=ALU.mult, op1=ALU.add)
                    dve.drain().then_inc(state_ready, 1)
                dve.wait_ge(o_ps, u + 1)
                for m in range(2):
                    nc.vector.tensor_copy(out[:, :, ds(u * P + HD * m, HD)],
                                          k.bank[(5, 3)[m]][:, 0:NT * HD].rearrange("p (c e) -> p c e", e=HD))
                dve.drain().then_inc(o_sb, 1)


def silu_stage(nc, k, A, m_t):
    w2 = A["w_in_2"][0]
    FIRST = [Z2 + P * c for c in range(3)] + [SBZ + P * c for c in range(2)] + [HGZ + P * c for c in range(3)]
    with Stage(nc, "silu") as st:
        w = [st.sb(f"w{c}", [P, NK, P]) for c in range(4)]
        sg = st.sb("sg", [P, 2, S])
        w_in = [st.sem(f"w{c}_in") for c in range(4)]
        z_ps, sg_ready, gated = st.sem("z_ps"), st.sem("sg_ready"), st.sem("gated")
        block = st.block()

        @block.sync
        def _(sp):
            for f, first in enumerate(FIRST):
                if f >= 4:
                    sp.wait_ge(z_ps, f - 3)
                sp.dma_start(w[f % 4][:, :, :], column_tiles(w2, first)).then_inc(w_in[f % 4], 16)

        @block.tensor
        def _(pe):
            for f in range(NK):
                pe.wait_ge(w_in[f % 4], 16 * (f // 4 + 1))
                if f >= 4:
                    pe.wait_ge(gated, f - 3)
                for c in range(NK):
                    last = nc.tensor.matmul(k.bank[f % 4][:, :], w[f % 4][:, c, :], k.x_t[:, c, :],
                                            start=c == 0, stop=c == NK - 1)
                last.then_inc(z_ps, 1)

        @block.scalar
        def _(act):
            for f in range(NK):
                act.wait_ge(z_ps, f + 1)
                if f >= 2:
                    act.wait_ge(gated, f - 1)
                nc.scalar.activation(sg[:, f % 2, :], k.bank[f % 4][:, :], ACT.Sigmoid).then_inc(sg_ready, 1)

        @block.vector
        def _(dve):
            for f in range(NK):
                dve.wait_ge(sg_ready, f + 1)
                nc.vector.tensor_tensor(sg[:, f % 2, :], sg[:, f % 2, :], k.bank[f % 4][:, :], ALU.mult)
                dve.drain()
                nc.vector.tensor_tensor(m_t[:, f, :], m_t[:, f, :], sg[:, f % 2, :], ALU.mult).then_inc(gated, 1)


def store_stage(nc, k, out):
    with Stage(nc, "store") as st:
        stored = st.sem("stored")
        block = st.block()

        @block.sync
        def _(sp):
            sp.dma_start(out[0].rearrange("(i p) n -> p i n", p=P), k.x[:, :, :]).then_inc(stored, 16)
            sp.wait_ge(stored, 16)


class Kernel:
    pass


def program(nc, A, out):
    k = Kernel()
    with ExitStack() as stack:
        def sb(name, shape, dt=F32):
            return stack.enter_context(nc.sbuf_tensor(name, shape, dt))

        k.bank = [stack.enter_context(nc.psum_tensor(f"bank{n}", [P, 512], F32)) for n in range(8)]
        k.const = sb("const", [P, C_END])
        k.hg_mask = sb("hg_mask", [P, 8 * P], I32)
        k.ident = k.const[:, C_ID:C_ID + P]
        k.neg_lam = sb("neg_lam", [P, 1])
        k.x, k.x_t = sb("xs", [P, NT, D]), sb("x_t", [P, NK, S])
        k.z_band_handle = nc.dram_tensor("z_band", (8, P, 640), F32, kind="Internal")
        k.z_t5_handle = nc.dram_tensor("z_t5", (6, P, 1024), F32, kind="Internal")
        k.z_band, k.z_t5 = k.z_band_handle.ap(), k.z_t5_handle.ap()
        k.h1 = nc.dram_tensor("h1", (S, D), F32, kind="Internal").ap()
        k.y_slots = nc.dram_tensor("y_slots", (SLOTS + P, D), F32, kind="Internal").ap()

        k.norm = SharedSemaphores(nc, stack, "norm", NORM_SEMS)
        k.attention = SharedSemaphores(nc, stack, "attention", ATTENTION_SEMS)
        k.heads = SharedSemaphores(nc, stack, "heads", HEADS_SEMS)
        k.output = SharedSemaphores(nc, stack, "output", ("w0_in", "w1_in", "product", "added"))

        setup_stage(nc, k, A)
        layer_norm_stage(nc, "ln0", k, k.x, A["ln_in_g"], A["ln_in_b"], x_t=k.x_t)
        with ExitStack() as mixer:
            def msb(name, shape, dt=F32):
                return mixer.enter_context(nc.sbuf_tensor(name, shape, dt))

            oa_t, ob_t = msb("oa_t", [P, 4, S]), msb("ob_t", [P, 4, S])
            with ExitStack() as s2:
                table = s2.enter_context(nc.sbuf_tensor("alibi_table", [P, 4, S], F32))
                oa = s2.enter_context(nc.sbuf_tensor("oa", [P, NT, WA], F32))
                alibi_stage(nc, k, table)
                project_heads_stage(
                    nc, "diff", k, A["w_in"][0], 0, WA, 2 * WA, 4,
                    lambda u, m, first, n: table[:, ds(u, 1), first:first + n].rearrange("p o n -> p (o n)"),
                    True, lambda m: k.neg_lam[:, :] if m else None, oa)
                transpose_heads_stage(nc, "diffnorm", k, oa[:, :, :], oa_t, 4,
                                      A["subln_w"].rearrange("o p -> p o"), LN_EPS, 1.0 - LAM_INIT)
            with ExitStack() as s2:
                table = s2.enter_context(nc.sbuf_tensor("band_table", [P, 8, S], F32))
                ob = s2.enter_context(nc.sbuf_tensor("ob", [P, NT, WA], F32))
                band_bias_stage(nc, k, table)
                project_heads_stage(
                    nc, "band", k, A["w_in"][0], 3 * WA, 4 * WA, 5 * WA, 4,
                    lambda u, m, first, n: table[:, ds(u * 2 + m, 1), first:first + n].rearrange("p o n -> p (o n)"),
                    False, lambda m: None, ob)
                transpose_heads_stage(nc, "bandt", k, ob[:, :, :], ob_t)
            m_t = msb("m_t", [P, NK, S])
            merge_stage(nc, k, A, oa_t, ob_t, m_t)
            output_stage(nc, "out1", k, A["w_out"][0], m_t, k.x)
        layer_norm_stage(nc, "ln1", k, k.x, A["ln1_g"][0], A["ln1_b"][0], x_t=k.x_t, save=k.h1)
        with ExitStack() as moe:
            def rsb(name, shape, dt=F32):
                return moe.enter_context(nc.sbuf_tensor(name, shape, dt))

            r = Kernel()
            r.weight, r.expert = rsb("weight", [P, NT, TOPK]), rsb("expert", [P, MAX_BLOCKS])
            r.expert_i = rsb("expert_i", [P, MAX_BLOCKS + 1], I32)
            r.row, r.token = rsb("row", [P, MAX_BLOCKS], U32), rsb("token", [P, MAX_BLOCKS + 1], U32)
            r.bias = rsb("bias", [96, 3 * FF], BF16)
            route_stage(nc, k, A, r)
            bias_split_stage(nc, k, A, r)
            experts_stage(nc, k, A, r)
            combine_stage(nc, k, r, k.x)
        layer_norm_stage(nc, "ln2", k, k.x, A["ln2_g"][0], A["ln2_b"][0], x_t=k.x_t)
        with ExitStack() as mixer:
            def msb(name, shape, dt=F32):
                return mixer.enter_context(nc.sbuf_tensor(name, shape, dt))

            m_t = msb("mixed_t", [P, NK, S])
            with ExitStack() as s2:
                def nsb(name, shape, dt=F32):
                    return s2.enter_context(nc.sbuf_tensor(name, shape, dt))

                n = Kernel()
                n.table = nsb("t5_table", [P, 6, BW])
                n.ks_t, n.kw_t, n.kc_t = nsb("ks_t", [P, S]), nsb("kw_t", [P, S]), nsb("kc_t", [P, N_CMP])
                n.vs, n.vw, n.vc = nsb("vs", [P, NT, P]), nsb("vw", [P, NT, P]), nsb("vc", [N_CMP, P])
                n.gates, o_nsa = nsb("gates", [P, NT, 18]), nsb("o_nsa", [P, NT, 384])
                nsa_keys_stage(nc, k, A, n)
                nsa_attention_stage(nc, k, A, n, o_nsa[:, :, :])
                transpose_heads_stage(nc, "nsat", k, o_nsa[:, :, :], m_t[:, 0:3, :])
            stick_breaking_stage(nc, k, A, m_t[:, 3:5, :])
            with ExitStack() as s2:
                o_hg = s2.enter_context(nc.sbuf_tensor("o_hg", [P, NT, 384], F32))
                hgrn_stage(nc, k, A, o_hg)
                transpose_heads_stage(nc, "hgt", k, o_hg[:, :, :], m_t[:, 5:8, :], 6,
                                      A["hg_norm_w_2"][0].rearrange("(c p) -> p c", p=P), RMS_EPS)
            silu_stage(nc, k, A, m_t)
            output_stage(nc, "out2", k, A["w_out_2"][0], m_t, k.x)
        layer_norm_stage(nc, "ln3", k, k.x, A["ln_g_2"][0], A["ln_b_2"][0])
        store_stage(nc, k, out)


def constants():
    import numpy as np

    p, f = np.arange(P)[:, None], np.arange(P)[None, :]
    c = np.zeros((P, C_END), np.float32)
    c[:, C_ID:C_ID + P] = p == f
    c[:, C_GT:C_GT + P] = p > f
    c[:, C_LT:C_LT + P] = p < f
    c[:, C_ONE:C_ONE + P] = 1.0
    c[:, C_IOTA:C_IOTA + P] = f
    c[:, C_DIST:C_DIST + S] = -np.abs(p - np.arange(S)[None, :] + S - P)
    c[:, C_P] = np.arange(P)
    c[:, C_P + 1] = np.arange(P) % NE
    c[:, C_P + 2] = np.arange(P) + SLOTS + 1
    mask = np.zeros((P, 8, P), np.int32)
    mask[:, 7] = p == f
    for n in range(7):
        mask[:, n] = ((p ^ f) >> n == 1) & (f > p)
    n = 511 - np.arange(512)
    large = 16 + (np.log(np.maximum(n, 1).astype(np.float32) / np.float32(16.0))
                  / np.float32(np.log(8.0)) * np.float32(16.0)).astype(np.int32)
    bucket = np.where(n < 16, n, np.clip(large, 0, 31))
    onehot = (np.arange(32)[:, None] == bucket[None, :]).astype(np.float32)
    return {"c_f32": c, "c_mask": mask.reshape(P, 8 * P), "c_onehot": onehot}


def kernel(**inputs):
    import numpy as np
    import concourse.bacc as bacc
    from concourse import mybir
    from concourse.bass_utils import run_bass_kernel_spmd

    nc = bacc.Bacc("TRN2", target_bir_lowering=False, num_devices=1)
    arrays, A = {}, {}
    for name, value in {**inputs, **constants()}.items():
        a = np.ascontiguousarray(value)
        arrays[f"in_{name}_dram"] = a
        A[name] = nc.dram_tensor(f"in_{name}_dram", a.shape, mybir.dt.from_np(a.dtype), kind="ExternalInput").ap()
    out = nc.dram_tensor("out_0_dram", (1, S, D), mybir.dt.float32, kind="ExternalOutput").ap()
    program(nc, A, out)
    results = run_bass_kernel_spmd(nc, [arrays], core_ids=[0])
    return results.results[0]["out_0_dram"]
```

```python
import concourse.bass as bass
from concourse import mybir
from contextlib import ExitStack

F32 = mybir.dt.float32
BF16 = mybir.dt.bfloat16
F32R = mybir.dt.float32r
I32 = mybir.dt.int32
U32 = mybir.dt.uint32
ALU = mybir.AluOpType
ACT = mybir.ActivationFunctionType
AX = mybir.AxisListType
ds = bass.ds

P = 128
D = 1024
S = 512
NT = S // P
NK = D // P
NEG = -1e30
LN_EPS = 1e-5
RMS_EPS = 1e-6
ALPHA = 2.0 ** 0.25
LAM_INIT = 0.8 - 0.6
HD = 64
WA = 512
NE, TOPK, FF = 32, 4, 1024
BLOCK = 128
MAX_BLOCKS = 48
SLOTS = S * TOPK
LIMIT, SWI = 7.0, 1.702
LOG_FLOOR = -69.07755278982137

C_ID, C_GT, C_LT, C_ONE, C_IOTA, C_DIST, C_P, C_END = 0, 128, 256, 384, 512, 640, 1152, 1160
Q2, KC2, VC2, KS2, VS2, KW2, VW2, G2, Z2 = 0, 384, 512, 640, 768, 896, 1024, 1152, 1170
SBQ, SBK, SBV, SBZ = 1554, 1810, 2066, 2322
HGQ, HGF, HGI, HGZ = 2578, 2962, 3346, 3730
NSA_J = 3
N_CMP = 31
BW = 896


def column_tiles(w, first, width=P):
    return w[:, ds(first, width)].rearrange("(k p) n -> p k n", p=P)


def row_broadcast(v):
    return v.partition_broadcast(P)
HG_UNITS, HG_W = 3, 384


def overlaid(nc, stack, name, shape):
    whole = stack.enter_context(nc.sbuf_tensor(name, shape, F32))
    size = 4
    for n in shape[1:]:
        size *= n
    return whole, nc.alloc_sbuf_tensor_at(name + "_lower", shape, F32R, offset=nc.sbuf_base - size)


class Stage:

    def __init__(self, nc, name):
        self.nc, self.name, self.stack = nc, name, ExitStack()

    def __enter__(self):
        self.stack.__enter__()
        return self

    def __exit__(self, *e):
        return self.stack.__exit__(*e)

    def sb(self, name, shape, dt=F32):
        return self.stack.enter_context(self.nc.sbuf_tensor(f"{self.name}_{name}", shape, dt))

    def overlaid(self, name, shape):
        return overlaid(self.nc, self.stack, f"{self.name}_{name}", shape)

    def sem(self, name):
        return self.stack.enter_context(self.nc.semaphore(f"{self.name}_{name}"))

    def block(self):
        return self.stack.enter_context(self.nc.Block())


class SharedSemaphores:

    def __init__(self, nc, stack, kind, names):
        self.sems = {n: stack.enter_context(nc.semaphore(f"{kind}_{n}")) for n in names}
        self.done = {n: 0 for n in names}

    def __getitem__(self, name):
        return self.sems[name]

    def counted(self, **counts):
        for name, count in counts.items():
            self.done[name] += count


def statistics(nc, k, i, halves=(0, 1)):
    for c in halves:
        nc.vector.bn_stats(k.stats[:, i, 6 * c:6 * c + 6], k.x[:, i, 512 * c:512 * c + 512])


class Split:

    def __init__(self, hi, lo, whole=None):
        self.hi, self.lo, self.whole = hi, lo, whole

    def __getitem__(self, key):
        return Split(self.hi[key], self.lo[key])


def split_product(nc, out, lhs, rhs, start, stop):
    nc.tensor.matmul(out, lhs.hi, rhs.hi, start=start, stop=False)
    nc.tensor.matmul(out, lhs.hi, rhs.lo, start=False, stop=False)
    return nc.tensor.matmul(out, lhs.lo, rhs.hi, start=False, stop=stop)


def split_lower(engine, raw, upper, lower):
    return engine.tensor_tensor(lower, raw, upper.bitcast(F32), ALU.subtract)


NORM_SEMS = ("gain_in", "shift_in", "var_ready", "std_ready", "normed", "transposed", "copied", "hi_copied")


def layer_norm_stage(nc, name, k, x, g_dram, b_dram, x_t=None, save=None, ahead=None, following=()):
    n = k.norm.done["var_ready"]
    with Stage(nc, name) as st:
        gain, shift = k.gain, k.shift
        stats, mv = k.stats, st.sb("mv", [P, NT, 2])
        ve, std, r, t = (st.sb(a, [P, NT]) for a in ("ve", "std", "r", "t"))
        gain_in, shift_in, var_ready, std_ready, normed, transposed, copied, hi_copied = (k.norm[x] for x in NORM_SEMS)
        if save is not None:
            saved = st.sem("saved")
        block = st.block()

        @block.sync
        def _(sp):
            def load(g, b):
                sp.dma_start(gain[:, :], row_broadcast(g)).then_inc(gain_in, 16)
                sp.dma_start(shift[:, :], row_broadcast(b)).then_inc(shift_in, 16)

            if n == 0:
                load(g_dram, b_dram)
            if ahead is not None:
                load_ahead(sp, k, ahead)
            if save is not None:
                for i in range(NT):
                    sp.wait_ge(normed, n * NT + i + 1)
                    sp.dma_start(save[i * P:(i + 1) * P, :], x[:, i, :]).then_inc(saved, 16)
                sp.wait_ge(saved, 16 * NT)
            if following:
                sp.wait_ge(normed, (n + 1) * NT)
                load(*following)

        @block.vector
        def _(dve):
            for i in range(NT):
                nc.vector.bn_aggr(mv[:, i, :], stats[:, i, :])
            dve.drain()
            nc.vector.tensor_scalar(ve[:, :], mv[:, :, 1], LN_EPS, None, ALU.add).then_inc(var_ready, 1)
            dve.wait_ge(std_ready, n + 1)
            nc.vector.reciprocal(r[:, :], std[:, :])
            dve.drain()
            nc.vector.tensor_tensor(t[:, :], r[:, :], r[:, :], ALU.mult)
            dve.drain()
            nc.vector.tensor_tensor(t[:, :], t[:, :], ve[:, :], ALU.mult)
            dve.drain()
            nc.vector.tensor_scalar(t[:, :], t[:, :], -0.5, 1.5, ALU.mult, ALU.add)
            dve.drain()
            nc.vector.tensor_tensor(r[:, :], r[:, :], t[:, :], ALU.mult)
            dve.drain()
            dve.wait_ge(gain_in, 16 * n + 16)
            dve.wait_ge(shift_in, 16 * n + 16)
            for i in range(NT):
                nc.vector.scalar_tensor_tensor(out=x[:, i, :], in0=x[:, i, :], scalar=mv[:, i, 0:1],
                                               in1=gain[:, :], op0=ALU.subtract, op1=ALU.mult)
                dve.drain()
                nc.vector.scalar_tensor_tensor(out=x[:, i, :], in0=x[:, i, :], scalar=r[:, i:i + 1],
                                               in1=shift[:, :], op0=ALU.mult, op1=ALU.add).then_inc(normed, 1)
            if x_t is not None:
                for c in range(NK):
                    dve.wait_ge(hi_copied, n * NK + c + 1)
                    split_lower(nc.vector, k.bank[c % 4][:, :], x_t.hi[:, c, :], x_t.lo[:, c, :]).then_inc(copied, 1)

        @block.scalar
        def _(act):
            act.wait_ge(var_ready, n + 1)
            nc.scalar.activation(std[:, :], ve[:, :], ACT.Sqrt).then_inc(std_ready, 1)
            if x_t is not None:
                for c in range(NK):
                    act.wait_ge(transposed, n * NK + c + 1)
                    nc.scalar.copy(x_t.hi[:, c, :], k.bank[c % 4][:, :]).then_inc(hi_copied, 1)

        if x_t is not None:
            @block.tensor
            def _(pe):
                for c in range(NK):
                    if c >= 4:
                        pe.wait_ge(copied, n * NK + c - 3)
                    for i in range(NT):
                        if c == 0:
                            pe.wait_ge(normed, n * NT + i + 1)
                        last = nc.tensor.transpose(k.bank[c % 4][:, i * P:(i + 1) * P],
                                                   x[:, i, c * P:(c + 1) * P], k.ident)
                    last.then_inc(transposed, 1)

    k.norm.counted(var_ready=1)


def load_ahead(sp, k, weights):
    width = weights.shape[2]
    sp.dma_start(k.ahead[:, :, 0:width], weights).then_inc(k.ahead_in, 16)
    k.ahead_loads += 16


def setup_stage(nc, k, A):
    with Stage(nc, "setup") as st:
        x_in, const_in = [st.sem(f"x{h}_in") for h in range(2)], st.sem("const_in")
        block = st.block()

        @block.sync
        def _(sp):
            for h in range(2):
                sp.dma_start(k.x[:, 2 * h:2 * h + 2, :], A["x"][0, 2 * h * P:2 * (h + 1) * P, :]
                             .rearrange("(i p) n -> p i n", p=P)).then_inc(x_in[h], 16)
            for h in range(2):
                sp.wait_ge(x_in[h], 16)
            load_ahead(sp, k, column_tiles(A["w_in"][0], 2 * WA, 512))

        @block.scalar
        def _(act):
            act.dma_start(k.const[:, :], A["c_f32"]).then_inc(const_in, 16)
            act.wait_ge(const_in, 16)

        @block.vector
        def _(dve):
            for i in range(NT):
                dve.wait_ge(x_in[i // 2], 16)
                statistics(nc, k, i)


def tables_stage(nc, k, A, alibi):
    with Stage(nc, "tables") as st:
        rb, onehot, table = st.sb("rb", [8, 257]), st.sb("onehot", [32, 512]), st.sb("table", [32, 6])
        wb, wt = k.band_row, k.t5_row
        lv, lp, lsum, lexp = (st.sb("lv", [P, 4, HD]), st.sb("lp", [P, 2, HD]), st.sb("lsum", [P, 2]),
                              st.sb("lexp", [P, 2]))
        small_in, lam_in, mask_in = st.sem("small_in"), st.sem("lam_in"), st.sem("mask_in")
        band_row, t5_ps, t5_row = st.sem("band_row"), st.sem("t5_ps"), st.sem("t5_row")
        lam_sum, lam_exp = st.sem("lam_sum"), st.sem("lam_exp")
        block = st.block()

        @block.sync
        def _(sp):
            sp.dma_start(rb[:, :], A["rel_bias"][0]).then_inc(small_in, 16)
            sp.dma_start(onehot[:, :], A["c_onehot"]).then_inc(small_in, 16)
            sp.dma_start(table[:, :], A["rel_bias_2"]).then_inc(small_in, 16)
            sp.dma_start(k.hg_mask[:, :], A["c_mask"]).then_inc(mask_in, 16)
            sp.wait_ge(band_row, 1)
            sp.dma_start(k.z_band[:, :, :], wb[:, :].unsqueeze(1).to_broadcast([8, P, 640])).then_inc(k.band_stored, 16)
            sp.wait_ge(t5_row, 1)
            sp.dma_start(k.z_t5[:, :, :], wt[:, :].unsqueeze(1).to_broadcast([6, P, 1024])).then_inc(k.t5_stored, 16)
            sp.wait_ge(mask_in, 16)

        @block.scalar
        def _(act):
            for n, v in enumerate(("lambda_q1", "lambda_k1", "lambda_q2", "lambda_k2")):
                act.dma_start(lv[:, n, :], row_broadcast(A[v][0])).then_inc(lam_in, 16)
            act.wait_ge(lam_sum, 1)
            nc.scalar.activation(lexp[:, :], lsum[:, :], ACT.Exp).then_inc(lam_exp, 1)

        @block.vector
        def _(dve):
            for h in range(4):
                nc.vector.tensor_scalar(alibi[:, h, :], k.const[:, C_DIST:C_DIST + S], 2.0 ** (-2 * (h + 1)),
                                        None, ALU.mult)
            dve.drain()
            nc.vector.memset(alibi[0:HD, :, S - HD:S], NEG)
            dve.wait_ge(small_in, 48)
            nc.vector.tensor_copy(wb[:, 0:383], rb[:, 0:1].to_broadcast([8, 383]))
            nc.vector.memset(wb[:, 639:640], 0.0)
            nc.vector.tensor_copy(wb[:, 383:639], rb[:, 0:256]).then_inc(band_row, 1)
            nc.vector.memset(wt[:, 512:1024], NEG)
            dve.wait_ge(t5_ps, 1)
            nc.vector.tensor_copy(wt[:, 0:512], k.bank[0][0:6, :]).then_inc(t5_row, 1)
            dve.wait_ge(lam_in, 64)
            nc.vector.tensor_tensor(lp[:, 0, :], lv[:, 0, :], lv[:, 1, :], ALU.mult)
            nc.vector.tensor_tensor(lp[:, 1, :], lv[:, 2, :], lv[:, 3, :], ALU.mult)
            dve.drain()
            nc.vector.tensor_reduce(lsum[:, :], lp[:, :, :], AX.X, ALU.add).then_inc(lam_sum, 1)
            dve.wait_ge(lam_exp, 1)
            nc.vector.tensor_tensor(k.neg_lam[:, :], lexp[:, 1:2], lexp[:, 0:1], ALU.subtract)
            dve.drain()
            nc.vector.tensor_scalar(k.neg_lam[:, :], k.neg_lam[:, :], -LAM_INIT, None, ALU.add)

        @block.tensor
        def _(pe):
            pe.wait_ge(small_in, 48)
            nc.tensor.matmul(k.bank[0][0:6, :], table[:, :], onehot[:, :], start=True, stop=True).then_inc(t5_ps, 1)


BETWEEN_LAG = 2
LOOK, NORM_LAG, COPY_LAG, PV_LAG = 2, 2, 3, 4


class Items:

    def __init__(self, tiles):
        self.tiles, self.n = tiles, len(tiles)

    def blocks(self, n):
        keys = self.tiles[n]["keys"]
        return [(j, min(P, keys - j * P)) for j in range((keys + P - 1) // P)]


ATTENTION_SEMS = ("scored", "biased", "exped", "normed", "transposed", "copied", "weighed", "out_copied")


def attention_buffers(k, st):
    b = dict(scores=st.sb("scores", [P, 4, S]), pt=st.sb("pt", [P, 3, S]), nm=st.sb("nm", [P, 4]),
             l=st.sb("l", [P, 4]), tiles_done=k.attention.done["scored"], out_done=k.attention.done["out_copied"])
    b.update((name, k.attention[name]) for name in ATTENTION_SEMS)
    return b


def attention_pe(nc, pe, k, items, b, u, between=()):
    N, between = items.n, list(between)
    per_step = -(-len(between) // (N + PV_LAG - BETWEEN_LAG))
    at = b["tiles_done"] + u * N
    for t in range(N + PV_LAG):
        if t < N:
            it = items.tiles[t]
            if t >= LOOK:
                pe.wait_ge(b["biased"], at + t - LOOK + 1)
            nc.tensor.matmul(k.bank[t % 2][:, 0:it["keys"]], it["q"], it["kt"], start=True, stop=True)\
                .then_inc(b["scored"], 1)
        for piece in between[max(0, t - BETWEEN_LAG) * per_step:max(0, t + 1 - BETWEEN_LAG) * per_step]:
            piece()
        n = t - COPY_LAG
        if 0 <= n < N:
            pe.wait_ge(b["normed"], at + n + 1)
            if n >= 2:
                pe.wait_ge(b["copied"], at + n - 1)
            for j, rows in items.blocks(n):
                last = nc.tensor.transpose(k.bank[3 + n % 2][0:rows, j * P:(j + 1) * P],
                                           b["scores"][:, n % 4, j * P:j * P + rows], k.ident)
            last.then_inc(b["transposed"], 1)
        n = t - PV_LAG
        if 0 <= n < N:
            it = items.tiles[n]
            pe.wait_ge(b["copied"], at + n + 1)
            if it["first"] and (n == 0 or items.tiles[n - 1]["i"] != it["i"]):
                pe.wait_ge(b["out_copied"], b["out_done"] + u * NT + it["i"] + 1)
            col, width = it["out"]
            blocks = items.blocks(n)
            for j, rows in blocks:
                last = nc.tensor.matmul(k.bank[5 + it["i"] % 2][:, col:col + width],
                                        b["pt"][0:rows, n % 3, j * P:(j + 1) * P], it["v"](u, j),
                                        start=it["first"] and j == 0, stop=it["last"] and j == len(blocks) - 1)
            last.then_inc(b["weighed"], 1)


def attention_dve(nc, dve, k, items, b, u, copy_out):
    N = items.n
    at = b["tiles_done"] + u * N
    for t in range(N + PV_LAG + 1):
        if t < N:
            it = items.tiles[t]
            s = b["scores"][:, t % 4, 0:it["keys"]]
            dve.wait_ge(b["scored"], at + t + 1)
            if t >= 4:
                dve.wait_ge(b["transposed"], at + t - 3)
            nc.vector.tensor_tensor(s, k.bank[t % 2][:, 0:it["keys"]], it["bias"](u), ALU.add)
            dve.drain()
            nc.vector.tensor_reduce(b["nm"][:, t % 4:t % 4 + 1], s, AX.X, ALU.max, negate=True)\
                .then_inc(b["biased"], 1)
        n = t - NORM_LAG
        if 0 <= n < N:
            it = items.tiles[n]
            e, l = b["scores"][:, n % 4, 0:it["keys"]], b["l"][:, n % 4:n % 4 + 1]
            dve.wait_ge(b["exped"], at + n + 1)
            nc.vector.reciprocal(l, l)
            if it["masked"]:
                nc.vector.scalar_tensor_tensor(out=e, in0=it["bias"](u), scalar=0.1 * NEG, in1=e,
                                               op0=ALU.is_gt, op1=ALU.mult)
            dve.drain()
            extra = it["scale"](u)
            if extra is None:
                nc.vector.tensor_scalar(e, e, l, None, ALU.mult).then_inc(b["normed"], 1)
            else:
                nc.vector.tensor_scalar(e, e, l, extra, ALU.mult, ALU.mult).then_inc(b["normed"], 1)
        n = t - PV_LAG - 1
        if 0 <= n < N and (n == N - 1 or items.tiles[n + 1]["i"] != items.tiles[n]["i"]):
            dve.wait_ge(b["weighed"], at + n + 1)
            copy_out(u, items.tiles[n]["i"]).then_inc(b["out_copied"], 1)


def attention_act(nc, act, k, items, b, u):
    N = items.n
    at = b["tiles_done"] + u * N
    for t in range(N + COPY_LAG):
        if t < N:
            s = b["scores"][:, t % 4, 0:items.tiles[t]["keys"]]
            act.wait_ge(b["biased"], at + t + 1)
            nc.scalar.activation(s, s, ACT.Exp, bias=b["nm"][:, t % 4:t % 4 + 1],
                                 accum_out=b["l"][:, t % 4:t % 4 + 1]).then_inc(b["exped"], 1)
        n = t - COPY_LAG
        if 0 <= n < N:
            blocks = items.blocks(n)
            rows, cols = blocks[0][1], len(blocks) * P
            act.wait_ge(b["transposed"], at + n + 1)
            if n >= 3:
                act.wait_ge(b["weighed"], at + n - 2)
            nc.scalar.activation(b["pt"][0:rows, n % 3, 0:cols], k.bank[3 + n % 2][0:rows, 0:cols],
                                 ACT.Copy).then_inc(b["copied"], 1)


def load_band_table(sp, k, table):
    sp.wait_ge(k.band_stored, 16)
    sp.wait_ge(k.t5_stored, 16)
    skewed = bass.AP(k.z_band_handle, P - 1, [[639, P], [P * 640, 8], [1, S]])
    sp.dma_start(table[:, :, :], skewed).then_inc(k.band_table_in, 16)


def band_bias_stage(nc, k, table):
    with Stage(nc, "bandbias") as st:
        block = st.block()

        @block.vector
        def _(dve):
            dve.wait_ge(k.band_table_in, 16)
            nc.vector.memset(table[0:HD, :, S - HD:S], NEG)


def wait_carrier(engine, carrier):
    engine.tensor_tensor(carrier[:, 0:1], carrier[:, 1:2], carrier[:, 1:2], ALU.add)


UNIT_SEMS = ("w_in", "w_hi", "w_split", "projected", "evacuated", "v_hi", "v_lo", "v_ps", "v_sb", "zeroed")


def heads_stage(nc, name, k, units, load, projections, items, values, place, copy_out, keys=None):
    with Stage(nc, name) as st:
        raw, upper = st.sb("raw", [P, projections, NK, P]), st.sb("upper", [P, projections, NK, P], F32R)
        lower = st.sb("lower", [P, projections, NK, P], F32R)
        w = Split(upper, lower)
        b = attention_buffers(k, st)
        w_in, w_hi, w_split, projected, evacuated, v_hi, v_lo, v_ps, v_sb, zeroed = (k.units[x] for x in UNIT_SEMS)
        w_hi0 = k.units.done["w_split"]
        loads = 16 * k.loads_per_unit
        w_in0, split0, projected0, evacuated0, v0, zeroed0 = (
            k.units.done[x] for x in ("w_in", "w_split", "projected", "evacuated", "v_hi", "zeroed"))
        BANKS = (2, 7)
        PIECES = [(n, c) for n in range(projections) for c in range(NK)]
        if values is not None:
            v_upper = st.sb("v_upper", [P, NK, 512], F32R)
            v_w = Split(v_upper[:, :, :], k.ahead_lower[:, :, :])
        block = st.block()

        @block.sync
        def _(sp):
            for dma in load(sp, 0, raw):
                dma.then_inc(w_in, 16)
            with sp.Fori(1, units) as u:
                sp.wait_ge(w_split, split0 + u * projections)
                for dma in load(sp, u, raw):
                    dma.then_inc(w_in, 16)

        @block.gpsimd
        def _(pool):
            with pool.Fori(0, units) as u:
                for n in range(projections):
                    pool.wait_ge(w_hi, w_hi0 + u * projections + n + 1)
                    split_lower(nc.gpsimd, raw[:, n, :, :], upper[:, n, :, :], lower[:, n, :, :]).then_inc(w_split, 1)

        @block.tensor
        def _(pe):
            def project(u, n, c):
                if c == 0:
                    pe.wait_ge(w_split, split0 + u * projections + n + 1)
                last = split_product(nc, k.bank[BANKS[n]][:, :], w[:, n, c, :], k.x_parts[:, c, :],
                                     c == 0, c == NK - 1)
                if c == NK - 1:
                    last.then_inc(projected, 1)

            if values is not None:
                for h in range(4):
                    pe.wait_ge(v_lo, v0 + h + 1)
                    for i in range(NT):
                        for c in (2 * h, 2 * h + 1):
                            last = split_product(nc, k.bank[3 + i][:, :], k.x_parts[:, c, i * P:(i + 1) * P],
                                                 v_w[:, c, :], c == 0, c == NK - 1)
                        if h == 3:
                            last.then_inc(v_ps, 1)
            for n, c in PIECES:
                project(0, n, c)
            if values is not None:
                pe.wait_ge(v_sb, v0 + NT)
            pe.wait_ge(zeroed, zeroed0 + 1)
            with pe.Fori(0, units - 1) as u:
                pe.wait_ge(evacuated, evacuated0 + u * 2 + 2)
                attention_pe(nc, pe, k, items, b, u, [lambda n=n, c=c: project(u + 1, n, c) for n, c in PIECES])
            pe.wait_ge(evacuated, evacuated0 + units * 2)
            attention_pe(nc, pe, k, items, b, units - 1, [])

        @block.scalar
        def _(act):
            def upper_parts(u):
                act.wait_ge(w_in, w_in0 + u * loads + loads)
                for n in range(projections):
                    nc.scalar.copy(upper[:, n, :, :], raw[:, n, :, :]).then_inc(w_hi, 1)

            if values is not None:
                act.wait_ge(k.ahead_in, k.ahead_loads)
                for h in range(4):
                    nc.scalar.copy(v_upper[:, 2 * h:2 * h + 2, :], k.ahead[:, 2 * h:2 * h + 2, :]).then_inc(v_hi, 1)
            upper_parts(0)
            if values is not None:
                for i in (0, 2):
                    act.wait_ge(v_ps, v0 + i + 1)
                    nc.scalar.copy(values[:, i, :], k.bank[3 + i][:, :]).then_inc(v_sb, 1)
            with act.Fori(0, units) as u:
                act.wait_ge(projected, projected0 + u * projections + projections)
                for m in range(2):
                    rows = slice(HD * m, HD * m + HD)
                    last = nc.scalar.activation(place["q"][m][rows, :], k.bank[BANKS[0]][rows, :], ACT.Copy,
                                                scale=HD ** -0.5)
                last.then_inc(evacuated, 1 if keys is not None else 2)
                with act.If(u < units - 1):
                    upper_parts(u + 1)
                attention_act(nc, act, k, items, b, u)

        @block.vector
        def _(dve):
            if values is not None:
                for h in range(4):
                    dve.wait_ge(v_hi, v0 + h + 1)
                    part = slice(2 * h, 2 * h + 2)
                    split_lower(nc.vector, k.ahead[:, part, :], v_upper[:, part, :],
                                v_w.lo[:, part, :]).then_inc(v_lo, 1)
                for i in (1, 3):
                    dve.wait_ge(v_ps, v0 + i + 1)
                    nc.vector.tensor_copy(values[:, i, :], k.bank[3 + i][:, :]).then_inc(v_sb, 1)
            for m in range(2):
                nc.vector.memset(place["q"][m][HD - HD * m:P - HD * m, :], 0.0)
            if b["out_done"] == 0:
                dve.drain().then_inc(b["out_copied"], 2)
            dve.drain().then_inc(zeroed, 1)
            with dve.Fori(0, units) as u:
                if keys is not None:
                    dve.wait_ge(projected, projected0 + u * projections + projections)
                    nc.vector.tensor_copy(keys, k.bank[BANKS[1]][:, :]).then_inc(evacuated, 1)
                attention_dve(nc, dve, k, items, b, u, copy_out)

    k.attention.counted(scored=units * items.n, out_copied=units * NT)
    k.units.counted(w_in=16 * k.loads_per_unit * units, w_split=units * projections, projected=units * projections,
                    evacuated=2 * units, zeroed=1, v_hi=NT if values is not None else 0)


def first_attention_stage(nc, name, k, w, first_q, first_k, bias, shared_v, scale, out):
    with Stage(nc, name + "_heads") as st:
        q, kt = [st.sb(f"q{m}", [P, S]) for m in range(2)], st.sb("kt", [P, S])
        v = st.sb("v", [P, NT, 512])
        width = P if shared_v else HD
        tiles = []
        for i in range(NT):
            for m in range(2):
                col = 0 if shared_v else HD * m
                tiles.append(dict(
                    i=i, keys=(i + 1) * P, q=q[m][:, i * P:(i + 1) * P], kt=kt[:, 0:(i + 1) * P],
                    bias=lambda u, i=i, m=m: bias(u, m, (NT - 1 - i) * P, (i + 1) * P),
                    v=lambda u, j, col=col: v[:, ds(j, 1), ds(u * P + col, width)].rearrange("p o n -> p (o n)"),
                    out=(col, width), first=m == 0 or not shared_v, last=m == 1 or not shared_v, masked=False,
                    scale=lambda u, m=m: scale(m)))

        def load(sp, u, raw):
            return [sp.dma_start(raw[:, n, :, :], column_tiles(w, first + u * P))
                    for n, first in enumerate((first_q, first_k))]

        def copy_out(u, i):
            return nc.vector.tensor_copy(out[:, i, ds(u * P, P)], k.bank[5 + i % 2][:, 0:P])

        k.loads_per_unit = 2
        heads_stage(nc, name, k, 4, load, 2, Items(tiles), v, dict(q=q), copy_out, keys=kt[:, :])


HEADS_SEMS = ("ready", "transposed", "sum_ready", "std_ready", "weight_in", "weight_ready", "tile_out")


def transpose_heads_stage(nc, name, k, o, o_t, heads=0, weight=None, eps=LN_EPS, factor=1.0, ahead=None):
    width = o.shape[2]
    tiles = width // P
    n, t0 = k.heads.done["ready"], k.heads.done["transposed"]
    with Stage(nc, name) as st:
        ready, transposed, sum_ready, std_ready, weight_in, weight_ready, tile_out = (
            k.heads[x] for x in HEADS_SEMS)
        parts = isinstance(o_t, Split)
        out = o_t.whole if parts else o_t
        sq = sums = wcol = None
        if heads:
            hw = width // heads
            sq, sums, std = st.sb("sq", [P, NT, width]), st.sb("sums", [P, NT * heads]), st.sb("std", [P, NT * heads])
            wcol = st.sb("wcol", [P, weight.shape[1]])
        block = st.block()

        @block.sync
        def _(sp):
            if heads:
                with nc.allow_non_contiguous_dma(reason="a column of weights"):
                    sp.dma_start(wcol[:, :], weight).then_inc(weight_in, 16)
            if ahead is not None:
                ahead(sp)

        @block.vector
        def _(dve):
            if heads:
                dve.wait_ge(weight_in, 16 * n + 16)
                nc.vector.tensor_scalar(wcol[:, :], wcol[:, :], factor, None, ALU.mult).then_inc(weight_ready, 1)
                nc.vector.tensor_tensor(sq[:, :, :], o, o, ALU.mult)
                dve.drain()
                nc.vector.tensor_reduce(sums[:, :], sq[:, :, :].rearrange("p i (h e) -> p (i h) e", e=hw),
                                        AX.X, ALU.add)
                dve.drain()
                nc.vector.tensor_scalar(sums[:, :], sums[:, :], 1.0 / hw, eps, ALU.mult, ALU.add)\
                    .then_inc(sum_ready, 1)
                dve.wait_ge(std_ready, n + 1)
                nc.vector.reciprocal(sums[:, :], std[:, :])
                dve.drain()
                o3 = o.rearrange("p i (h e) -> p (i h) e", e=hw)
                r3 = sums[:, :].unsqueeze(2).to_broadcast([P, NT * heads, hw])
                nc.vector.tensor_tensor(o3, o3, r3, ALU.mult).then_inc(ready, 1)
            if parts:
                for c in range(tiles):
                    dve.wait_ge(tile_out, t0 + c + 1)
                    nc.vector.tensor_copy(o_t.hi[:, c, :], out[:, c, :])
                    dve.drain()
                    split_lower(nc.vector, out[:, c, :], o_t.hi[:, c, :], o_t.lo[:, c, :])

        @block.scalar
        def _(act):
            if heads:
                act.wait_ge(sum_ready, n + 1)
                nc.scalar.activation(std[:, :], sums[:, :], ACT.Sqrt).then_inc(std_ready, 1)
                act.wait_ge(weight_ready, n + 1)
            for c in range(tiles):
                act.wait_ge(transposed, t0 + c + 1)
                if heads:
                    w1 = wcol[:, c % wcol.shape[1]:c % wcol.shape[1] + 1]
                    nc.scalar.activation(out[:, c, :], k.bank[c][:, :], ACT.Copy, scale=w1).then_inc(tile_out, 1)
                else:
                    nc.scalar.copy(out[:, c, :], k.bank[c][:, :]).then_inc(tile_out, 1)

        @block.tensor
        def _(pe):
            if heads:
                pe.wait_ge(ready, n + 1)
            for c in range(tiles):
                for i in range(NT):
                    last = nc.tensor.transpose(k.bank[c][:, i * P:(i + 1) * P], o[:, i, c * P:(c + 1) * P], k.ident)
                last.then_inc(transposed, 1)

    k.heads.counted(transposed=tiles, ready=1 if heads else 0)


def load_merge(sp, w_in, branches, raw, f, loaded):
    for g in range(2):
        sp.dma_start(raw[:, NK * g:NK * g + NK, :], column_tiles(w_in, 3072 + D * g + f * P)).then_inc(loaded, 16)
        sp.dma_start(raw[:, 16 + 4 * g:20 + 4 * g, :], column_tiles(branches[g], f * P)).then_inc(loaded, 16)


def merge_stage(nc, k, A, oa_t, ob_t, m_t):
    w_in_all, branches = A["w_in"][0], (A["w_branch_a"][0], A["w_branch_b"][0])
    GATES, BRANCHES = slice(0, 16), slice(16, 24)
    ahead_loads = k.ahead_loads
    with Stage(nc, "merge") as st:
        raw1, lower1 = st.overlaid("raw", [P, 24, P])
        raw, lower = [k.ahead_tiles[:, 0:24, :], raw1[:, :, :]], [k.ahead_lower_tiles[:, 0:24, :], lower1[:, :, :]]
        upper = [st.sb(f"upper{p}", [P, 24, P], F32R)[:, :, :] for p in range(2)]
        w = [Split(upper[p], lower[p]) for p in range(2)]
        bg, bcol, sig = st.sb("bg", [P, 2, NK + 1]), st.sb("bcol", [P, 2]), st.sb("sig", [P, 2, S])
        bg_in, gates_ps, branches_ps = (st.sem(n) for n in ("bg_in", "gates_ps", "branches_ps"))
        w_in = [st.sem("w0_in"), st.sem("w1_in")]
        gates, merged, tmp = st.sem("gates"), st.sem("merged"), st.sb("tmp", [P, S])
        w_hi, w_lo = st.sem("w_hi"), st.sem("w_lo")
        block = st.block()

        @block.sync
        def _(sp):
            with nc.allow_non_contiguous_dma(reason="a column of biases"):
                for g in range(2):
                    sp.dma_start(bg[:, g, 0:NK], A["b_gate"][0][g * D:(g + 1) * D].rearrange("(k p) -> p k", p=P))\
                        .then_inc(bg_in, 16)
            load_merge(sp, w_in_all, branches, raw[1], 1, w_in[1])
            with sp.Fori(1, NK // 2) as q:
                for p in range(2):
                    f = q * 2 + p
                    sp.wait_ge(branches_ps, f - 1)
                    load_merge(sp, w_in_all, branches, raw[p], f, w_in[p])
            sp.wait_ge(branches_ps, NK - 1)
            load_ahead(sp, k, column_tiles(A["w_out"][0], 0, 512))

        @block.gpsimd
        def _(pool):
            def split(p, f):
                for n, part in enumerate((GATES, BRANCHES)):
                    pool.wait_ge(w_hi, f * 2 + n + 1)
                    split_lower(nc.gpsimd, raw[p][:, part, :], upper[p][:, part, :], w[p].lo[:, part, :])\
                        .then_inc(w_lo, 1)

            with pool.Fori(0, NK // 2) as q:
                for p in range(2):
                    split(p, q * 2 + p)

        @block.tensor
        def _(pe):
            with pe.Fori(0, NK // 2) as q:
                for p in range(2):
                    f = q * 2 + p
                    pe.wait_ge(w_lo, f * 2 + 1)
                    pe.wait_ge(gates, f * 2 + 1)
                    for g in range(2):
                        for c in range(NK):
                            last = split_product(nc, k.bank[g][:, :], w[p][:, NK * g + c, :], k.x_parts[:, c, :],
                                                 c == 0, c == NK - 1)
                        last.then_inc(gates_ps, 1)
                    pe.wait_ge(w_lo, f * 2 + 2)
                    pe.wait_ge(merged, f + 1)
                    for g, o_t in enumerate((oa_t, ob_t)):
                        for c in range(4):
                            last = split_product(nc, k.bank[2 + g][:, :], w[p][:, 16 + 4 * g + c, :], o_t[:, c, :],
                                                 c == 0, c == 3)
                    last.then_inc(branches_ps, 1)

        @block.scalar
        def _(act):
            def upper_parts(p, f, loaded):
                act.wait_ge(*loaded)
                for part in (GATES, BRANCHES):
                    nc.scalar.copy(upper[p][:, part, :], raw[p][:, part, :]).then_inc(w_hi, 1)

            upper_parts(0, 0, (k.ahead_in, ahead_loads))
            act.drain().then_inc(gates, 1)
            upper_parts(1, 1, (w_in[1], 64))
            with act.Fori(0, NK // 2) as q:
                for p in range(2):
                    f = q * 2 + p
                    act.wait_ge(merged, f + 1)
                    for g in range(2):
                        act.wait_ge(gates_ps, f * 2 + g + 1)
                        nc.scalar.activation(sig[:, g, :], k.bank[g][:, :], ACT.Sigmoid, bias=bcol[:, g:g + 1])\
                            .then_inc(gates, 1)
                    with act.If(q < NK // 2 - 1):
                        act.wait_ge(branches_ps, f + 1)
                        upper_parts(p, f + 2, (w_in[p], q * 64 + 64 + 64 * p))

        @block.vector
        def _(dve):
            nc.vector.memset(bg[:, :, NK:NK + 1], 0.0)
            dve.wait_ge(bg_in, 32)
            nc.vector.tensor_copy(bcol[:, :], bg[:, :, 0])
            dve.drain().then_inc(merged, 1)
            with dve.Fori(0, NK) as f:
                dve.wait_ge(branches_ps, f + 1)
                dve.wait_ge(gates, f * 2 + 3)
                nc.vector.tensor_tensor(tmp[:, :], sig[:, 0, :], k.bank[2][:, :], ALU.mult)
                nc.vector.tensor_tensor(sig[:, 1, :], sig[:, 1, :], k.bank[3][:, :], ALU.mult)
                dve.drain()
                nc.vector.tensor_tensor(m_t[:, ds(f, 1), :], tmp[:, :].unsqueeze(1), sig[:, 1, :].unsqueeze(1),
                                        ALU.add)
                nc.vector.tensor_copy(bcol[:, :].unsqueeze(2), bg[:, :, ds(f + 1, 1)])
                dve.drain().then_inc(merged, 1)


OUTPUT_SEMS = ("w0_in", "w1_in", "m_hi", "m_lo", "w_hi", "w_lo", "product", "added")


def output_stage(nc, name, k, w_dram, m_t, m_lower, x):
    o = k.output.done["w0_in"]
    with Stage(nc, name) as st:
        raw1, lower1 = st.overlaid("w", [P, NK, 512])
        raws = [k.ahead[:, :, :], raw1[:, :, :]]
        w = [Split(k.x_parts.lo, k.ahead_lower[:, :, :]), Split(st.sb("upper", [P, NK, 512], F32R)[:, :, :],
                                                                lower1[:, :, :])]
        m = Split(k.x_parts.hi, m_lower)
        w0_in, w1_in, m_hi, m_lo, w_hi, w_lo, product, added = (k.output[n] for n in OUTPUT_SEMS)
        loaded = [(k.ahead_in, k.ahead_loads), (w1_in, 16 * o + 16)]
        block = st.block()

        @block.sync
        def _(sp):
            sp.dma_start(raws[1], column_tiles(w_dram, 512, 512)).then_inc(w1_in, 16)

        @block.scalar
        def _(act):
            for c in range(2):
                act.wait_ge(*loaded[c])
                for t in range(NK):
                    if c == 0:
                        nc.scalar.copy(m.hi[:, t, :], m_t[:, t, :]).then_inc(m_hi, 1)
                    nc.scalar.copy(w[c].hi[:, t, :], raws[c][:, t, :]).then_inc(w_hi, 1)

        @block.gpsimd
        def _(pool):
            for c in range(2):
                for t in range(NK):
                    pool.wait_ge(w_hi, 2 * NK * o + NK * c + t + 1)
                    split_lower(nc.gpsimd, raws[c][:, t, :], w[c].hi[:, t, :], w[c].lo[:, t, :]).then_inc(w_lo, 1)

        @block.tensor
        def _(pe):
            for c in range(2):
                for i in range(NT):
                    n = c * NT + i
                    if n >= 4:
                        pe.wait_ge(added, 2 * NT * o + n - 3)
                    for t in range(NK):
                        if n == 0:
                            pe.wait_ge(m_lo, NK * o + t + 1)
                        if i == 0:
                            pe.wait_ge(w_lo, 2 * NK * o + NK * c + t + 1)
                        last = split_product(nc, k.bank[n % 4][:, :], m[:, t, i * P:(i + 1) * P], w[c][:, t, :],
                                             t == 0, t == NK - 1)
                    last.then_inc(product, 1)

        @block.vector
        def _(dve):
            for t in range(NK):
                dve.wait_ge(m_hi, NK * o + t + 1)
                split_lower(nc.vector, m_t[:, t, :], m.hi[:, t, :], m.lo[:, t, :]).then_inc(m_lo, 1)
            for c in range(2):
                for i in range(NT):
                    n = c * NT + i
                    xs = x[:, i, 512 * c:512 * c + 512]
                    dve.wait_ge(product, 2 * NT * o + n + 1)
                    nc.vector.scalar_tensor_tensor(out=xs, in0=xs, scalar=ALPHA, in1=k.bank[n % 4][:, :],
                                                   op0=ALU.mult, op1=ALU.add).then_inc(added, 1)
                    dve.drain()
                    statistics(nc, k, i, (c,))

    k.output.counted(w0_in=1)


HALVES = 12
LOADED, SPLIT = 8, 4
PIECES = [(c, kh) for c in (0, FF, 512, FF + 512) for kh in range(2)] + [(c, kh) for kh in range(2) for c in (0, 512)]


def weight_piece(A, e, h):
    col, kh = PIECES[h]
    w = A["w_exp_in" if h < 8 else "w_exp_out"][0].rearrange("e (k p) n -> e p k n", p=P)
    return w[ds(e, 1), :, 4 * kh:4 * kh + 4, col:col + 512].rearrange("o p k n -> (o p) k n")


def route_stage(nc, k, A, r):
    with Stage(nc, "route") as st:
        (wr, wr_lower), br = st.overlaid("wr", [P, NK, NE]), st.sb("br", [P, NE])
        logits, top, idx = st.sb("logits", [P, NT, NE]), st.sb("top", [P, NT, 8]), st.sb("idx", [P, NT, 8], U32)
        idxf, nmax, wsum = st.sb("idxf", [P, NT, 8]), st.sb("nmax", [P, NT]), st.sb("wsum", [P, NT])
        pick = st.sb("pick", [P, NT, TOPK, NE])
        chosen = st.sb("chosen", [P, NT, NE])
        counts, nb, ends = st.sb("counts", [P, NE]), st.sb("nb", [P, NE]), st.sb("ends", [P, NE])
        step, starts, zero = st.sb("step", [P, NE]), st.sb("starts", [P, NE]), st.sb("zero", [P, NE])
        dest, picked = st.sb("dest", [P, NT, NE]), st.sb("picked", [P, NT, TOPK, NE])
        destk = st.sb("destk", [P, NT * TOPK])
        desti, lane_i, blk_i = (st.sb(n, [P, NT * TOPK], I32) for n in ("desti", "lane_i", "blk_i"))
        lane_f, blk_f = st.sb("lane_f", [P, NT * TOPK]), st.sb("blk_f", [P, NT * TOPK])
        slot_no = st.sb("slot_no", [P, NT * TOPK])
        lane_hot, blk_hot = st.sb("lane_hot", [P, 16, P]), st.sb("blk_hot", [P, 16, MAX_BLOCKS])
        before = st.sb("before", [P, MAX_BLOCKS, NE])
        slots, token, row, isnone = (st.sb(n, [P, MAX_BLOCKS]) for n in ("slots", "token", "row", "isnone"))
        token_i = st.sb("token_i", [P, MAX_BLOCKS], I32)
        w_in, logits_ps = st.sem("w_in"), st.sem("logits_ps")
        exped, chosen_ready, counted = (st.sem(n) for n in ("exped", "chosen_ready", "counted"))
        slot_ready, hot, listed = st.sem("slot_ready"), st.sem("hot"), st.sem("listed")
        top_ready, wr_split, s0 = st.sem("top_ready"), k.split["lo_ready"], k.split.done["lo_ready"]
        wr_hi = st.sb("wr_hi", [P, NK, NE], F32R)
        wr_parts = Split(wr_hi[:, :, :], wr_lower[:, :, :])
        full, hi = st.sb("full", [96, 3 * FF]), st.sb("hi", [96, 3 * FF], BF16)
        bias_in, bias_hi, bias_rest = st.sem("bias_in"), st.sem("bias_hi"), st.sem("bias_rest")
        expert_ready = st.sem("expert_ready")
        block = st.block()

        @block.sync
        def _(sp):
            sp.dma_start(wr[:, :, :], A["w_router"][0].rearrange("(k p) n -> p k n", p=P)).then_inc(w_in, 16)
            sp.dma_start(br[:, :], row_broadcast(A["b_router"][0])).then_inc(w_in, 16)
            for g in range(3):
                rows = full[32 * g:32 * g + 32, :]
                sp.dma_start(rows[:, 0:2 * FF], A["b_exp_in"][0]).then_inc(bias_in, 16)
                sp.dma_start(rows[:, 2 * FF:3 * FF], A["b_exp_out"][0]).then_inc(bias_in, 16)
            sp.wait_ge(expert_ready, 1)
            e = sp.value_load(r.expert_i[0:1, 0:1], min_val=0, max_val=NE - 1)
            for h in range(LOADED):
                sp.dma_start(r.ring[h][:, :, :], weight_piece(A, e, h)).then_inc(r.piece_in[h], 16)

        @block.gpsimd
        def _(pool):
            nc.gpsimd.iota(slot_no[:, :], pattern=[[P * TOPK, NT], [1, TOPK]], base=1, channel_multiplier=TOPK,
                           allow_small_or_imprecise_dtypes=True).then_inc(slot_ready, 1)
            for g in range(2):
                pool.wait_ge(bias_hi, g + 1)
                nc.gpsimd.tensor_tensor(full[:, :], full[:, :], hi[:, :], ALU.subtract)
                pool.drain().then_inc(bias_rest, 1)

        @block.tensor
        def _(pe):
            pe.wait_ge(wr_split, s0 + 1)
            for i in range(NT):
                for c in range(NK):
                    last = split_product(nc, k.bank[i][:, 0:NE], k.x_parts[:, c, i * P:(i + 1) * P],
                                         wr_parts[:, c, :], c == 0, c == NK - 1)
                last.then_inc(logits_ps, 1)
            pe.wait_ge(chosen_ready, 1)
            for i in range(NT):
                nc.tensor.matmul(k.bank[4][:, 0:NE], k.const[:, C_ONE:C_ONE + P], chosen[:, i, :],
                                 start=i == 0, stop=i == NT - 1)
            for i in range(NT):
                for h in range(i + 1):
                    earlier = C_LT if h == i else C_ONE
                    last = nc.tensor.matmul(k.bank[i][:, 0:NE], k.const[:, earlier:earlier + P], chosen[:, h, :],
                                            start=h == 0, stop=h == i)
            last.then_inc(counted, 1)
            pe.wait_ge(hot, 1)
            for n in range(16):
                last = nc.tensor.matmul(k.bank[5][:, 0:MAX_BLOCKS], lane_hot[:, n, :], blk_hot[:, n, :],
                                        start=n == 0, stop=n == 15)
            last.then_inc(listed, 1)

        @block.scalar
        def _(act):
            act.wait_ge(top_ready, 1)
            for i in range(NT):
                last = nc.scalar.activation(r.weight[:, i, :], top[:, i, 0:TOPK], ACT.Exp, bias=nmax[:, i:i + 1],
                                            accum_out=wsum[:, i:i + 1])
            last.then_inc(exped, 1)
            act.wait_ge(bias_in, 96)
            for g in range(3):
                if g:
                    act.wait_ge(bias_rest, g)
                nc.scalar.copy(hi[:, :], full[:, :])
                act.drain().then_inc(bias_hi, 1)
                nc.scalar.copy(r.bias[32 * g:32 * g + 32, :], hi[32 * g:32 * g + 32, :])
                act.drain()
        @block.vector
        def _(dve):
            dve.wait_ge(w_in, 32)
            nc.vector.tensor_copy(wr_hi[:, :, :], wr[:, :, :])
            dve.drain()
            split_lower(nc.vector, wr[:, :, :], wr_hi[:, :, :], wr_parts.lo).then_inc(wr_split, 1)
            for i in range(NT):
                dve.wait_ge(logits_ps, i + 1)
                nc.vector.tensor_tensor(logits[:, i, :], k.bank[i][:, 0:NE], br[:, :], ALU.add)
            dve.drain()
            for i in range(NT):
                nc.vector.max(top[:, i, :], logits[:, i, :])
            dve.drain()
            for i in range(NT):
                nc.vector.max_index(idx[:, i, :], top[:, i, :], logits[:, i, :])
            nc.vector.tensor_scalar(nmax[:, :], top[:, :, 0], -1.0, None, ALU.mult).then_inc(top_ready, 1)
            dve.drain()
            nc.vector.tensor_copy(idxf[:, :, :], idx[:, :, :])
            dve.drain()
            for i in range(NT):
                for c in range(TOPK):
                    nc.vector.tensor_scalar(pick[:, i, c, :], k.const[:, C_IOTA:C_IOTA + NE], idxf[:, i, c:c + 1],
                                            None, ALU.is_equal)
            dve.drain()
            nc.vector.tensor_reduce(chosen[:, :, :], pick[:, :, :, :].rearrange("p i c e -> p i e c"), AX.X, ALU.add)\
                .then_inc(chosen_ready, 1)
            nc.vector.memset(zero[:, :], 0.0)
            dve.wait_ge(exped, 1)
            nc.vector.reciprocal(wsum[:, :], wsum[:, :])
            dve.drain()
            nc.vector.tensor_tensor(r.weight[:, :, :], r.weight[:, :, :],
                                    wsum[:, :].unsqueeze(2).to_broadcast([P, NT, TOPK]), ALU.mult)
            dve.wait_ge(counted, 1)
            nc.vector.tensor_copy(counts[:, :], k.bank[4][:, 0:NE])
            dve.drain()
            nc.vector.tensor_scalar(nb[:, :], counts[:, :], 0.0, None, ALU.is_gt)
            dve.drain()
            for n in range(1, S // BLOCK):
                nc.vector.scalar_tensor_tensor(out=nb[:, :], in0=counts[:, :], scalar=float(n * BLOCK), in1=nb[:, :],
                                               op0=ALU.is_gt, op1=ALU.add)
                dve.drain()
            nc.vector.tensor_tensor_scan(ends[:, :], nb[:, :], zero[:, :], 0.0, ALU.add, ALU.add)
            dve.drain()
            nc.vector.tensor_tensor(starts[:, :], ends[:, :], nb[:, :], ALU.subtract)
            nc.vector.tensor_tensor(before[:, :, :],
                                    k.const[:, C_IOTA:C_IOTA + MAX_BLOCKS].unsqueeze(2).to_broadcast([P, MAX_BLOCKS, NE]),
                                    ends[:, :].unsqueeze(1).to_broadcast([P, MAX_BLOCKS, NE]), ALU.is_ge)
            dve.drain()
            nc.vector.tensor_reduce(r.expert[:, :], before[:, :, :], AX.X, ALU.add)
            nc.vector.tensor_scalar(starts[:, :], starts[:, :], float(BLOCK), None, ALU.mult)
            dve.drain()
            nc.vector.tensor_copy(r.expert_i[:, 0:MAX_BLOCKS], r.expert[:, :])
            nc.vector.tensor_copy(r.expert_i[:, MAX_BLOCKS:MAX_BLOCKS + 1], ends[:, NE - 1:NE])
            dve.drain().then_inc(expert_ready, 1)
            for i in range(NT):
                nc.vector.tensor_tensor(dest[:, i, :], k.bank[i][:, 0:NE], starts[:, :], ALU.add)
            dve.drain()
            nc.vector.tensor_tensor(picked[:, :, :, :], pick[:, :, :, :],
                                    dest[:, :, :].unsqueeze(2).to_broadcast([P, NT, TOPK, NE]), ALU.mult)
            dve.drain()
            nc.vector.tensor_reduce(destk[:, :], picked[:, :, :, :].rearrange("p i c e -> p (i c) e"), AX.X, ALU.add)
            dve.drain()
            nc.vector.tensor_copy(desti[:, :], destk[:, :])
            dve.drain()
            nc.vector.tensor_scalar(lane_i[:, :], desti[:, :], BLOCK - 1, None, ALU.bitwise_and)
            nc.vector.tensor_scalar(blk_i[:, :], desti[:, :], 7, None, ALU.arith_shift_right)
            dve.drain()
            nc.vector.tensor_copy(lane_f[:, :], lane_i[:, :])
            nc.vector.tensor_copy(blk_f[:, :], blk_i[:, :])
            dve.drain()
            dve.wait_ge(slot_ready, 1)
            for n in range(16):
                nc.vector.tensor_scalar(lane_hot[:, n, :], k.const[:, C_IOTA:C_IOTA + P], lane_f[:, n:n + 1], None,
                                        ALU.is_equal)
                nc.vector.tensor_scalar(blk_hot[:, n, :], k.const[:, C_IOTA:C_IOTA + MAX_BLOCKS], blk_f[:, n:n + 1],
                                        slot_no[:, n:n + 1], ALU.is_equal, ALU.mult)
            dve.drain().then_inc(hot, 1)
            dve.wait_ge(listed, 1)
            nc.vector.tensor_scalar(slots[:, :], k.bank[5][:, 0:MAX_BLOCKS], 1.0, None, ALU.subtract)
            dve.drain()
            nc.vector.tensor_scalar(isnone[:, :], slots[:, :], 0.0, k.const[:, C_P + 2:C_P + 3], ALU.is_lt, ALU.mult)
            nc.vector.tensor_scalar(token[:, :], slots[:, :], 0.0, None, ALU.max)
            dve.drain()
            nc.vector.tensor_tensor(row[:, :], slots[:, :], isnone[:, :], ALU.add)
            nc.vector.tensor_copy(token_i[:, :], token[:, :])
            dve.drain()
            nc.vector.tensor_copy(r.row[:, :], row[:, :])
            nc.vector.tensor_scalar(r.token[:, 0:MAX_BLOCKS].bitcast(I32), token_i[:, :], 2, None, ALU.arith_shift_right)
            nc.vector.memset(r.token[:, MAX_BLOCKS:MAX_BLOCKS + 2], 0)

    k.split.counted(lo_ready=1)


def experts_stage(nc, k, A, r):
    with Stage(nc, "moe") as st:
        ring, lower, piece_in = r.ring, r.lower, r.piece_in
        upper = [st.sb(f"upper{s}", [P, 4, 512], F32R) for s in range(SPLIT)]
        rows_in = [k.ahead[:, 2 * p:2 * p + 2, :].rearrange("p a b -> p (a b)") for p in range(2)]
        tok, dst = st.sb("tok", [P, 2], U32), st.sb("dst", [P, 1], U32)
        x_hi, x_lo, a_hi, a_lo = (k.x_parts.hi[:, 2 * n:2 * n + 2, :].rearrange("p a (b t) -> p (a b) t", t=P)
                                  for n in range(4))
        sel = [st.sb(f"sel{p}", [96, P], BF16) for p in range(2)]
        g2, u2, sg2, a2 = ([st.sb(f"{n}{half}", [P, 512]) for half in range(2)] for n in ("g", "u", "sg", "a"))
        y = st.sb("y", [P, D])
        rows_sem = [st.sem(f"rows{p}_in") for p in range(2)]
        used, hi_ready, lo_ready = st.sem("used"), st.sem("hi_ready"), st.sem("lo_ready")
        x_ps, x_hi_ready, x_lo_ready, sel_ready = (st.sem(n) for n in ("x_ps", "x_hi_ready", "x_lo_ready", "sel_ready"))
        g_ready, sg_ready, a_ready = (st.sem(n) for n in ("g_ready", "sg_ready", "a_ready"))
        a_ps, a_hi_ready, a_lo_ready = (st.sem(n) for n in ("a_ps", "a_hi_ready", "a_lo_ready"))
        y_sb, y_free, stored = st.sem("y_sb"), st.sem("y_free"), st.sem("stored")
        block = st.block()

        def use(j, h):
            return LOADED + HALVES * j + h + 1

        def each_block(eng, body, before=None):
            count = eng.value_load(r.expert_i[0:1, MAX_BLOCKS:MAX_BLOCKS + 1], min_val=0, max_val=MAX_BLOCKS)
            if before:
                before()
            with eng.Fori(0, MAX_BLOCKS // 2) as q:
                for p in range(2):
                    with eng.If(q * 2 + p < count):
                        body(q, p, q * 2 + p)

        @block.sync
        def _(sp):
            def body(q, p, j):
                e = sp.value_load(r.expert_i[0:1, ds(j, 1)], min_val=0, max_val=NE - 1)

                def load(pieces):
                    for h in pieces:
                        s = (HALVES * p + h) % LOADED
                        sp.wait_ge(used, use(j, h - LOADED))
                        sp.dma_start(ring[s][:, :, :], weight_piece(A, e, h)).then_inc(piece_in[s], 16)

                if p == 0:
                    with sp.If(q > 0):
                        load(range(LOADED))
                    load(range(LOADED, HALVES))
                else:
                    load(range(HALVES))

            each_block(sp, body)

        @block.gpsimd
        def _(pool):
            def gather(p, j):
                nc.gpsimd.tensor_copy(tok[:, p:p + 1], r.token[:, ds(j, 1)])
                pool.drain()
                nc.gpsimd.indirect_dma_start(
                    out=rows_in[p][:, :], out_offset=None, in_=k.h1[:, :],
                    in_offset=bass.IndirectOffsetOnAxis(ap=tok[:, p:p + 1], axis=0)).then_inc(rows_sem[p], 16)

            def body(q, p, j):
                pool.wait_ge(x_ps, j * 2 + 2)
                gather(p, j + 2)
                pool.wait_ge(y_sb, j * 2 + 4)
                nc.gpsimd.tensor_copy(dst[:, :], r.row[:, ds(j, 1)])
                pool.drain()
                nc.gpsimd.indirect_dma_start(
                    out=k.y_slots[:, :], out_offset=bass.IndirectOffsetOnAxis(ap=dst[:, 0:1], axis=0),
                    in_=y[:, :], in_offset=None).then_inc(stored, 16)
                pool.wait_ge(stored, j * 16 + 16)
                pool.sem_inc(y_free, 1)

            def start():
                gather(0, 0)
                gather(1, 1)

            each_block(pool, body, start)
            pool.drain()

        @block.tensor
        def _(pe):
            def transpose_rows(q, p, j):
                pe.wait_ge(rows_sem[p], q * 16 + 16)
                for half in range(2):
                    for c in range(4):
                        t = half * 4 + c
                        last = nc.tensor.transpose(k.bank[6 + half][:, c * P:(c + 1) * P],
                                                   rows_in[p][:, t * P:(t + 1) * P], k.ident)
                    last.then_inc(x_ps, 1)

            def start():
                pe.drain().then_inc(used, LOADED)
                transpose_rows(0, 0, 0)

            def products(j, h, bank, first, last, hi, lo, bias_cols, p):
                s, u = (HALVES * p + h) % LOADED, h % SPLIT
                if first:
                    nc.tensor.matmul(bank, sel[p][:, :], r.bias[:, bias_cols:bias_cols + 512], start=True, stop=False)
                pe.wait_ge(lo_ready, HALVES * j + h + 1)
                for t in range(4):
                    w_lo = lower[s][:, t, :]
                    nc.tensor.matmul(bank, hi[:, t, :], upper[u][:, t, :], start=False, stop=False)
                    nc.tensor.matmul(bank, hi[:, t, :], w_lo, start=False, stop=False)
                    done = nc.tensor.matmul(bank, lo[:, t, :], upper[u][:, t, :], start=False, stop=last and t == 3)
                done.then_inc(used, 1)

            def transpose_half(j, half):
                pe.wait_ge(a_ready, j * 2 + half + 1)
                for c in range(4):
                    last = nc.tensor.transpose(k.bank[6 + half][:, c * P:(c + 1) * P],
                                               a2[half][:, c * P:(c + 1) * P], k.ident)
                last.then_inc(a_ps, 1)

            def body(q, p, j):
                pe.wait_ge(sel_ready, j + 1)
                for h in range(8):
                    col, kh = PIECES[h]
                    if h < 2:
                        pe.wait_ge(x_lo_ready, j * 2 + kh + 1)
                    products(j, h, k.bank[h // 2][:, :], kh == 0, kh == 1, x_hi[:, 4 * kh:4 * kh + 4, :],
                             x_lo[:, 4 * kh:4 * kh + 4, :], col, p)
                    if h == 5:
                        transpose_half(j, 0)
                pe.wait_ge(y_sb, j * 2 + 2)
                for h in range(8, HALVES):
                    col, kh = PIECES[h]
                    if h % 2 == 0:
                        pe.wait_ge(a_lo_ready, j * 2 + kh + 1)
                    products(j, h, k.bank[4 + h % 2][:, :], kh == 0, kh == 1, a_hi[:, 4 * kh:4 * kh + 4, :],
                             a_lo[:, 4 * kh:4 * kh + 4, :], 2 * FF + col, p)
                    if h == 8:
                        transpose_half(j, 1)
                    if h == 10:
                        transpose_rows(q + p, 1 - p, j + 1)

            each_block(pe, body, start)

        @block.scalar
        def _(act):
            def tokens_hi(j):
                for half in range(2):
                    act.wait_ge(x_ps, j * 2 + half + 1)
                    nc.scalar.copy(x_hi[:, 4 * half:4 * half + 4, :], k.bank[6 + half][:, :]).then_inc(x_hi_ready, 1)

            def output(j):
                act.wait_ge(used, use(j, HALVES - 1))
                act.wait_ge(y_free, j + 1)
                for c in range(2):
                    nc.scalar.copy(y[:, 512 * c:512 * c + 512], k.bank[4 + c][:, :]).then_inc(y_sb, 1)

            def activations_hi(j, half):
                act.wait_ge(a_ps, j * 2 + half + 1)
                nc.scalar.copy(a_hi[:, 4 * half:4 * half + 4, :], k.bank[6 + half][:, :]).then_inc(a_hi_ready, 1)

            def body(q, p, j):
                for h in range(HALVES):
                    if h == 10:
                        activations_hi(j, 0)
                    s, round_ = (HALVES * p + h) % LOADED, (HALVES * p + h) // LOADED
                    act.wait_ge(piece_in[s], 16 * (2 * HALVES // LOADED * q + round_ + 1))
                    act.wait_ge(used, use(j, h - SPLIT))
                    nc.scalar.copy(upper[h % SPLIT][:, :, :], ring[s][:, :, :]).then_inc(hi_ready, 1)
                    if h == 1:
                        tokens_hi(j)
                    if h == 3 and p == 0:
                        with act.If(q > 0):
                            output(j - 1)
                    elif h == 3:
                        output(j - 1)
                    if h in (5, 9):
                        half = (5, 9).index(h)
                        act.wait_ge(g_ready, j * 2 + half + 1)
                        nc.scalar.activation(sg2[half][:, :], g2[half][:, :], ACT.Sigmoid, scale=SWI)\
                            .then_inc(sg_ready, 1)
                activations_hi(j, 1)

            each_block(act, body)
            count = act.value_load(r.expert_i[0:1, MAX_BLOCKS:MAX_BLOCKS + 1], min_val=1, max_val=MAX_BLOCKS)
            output(count - 1)

        @block.vector
        def _(dve):
            def tokens_lo(j):
                for half in range(2):
                    part = slice(4 * half, 4 * half + 4)
                    dve.wait_ge(x_hi_ready, j * 2 + half + 1)
                    nc.vector.tensor_tensor(x_lo[:, part, :].rearrange("p t n -> p (t n)"), k.bank[6 + half][:, :],
                                            x_hi[:, part, :].bitcast(F32).rearrange("p t n -> p (t n)"),
                                            ALU.subtract).then_inc(x_lo_ready, 1)

            def start():
                dve.drain().then_inc(y_sb, 2)
                dve.drain().then_inc(y_free, 1)

            def gates(j, half):
                dve.wait_ge(used, use(j, 4 * half + 1))
                nc.vector.tensor_scalar(g2[half][:, :], k.bank[2 * half][:, :], LIMIT, None, ALU.min)\
                    .then_inc(g_ready, 1)

            def activations(j, half):
                dve.wait_ge(used, use(j, 4 * half + 3))
                nc.vector.tensor_scalar(u2[half][:, :], k.bank[2 * half + 1][:, :], LIMIT, -LIMIT, ALU.min, ALU.max)
                dve.drain()
                nc.vector.scalar_tensor_tensor(out=u2[half][:, :], in0=u2[half][:, :], scalar=1.0,
                                               in1=g2[half][:, :], op0=ALU.add, op1=ALU.mult)
                dve.drain()
                dve.wait_ge(sg_ready, j * 2 + half + 1)
                nc.vector.tensor_tensor(a2[half][:, :], u2[half][:, :], sg2[half][:, :], ALU.mult)\
                    .then_inc(a_ready, 1)

            def activations_lo(j, half):
                part = slice(4 * half, 4 * half + 4)
                dve.wait_ge(a_hi_ready, j * 2 + half + 1)
                nc.vector.tensor_tensor(a_lo[:, part, :].rearrange("p t n -> p (t n)"), k.bank[6 + half][:, :],
                                        a_hi[:, part, :].bitcast(F32).rearrange("p t n -> p (t n)"),
                                        ALU.subtract).then_inc(a_lo_ready, 1)

            def body(q, p, j):
                nc.vector.tensor_scalar(sel[p][:, :], k.const[0:96, C_P + 1:C_P + 2].to_broadcast([96, P]),
                                        r.expert[0:96, ds(j, 1)], None, ALU.is_equal).then_inc(sel_ready, 1)
                for h in range(HALVES):
                    if h in (5, 9):
                        gates(j, (5, 9).index(h))
                    if h in (7, 11):
                        activations(j, (7, 11).index(h))
                    if h == 10:
                        activations_lo(j, 0)
                    s = (HALVES * p + h) % LOADED
                    dve.wait_ge(hi_ready, HALVES * j + h + 1)
                    nc.vector.tensor_tensor(lower[s][:, :, :], ring[s][:, :, :],
                                            upper[h % SPLIT][:, :, :].bitcast(F32), ALU.subtract).then_inc(lo_ready, 1)
                    if h == 1:
                        tokens_lo(j)
                activations_lo(j, 1)

            each_block(dve, body, start)


def combine_stage(nc, k, r, x):
    with Stage(nc, "combine") as st:
        ys = [st.sb(f"ys{i}", [P, TOPK, D]) for i in range(NT - 1)]
        first_added = st.sem("first_added")
        y_in = [st.sem(f"y{i}_in") for i in range(NT)]
        rows = k.y_slots[0:SLOTS, :].rearrange("(i p c) n -> i p c n", p=P, c=TOPK)
        block = st.block()

        @block.sync
        def _(sp):
            for i in range(NT):
                if i == NT - 1:
                    sp.wait_ge(first_added, 1)
                for c in (0, 2):
                    sp.dma_start(ys[i % (NT - 1)][:, c:c + 2, :], rows[i][:, c:c + 2, :]).then_inc(y_in[i], 16)

        @block.vector
        def _(dve):
            for i in range(NT):
                nc.vector.tensor_scalar(x[:, i, :], x[:, i, :], ALPHA, None, ALU.mult)
            for i in range(NT):
                dve.wait_ge(y_in[i], 32)
                for c in range(TOPK):
                    dve.drain()
                    last = nc.vector.scalar_tensor_tensor(out=x[:, i, :], in0=ys[i % (NT - 1)][:, c, :],
                                                          scalar=r.weight[:, i, c:c + 1], in1=x[:, i, :],
                                                          op0=ALU.mult, op1=ALU.add)
                if i == 0:
                    last.then_inc(first_added, 1)
                dve.drain()
                statistics(nc, k, i)


def nsa_keys_stage(nc, k, A, n, scratch):
    w2 = A["w_in_2"][0]
    NW = P + (Z2 - VW2)
    h0, l0, p0, w0, c0 = (k.split.done[x] for x in ("hi_ready", "lo_ready", "projected", "w_in", "copied"))
    with Stage(nc, "nsakv") as st:
        (wkw, wkw_lower), (wnat, wnat_lower) = st.overlaid("wkw", [P, NK, P]), st.overlaid("wnat", [P, NK, NW])
        up = [st.sb(f"up{c}", [P, NK, P], F32R) for c in range(4)]
        up_nat = st.sb("up_nat", [P, NK, NW], F32R)
        raws = [k.ahead[:, :, P * c:P * c + P] for c in range(3)] + [wkw[:, :, :]]
        lowers = [k.ahead_lower[:, :, P * c:P * c + P] for c in range(3)] + [wkw_lower[:, :, :]]
        w = [Split(up[c][:, :, :], lowers[c]) for c in range(4)]
        w_nat = Split(up_nat[:, :, :], wnat_lower[:, :, :])
        w1 = [x.rearrange("p k (l h) -> p (k l) h", h=P) for x in (scratch, k.ahead[:, :, :])]
        wc2 = [st.sb(f"wc2{c}", [P, HD]) for c in range(2)]
        pos = st.sb("pos", [P, 32])
        src = [st.sb(f"src{c}", [P, S]) for c in range(2)]
        blk = [st.sb(f"blk{c}", [P, 32, N_CMP]) for c in range(2)]
        NH = 4 * N_CMP
        hid, t, th, act_h = (st.sb(x, [P, NH]) for x in ("hid", "t", "th", "act_h"))
        w_in, pos_in, table_in = k.split["w_in"], st.sem("pos_in"), st.sem("table_in")
        c1_in = [st.sem("ck1_in"), st.sem("cv1_in")]
        hi_ready, lo_ready = k.split["hi_ready"], k.split["lo_ready"]
        projected, evacuated, blocks = k.split["projected"], k.split["copied"], st.sem("blocks")
        hid_ps, arg_ready, tanh_ready, hid_ready = (st.sem(x) for x in ("hid_ps", "arg_ready", "tanh_ready", "hid_ready"))
        cmp_ps, nat_ps = st.sem("cmp_ps"), st.sem("nat_ps")
        block = st.block()

        @block.sync
        def _(sp):
            sp.dma_start(wkw[:, :, :], column_tiles(w2, KW2)).then_inc(w_in, 16)
            sp.dma_start(wnat[:, :, 0:P], column_tiles(w2, VS2)).then_inc(w_in, 16)
            sp.dma_start(wnat[:, :, P:NW], column_tiles(w2, VW2, Z2 - VW2)).then_inc(w_in, 16)
            sp.wait_ge(k.t5_stored, 16)
            skewed = bass.AP(k.z_t5_handle, P - 1, [[1023, P], [P * 1024, 6], [1, BW]])
            sp.dma_start(n.table[:, :, :], skewed).then_inc(table_in, 16)
            sp.wait_ge(projected, p0 + 3)
            for g in range(2):
                sp.dma_start(w1[1][HD * g:HD * g + HD, :, :],
                             A["w_cv1_2"][0].rearrange("(l d) h -> d l h", d=HD)).then_inc(c1_in[1], 16)
            sp.wait_ge(table_in, 16)

        @block.scalar
        def _(act):
            with nc.allow_non_contiguous_dma(reason="positions by feature"):
                for g in range(2):
                    act.dma_start(pos[HD * g:HD * g + HD, :], A["cmp_pos_2"][0].rearrange("l d -> d l"))\
                        .then_inc(pos_in, 16)
            for g in range(2):
                act.dma_start(w1[0][HD * g:HD * g + HD, :, :],
                              A["w_ck1_2"][0].rearrange("(l d) h -> d l h", d=HD)).then_inc(c1_in[0], 16)
            for c, name in enumerate(("w_ck2_2", "w_cv2_2")):
                act.dma_start(wc2[c][:, :], A[name][0]).then_inc(c1_in[0], 16)
            act.wait_ge(k.ahead_in, k.ahead_loads)
            for c in range(4):
                if c == 3:
                    act.wait_ge(w_in, w0 + 48)
                nc.scalar.copy(up[c][:, :, :], raws[c]).then_inc(hi_ready, 1)
            nc.scalar.copy(up_nat[:, :, :], wnat[:, :, :]).then_inc(hi_ready, 1)
            for c, dst in enumerate((src[0], src[1], n.ks_t, n.kw_t)):
                act.wait_ge(projected, p0 + c + 1)
                nc.scalar.copy(dst[:, :], k.bank[c][:, :]).then_inc(evacuated, 1)
            for i in range(NT):
                act.wait_ge(nat_ps, i + 1)
                nc.scalar.copy(n.vs[:, i, :], k.bank[4 + i][:, 0:P])
                nc.scalar.copy(n.vw[:, i, :], k.bank[4 + i][:, P:2 * P])
            for i in range(NT):
                nc.scalar.activation(n.gates[:, i, :], k.bank[4 + i][:, 2 * P:NW], ACT.Sigmoid)
            act.wait_ge(arg_ready, 1)
            nc.scalar.activation(th[:, :], t[:, :], ACT.Tanh, scale=0.7978845608028654).then_inc(tanh_ready, 1)

        @block.tensor
        def _(pe):
            for c in range(4):
                pe.wait_ge(lo_ready, l0 + c + 1)
                for f in range(NK):
                    last = split_product(nc, k.bank[c][:, :], w[c][:, f, :], k.x_parts[:, f, :], f == 0, f == NK - 1)
                last.then_inc(projected, 1)
            pe.wait_ge(lo_ready, l0 + 5)
            for i in range(NT):
                for f in range(NK):
                    last = split_product(nc, k.bank[4 + i][:, 0:NW], k.x_parts[:, f, i * P:(i + 1) * P],
                                         w_nat[:, f, :], f == 0, f == NK - 1)
                last.then_inc(nat_ps, 1)
            pe.wait_ge(evacuated, c0 + 4)
            for c in range(2):
                pe.wait_ge(c1_in[c], (64, 32)[c])
                pe.wait_ge(blocks, c + 1)
                for g, bank in enumerate((2, 3)):
                    rows, cols = slice(HD * g, HD * g + HD), slice(c * N_CMP, (c + 1) * N_CMP)
                    for l in range(32):
                        last = nc.tensor.matmul(k.bank[bank][:, cols], w1[c][rows, l, :], blk[c][rows, l, :],
                                                start=l == 0, stop=l == 31)
            last.then_inc(hid_ps, 1)
            pe.wait_ge(hid_ready, 1)
            for g in range(2):
                nc.tensor.matmul(k.bank[0][HD * g:HD * g + HD, 0:N_CMP], wc2[0][:, :],
                                 act_h[:, g * N_CMP:(g + 1) * N_CMP], start=True, stop=True)
                last = nc.tensor.matmul(k.bank[1][0:N_CMP, HD * g:HD * g + HD],
                                        act_h[:, (2 + g) * N_CMP:(3 + g) * N_CMP], wc2[1][:, :],
                                        start=True, stop=True)
            last.then_inc(cmp_ps, 1)

        @block.vector
        def _(dve):
            for c in range(4):
                dve.wait_ge(hi_ready, h0 + c + 1)
                split_lower(nc.vector, raws[c], up[c][:, :, :], w[c].lo).then_inc(lo_ready, 1)
            dve.wait_ge(hi_ready, h0 + 5)
            split_lower(nc.vector, wnat[:, :, :], up_nat[:, :, :], w_nat.lo).then_inc(lo_ready, 1)
            dve.wait_ge(pos_in, 32)
            for c in range(2):
                dve.wait_ge(evacuated, c0 + c + 1)
                by_block = src[c][:, :].rearrange("p (n b) -> p b n", b=16)
                for a in range(2):
                    last = nc.vector.tensor_tensor(
                        blk[c][:, 16 * a:16 * a + 16, :], by_block[:, :, a:a + N_CMP],
                        pos[:, 16 * a:16 * a + 16].unsqueeze(2).to_broadcast([P, 16, N_CMP]), ALU.add)
                last.then_inc(blocks, 1)
            dve.wait_ge(hid_ps, 1)
            for g, bank in enumerate((2, 3)):
                nc.vector.tensor_copy(hid[:, :].rearrange("p (c g n) -> p c g n", c=2, g=2)[:, :, g, :],
                                      k.bank[bank][:, 0:2 * N_CMP].rearrange("p (c n) -> p c n", c=2))
            dve.drain()
            nc.vector.tensor_tensor(t[:, :], hid[:, :], hid[:, :], ALU.mult)
            dve.drain()
            nc.vector.tensor_scalar(t[:, :], t[:, :], 0.044715, 1.0, ALU.mult, ALU.add)
            dve.drain()
            nc.vector.tensor_tensor(t[:, :], t[:, :], hid[:, :], ALU.mult).then_inc(arg_ready, 1)
            dve.wait_ge(tanh_ready, 1)
            nc.vector.tensor_scalar(th[:, :], th[:, :], 1.0, 0.5, ALU.add, ALU.mult)
            dve.drain()
            nc.vector.tensor_tensor(act_h[:, :], th[:, :], hid[:, :], ALU.mult).then_inc(hid_ready, 1)
            dve.wait_ge(cmp_ps, 1)
            nc.vector.tensor_copy(n.kc_t[:, :], k.bank[0][:, 0:N_CMP])
            nc.vector.tensor_copy(n.vc[:, :], k.bank[1][0:N_CMP, 0:P])

    k.split.counted(hi_ready=5, lo_ready=5, projected=4, w_in=48, copied=4)


def nsa_attention_stage(nc, k, A, n, out):
    w2 = A["w_in_2"][0]
    with Stage(nc, "nsa_heads") as st:
        q = [st.sb(f"q{g}", [P, S]) for g in range(2)]
        tiles = []
        for i in range(NT):
            for g in range(2):
                for br in range(3):
                    keys = N_CMP if br == 0 else (i + 1) * P
                    kt = (n.kc_t, n.ks_t, n.kw_t)[br]
                    if br == 0:
                        first = BW - 481 - P * i
                        cols = slice(first, first + 16 * (N_CMP - 1) + 1, 16)
                    else:
                        cols = slice((NT - 1 - i) * P, S)
                    if br == 0:
                        def value(u, j, g=g):
                            return n.vc[0:N_CMP, HD * g:HD * g + HD]
                    else:
                        def value(u, j, g=g, v=(None, n.vs, n.vw)[br]):
                            return v[:, j, HD * g:HD * g + HD]
                    tiles.append(dict(
                        i=i, keys=keys, q=q[g][:, i * P:(i + 1) * P], kt=kt[:, 0:keys],
                        bias=lambda u, g=g, cols=cols: n.table[:, ds(u + 3 * g, 1), cols]
                            .rearrange("p o n -> p (o n)"),
                        v=value, out=(HD * g, HD), first=br == 0, last=br == 2, masked=br == 0 and i == 0,
                        scale=lambda u, i=i, c=9 * g + br: n.gates[:, i, ds(u * 3 + c, 1)]))
        out4 = out.rearrange("p i (g d) -> p i g d", g=2)

        def load(sp, u, raw):
            return [sp.dma_start(raw[:, 0, :, HD * g:HD * g + HD], column_tiles(w2, Q2 + 192 * g + u * HD, HD))
                    for g in range(2)]

        def copy_out(u, i):
            return nc.vector.tensor_copy(out4[:, i, :, ds(u * HD, HD)],
                                         k.bank[5 + i % 2][:, 0:P].rearrange("p (g d) -> p g d", g=2))

        k.loads_per_unit = 2
        heads_stage(nc, "nsa", k, NSA_J, load, 1, Items(tiles), None, dict(q=q), copy_out)


def negative_abs(nc, out, x, floor):
    return nc.vector.scalar_tensor_tensor(out=out, in0=floor, scalar=2.0, in1=x, op0=ALU.mult, op1=ALU.subtract)


def stick_breaking_stage(nc, k, A, out_t):
    w2, ahead_loads = A["w_in_2"][0], k.ahead_loads
    HEADS, WIDTHS = 4, [S - P * j for j in range(NT)]
    AT = [sum(WIDTHS[:j]) for j in range(NT)]
    W = sum(WIDTHS)
    h0, l0, p0, w0, c0 = (k.split.done[x] for x in ("hi_ready", "lo_ready", "projected", "w_in", "copied"))
    with Stage(nc, "sb") as st:
        up_qk, (raw_v, v_lower) = st.sb("up_qk", [P, NK, 512], F32R), st.overlaid("raw_v", [P, NK, 256])
        up_v = st.sb("up_v", [P, NK, 256], F32R)
        w_qk, w_v = Split(up_qk[:, :, :], k.ahead_lower[:, :, :]), Split(up_v[:, :, :], v_lower[:, :, :])
        q, kt = st.sb("q", [P, HEADS, S]), st.sb("kt", [P, 2, S])
        v = st.sb("v", [P, NT, 256])
        ex, ls, rest = ([st.sb(f"{x}{p}", [P, W]) for p in range(2)] for x in ("ex", "ls", "rest"))
        w_in, hi_ready, lo_ready = k.split["w_in"], k.split["hi_ready"], k.split["lo_ready"]
        projected, q_sb, v_sb = k.split["projected"], k.split["copied"], st.sem("v_sb")
        z_ps, z_read, log_ready, rest_ready = (st.sem(x) for x in ("z_ps", "z_read", "log_ready", "rest_ready"))
        between, sum_ready, a_exp, a_ready, o_ps, o_sb = (st.sem(x) for x in (
            "between", "sum_ready", "a_exp", "a_ready", "o_ps", "o_sb"))
        zeroed = st.sem("zeroed")
        below = k.const[:, C_LT:C_LT + P]
        block = st.block()

        @block.sync
        def _(sp):
            sp.dma_start(raw_v[:, :, :], column_tiles(w2, SBV, 256)).then_inc(w_in, 16)
            sp.wait_ge(projected, p0 + 4)
            load_ahead(sp, k, column_tiles(w2, HGF, HG_W))

        @block.tensor
        def _(pe):
            for n in range(4):
                if n % 2 == 0:
                    pe.wait_ge(lo_ready, l0 + n // 2 + 1)
                for c in range(NK):
                    last = split_product(nc, k.bank[n][:, :], w_qk[:, c, n * P:(n + 1) * P], k.x_parts[:, c, :],
                                         c == 0, c == NK - 1)
                last.then_inc(projected, 1)
            pe.wait_ge(lo_ready, l0 + 3)
            for i in range(NT):
                for c in range(NK):
                    last = split_product(nc, k.bank[4 + i][:, 0:256], k.x_parts[:, c, i * P:(i + 1) * P],
                                         w_v[:, c, :], c == 0, c == NK - 1)
            last.then_inc(projected, 1)

            def scores(s):
                if s:
                    pe.wait_ge(z_read, s)
                for j in range(NT):
                    last = nc.tensor.matmul(k.bank[j][:, 0:WIDTHS[j]], kt[:, s // 2, j * P:(j + 1) * P],
                                            q[:, s, j * P:S], start=True, stop=True)
                last.then_inc(z_ps, 1)

            pe.wait_ge(zeroed, 1)
            pe.wait_ge(q_sb, c0 + 4)
            scores(0)
            pe.wait_ge(v_sb, 1)
            for s in range(HEADS):
                if s + 1 < HEADS:
                    scores(s + 1)
                pe.wait_ge(rest_ready, s + 1)
                if s:
                    pe.wait_ge(o_sb, s)
                for j in range(NT):
                    for h in range(j, NT):
                        later = C_GT if h == j else C_ONE
                        last = nc.tensor.matmul(k.bank[4 + j][:, (h - j) * P:WIDTHS[j]],
                                                k.const[:, later:later + P], rest[s % 2][:, AT[h]:AT[h] + WIDTHS[h]],
                                                start=h == j, stop=h == NT - 1)
                    last.then_inc(between, 1)
                pe.wait_ge(a_ready, s + 1)
                rows, cols = slice(HD * (s % 2), HD * (s % 2) + HD), slice(HD * s, HD * s + HD)
                for j in range(NT):
                    last = nc.tensor.matmul(k.bank[4][rows, j * P:S], v[:, j, cols],
                                            rest[s % 2][:, AT[j]:AT[j] + WIDTHS[j]], start=j == 0, stop=j == NT - 1)
                last.then_inc(o_ps, 1)

        @block.scalar
        def _(act):
            act.wait_ge(k.ahead_in, ahead_loads)
            for n in range(2):
                nc.scalar.copy(up_qk[:, :, 256 * n:256 * n + 256], k.ahead[:, :, 256 * n:256 * n + 256])\
                    .then_inc(hi_ready, 1)
            act.wait_ge(w_in, w0 + 16)
            nc.scalar.copy(up_v[:, :, :], raw_v[:, :, :]).then_inc(hi_ready, 1)
            for n in range(2):
                act.wait_ge(projected, p0 + n + 1)
                for m in range(2):
                    rows = slice(HD * m, HD * m + HD)
                    last = nc.scalar.activation(q[rows, 2 * n + m, :], k.bank[n][rows, :], ACT.Copy, scale=HD ** -0.5)
                last.then_inc(q_sb, 1)
            for n in range(2):
                act.wait_ge(projected, p0 + n + 3)
                nc.scalar.copy(kt[:, n, :], k.bank[2 + n][:, :]).then_inc(q_sb, 1)
            act.wait_ge(projected, p0 + 5)
            for i in range(NT):
                last = nc.scalar.copy(v[:, i, :], k.bank[4 + i][:, 0:256])
            last.then_inc(v_sb, 1)

            def logs(s):
                act.wait_ge(z_read, s + 1)
                nc.scalar.activation(ex[s % 2][:, :], ex[s % 2][:, :], ACT.Exp)
                act.drain()
                nc.scalar.activation(ex[s % 2][:, :], ex[s % 2][:, :], ACT.Ln, bias=1.0).then_inc(log_ready, 1)

            logs(0)
            for s in range(HEADS):
                if s + 1 < HEADS:
                    logs(s + 1)
                act.wait_ge(sum_ready, s + 1)
                nc.scalar.activation(rest[s % 2][:, :], rest[s % 2][:, :], ACT.Exp).then_inc(a_exp, 1)

        @block.vector
        def _(dve):
            for n in range(2):
                part = slice(256 * n, 256 * n + 256)
                dve.wait_ge(hi_ready, h0 + n + 1)
                split_lower(nc.vector, k.ahead[:, :, part], up_qk[:, :, part], w_qk.lo[:, :, part]).then_inc(lo_ready, 1)
            dve.wait_ge(hi_ready, h0 + 3)
            split_lower(nc.vector, raw_v[:, :, :], up_v[:, :, :], w_v.lo).then_inc(lo_ready, 1)
            for s in range(HEADS):
                m = s % 2
                nc.vector.memset(q[HD - HD * m:P - HD * m, s, :], 0.0)
            dve.drain().then_inc(zeroed, 1)

            def below_zero(s):
                dve.wait_ge(z_ps, s + 1)
                for j in range(NT):
                    nc.vector.tensor_scalar(ls[s % 2][:, AT[j]:AT[j] + WIDTHS[j]], k.bank[j][:, 0:WIDTHS[j]], 0.0,
                                            None, ALU.min)
                dve.drain()
                for j in range(NT):
                    at = slice(AT[j], AT[j] + WIDTHS[j])
                    negative_abs(nc, ex[s % 2][:, at], k.bank[j][:, 0:WIDTHS[j]], ls[s % 2][:, at])
                    nc.vector.tensor_tensor(rest[s % 2][:, at], ls[s % 2][:, at], k.bank[j][:, 0:WIDTHS[j]],
                                            ALU.subtract)
                dve.drain().then_inc(z_read, 1)

            below_zero(0)
            for s in range(HEADS):
                p = s % 2
                dve.wait_ge(log_ready, s + 1)
                nc.vector.tensor_tensor(rest[p][:, :], rest[p][:, :], ex[p][:, :], ALU.subtract)
                nc.vector.tensor_tensor(ls[p][:, :], ls[p][:, :], ex[p][:, :], ALU.subtract)
                dve.drain()
                for j in range(NT):
                    diag = rest[p][:, AT[j]:AT[j] + P]
                    nc.vector.tensor_tensor(diag, diag, below, ALU.mult)
                dve.drain().then_inc(rest_ready, 1)
                if s + 1 < HEADS:
                    below_zero(s + 1)
                for j in range(NT):
                    at = slice(AT[j], AT[j] + WIDTHS[j])
                    dve.wait_ge(between, s * 4 + NT)
                    nc.vector.tensor_tensor(rest[p][:, at], ls[p][:, at], k.bank[4 + j][:, 0:WIDTHS[j]], ALU.add)
                dve.drain().then_inc(sum_ready, 1)
                dve.wait_ge(a_exp, s + 1)
                for j in range(NT):
                    diag = rest[p][:, AT[j]:AT[j] + P]
                    nc.vector.tensor_tensor(diag, diag, below, ALU.mult)
                dve.drain().then_inc(a_ready, 1)
                dve.wait_ge(o_ps, s + 1)
                rows = slice(HD * p, HD * p + HD)
                nc.vector.tensor_copy(out_t[rows, s // 2, :], k.bank[4][rows, :])
                dve.drain().then_inc(o_sb, 1)


    k.split.counted(hi_ready=3, lo_ready=3, projected=5, w_in=16, copied=4)


def hgrn_gates_stage(nc, k, A, h):
    w2, ahead_loads = A["w_in_2"][0], k.ahead_loads
    h0, l0, p0, w0, c0 = (k.split.done[x] for x in ("hi_ready", "lo_ready", "projected", "w_in", "copied"))
    with Stage(nc, "hgates") as st:
        raw_q, q_lower = st.overlaid("raw_q", [P, NK, HG_W])
        raws = [k.ahead[:, :, 0:HG_W], raw_q[:, :, :], k.ahead[:, :, 0:HG_W]]
        lowers = [k.ahead_lower[:, :, 0:HG_W], q_lower[:, :, :], k.ahead_lower[:, :, 0:HG_W]]
        up = [st.sb(f"up{x}", [P, NK, HG_W], F32R)[:, :, :] for x in "fq"]
        up.append(up[0])
        w = [Split(u, lower) for u, lower in zip(up, lowers)]
        ls, t1, t2 = h.qe, h.kd_t, h.kd
        zeros = st.sb("zeros", [P, P])
        q_in, v_in, hi_ready, lo_ready = k.split["w_in"], k.split["late_in"], k.split["hi_ready"], k.split["lo_ready"]
        arg_ready, act_done, kd_ps = (st.sem(x) for x in ("arg_ready", "act_done", "kd_ps"))
        projected, q_sb = k.split["projected"], k.split["copied"]
        edge_exp, kd_ready = st.sem("edge_exp"), st.sem("kd_ready")
        block = st.block()

        @block.sync
        def _(sp):
            sp.dma_start(raws[1], column_tiles(w2, HGQ, HG_W)).then_inc(q_in, 16)
            sp.wait_ge(projected, p0 + HG_UNITS)
            sp.dma_start(raws[2], column_tiles(w2, HGI, HG_W)).then_inc(v_in, 16)

        @block.tensor
        def _(pe):
            for n in range(2):
                pe.wait_ge(lo_ready, l0 + n + 1)
                for u in range(HG_UNITS):
                    for c in range(NK):
                        last = split_product(nc, k.bank[3 * n + u][:, :], w[n][:, c, u * P:(u + 1) * P],
                                             k.x_parts[:, c, :], c == 0, c == NK - 1)
                    last.then_inc(projected, 1)
            pe.wait_ge(lo_ready, l0 + 3)
            for i, bank in enumerate((6, 7, 3, 4)):
                if i == 2:
                    pe.wait_ge(q_sb, c0 + HG_UNITS)
                for c in range(NK):
                    last = split_product(nc, k.bank[bank][:, 0:HG_W], k.x_parts[:, c, i * P:(i + 1) * P],
                                         w[2][:, c, :], c == 0, c == NK - 1)
                last.then_inc(projected, 1)
            pe.wait_ge(kd_ready, 1)
            for u in range(HG_UNITS):
                for c in range(NT):
                    last = nc.tensor.transpose(k.bank[u][:, c * P:(c + 1) * P], h.kd[:, u, c * P:(c + 1) * P], k.ident)
                last.then_inc(kd_ps, 1)

        @block.scalar
        def _(act):
            for n, loaded in enumerate(((k.ahead_in, ahead_loads), (q_in, w0 + 16))):
                act.wait_ge(*loaded)
                nc.scalar.copy(up[n], raws[n]).then_inc(hi_ready, 1)
            act.wait_ge(arg_ready, 1)
            nc.scalar.activation(t1[:, :, :], t1[:, :, :], ACT.Exp)
            act.drain()
            nc.scalar.activation(t1[:, :, :], t1[:, :, :], ACT.Ln, bias=1.0).then_inc(act_done, 1)
            act.wait_ge(v_in, 16)
            nc.scalar.copy(up[2], raws[2]).then_inc(hi_ready, 1)
            for u in range(HG_UNITS):
                act.wait_ge(projected, p0 + HG_UNITS + u + 1)
                nc.scalar.copy(h.q[:, u, :], k.bank[3 + u][:, :]).then_inc(q_sb, 1)
            act.wait_ge(arg_ready, 2)
            nc.scalar.activation(t2[:, :, :], t2[:, :, :], ACT.Exp)
            nc.scalar.activation(h.key[:, :, :], h.key[:, :, :], ACT.Exp)
            act.drain()
            nc.scalar.activation(t2[:, :, :], t2[:, :, :], ACT.Ln, bias=1.0).then_inc(act_done, 1)
            for i, bank in enumerate((6, 7, 3, 4)):
                act.wait_ge(projected, p0 + 2 * HG_UNITS + i + 1)
                nc.scalar.copy(h.v[:, i, :], k.bank[bank][:, 0:HG_W])
            act.wait_ge(arg_ready, 3)
            nc.scalar.activation(h.kd[:, :, :], h.kd[:, :, :], ACT.Exp)
            nc.scalar.activation(h.eb[:, :, :], h.b[:, :, :], ACT.Exp).then_inc(edge_exp, 1)
            for u in range(HG_UNITS):
                act.wait_ge(kd_ps, u + 1)
                nc.scalar.copy(h.kd_t[:, u, :], k.bank[u][:, :])

        @block.vector
        def _(dve):
            nc.vector.memset(zeros[:, :], 0.0)
            def lower(n):
                dve.wait_ge(hi_ready, h0 + n + 1)
                split_lower(nc.vector, raws[n], up[n], w[n].lo).then_inc(lo_ready, 1)

            lower(0)
            lower(1)
            for u in range(HG_UNITS):
                dve.wait_ge(projected, p0 + u + 1)
                nc.vector.tensor_scalar(ls[:, u, :], k.bank[u][:, :], 0.0, None, ALU.min)
                dve.drain()
                negative_abs(nc, t1[:, u, :], k.bank[u][:, :], ls[:, u, :])
                nc.vector.tensor_tensor(h.key[:, u, :], ls[:, u, :], k.bank[u][:, :], ALU.subtract)
            dve.drain().then_inc(arg_ready, 1)
            lower(2)
            dve.wait_ge(act_done, 1)
            nc.vector.tensor_tensor(ls[:, :, :], ls[:, :, :], t1[:, :, :], ALU.subtract)
            nc.vector.tensor_tensor(h.key[:, :, :], h.key[:, :, :], t1[:, :, :], ALU.subtract)
            dve.drain()
            nc.vector.tensor_scalar(t1[:, :, :], ls[:, :, :], LOG_FLOOR, None, ALU.subtract)
            nc.vector.tensor_scalar(t2[:, :, :], ls[:, :, :], LOG_FLOOR, 0.0, ALU.subtract, ALU.min)
            dve.drain()
            negative_abs(nc, t2[:, :, :], t1[:, :, :], t2[:, :, :])
            dve.drain().then_inc(arg_ready, 1)
            nc.vector.tensor_scalar(ls[:, :, :], ls[:, :, :], LOG_FLOOR, None, ALU.max)
            dve.drain()
            dve.wait_ge(act_done, 2)
            nc.vector.tensor_tensor(ls[:, :, :], ls[:, :, :], t2[:, :, :], ALU.add)
            dve.drain()
            for u in range(HG_UNITS):
                for c in range(NT):
                    chunk = slice(c * P, (c + 1) * P)
                    nc.vector.tensor_tensor_scan(h.b[:, u, chunk], ls[:, u, chunk], zeros[:, :], 0.0, ALU.add, ALU.add)
            dve.drain()
            kd, b = (x[:, :, :].rearrange("p u (c t) -> p (u c) t", t=P) for x in (h.kd, h.b))
            nc.vector.tensor_tensor(kd, b[:, :, P - 1:P].to_broadcast([P, HG_UNITS * NT, P]), b, ALU.subtract)
            dve.drain().then_inc(arg_ready, 1)
            dve.wait_ge(edge_exp, 1)
            nc.vector.tensor_tensor(h.kd[:, :, :], h.kd[:, :, :], h.key[:, :, :], ALU.mult).then_inc(kd_ready, 1)
            dve.wait_ge(q_sb, c0 + HG_UNITS)
            nc.vector.tensor_tensor(h.qe[:, :, :], h.eb[:, :, :], h.q[:, :, :], ALU.mult)

    k.split.counted(hi_ready=3, lo_ready=3, projected=2 * HG_UNITS + NT, w_in=16, copied=HG_UNITS)


def hgrn_stage(nc, k, h, out):
    LEVELS = 8
    with Stage(nc, "hg") as st:
        lev = [st.sb(f"lev{x}", [P, S]) for x in range(2)]
        left = [[st.sb(f"left{x}{m}", [P, S]) for m in range(2)] for x in range(2)]
        att = [st.sb(f"att{m}", [P, S]) for m in range(2)]
        states, carrier = st.sb("states", [P, NT - 1, P]), st.sb("carrier", [P, 1])
        pool_carrier = st.sb("pool_carrier", [P, 2])
        kd_t, qe, picked = st.sb("kd_t", [P, S]), st.sb("qe", [P, S]), st.sem("picked")
        diff_ready, lev_exp, lev_ready, lev_ps, lev_done = (st.sem(x) for x in (
            "diff_ready", "lev_exp", "lev_ready", "lev_ps", "lev_done"))
        grown, states_ready, o_ps, o_sb = (st.sem(x) for x in ("grown", "states_ready", "o_ps", "o_sb"))
        block = st.block()

        @block.gpsimd
        def _(pool):
            nc.gpsimd.memset(pool_carrier[:, :], 0.0)
            pool.drain()
            with pool.Fori(0, HG_UNITS) as u:
                pool.wait_ge(o_sb, u + 1)
                wait_carrier(nc.gpsimd, pool_carrier)
                nc.gpsimd.tensor_copy(kd_t[:, :].unsqueeze(1), h.kd_t[:, ds(u, 1), :])
                nc.gpsimd.tensor_copy(qe[:, :].unsqueeze(1), h.qe[:, ds(u, 1), :])
                pool.drain().then_inc(picked, 1)

        @block.tensor
        def _(pe):
            with pe.Fori(0, HG_UNITS) as u:
                pe.wait_ge(o_sb, u + 1)
                pe.wait_ge(picked, u + 1)
                for c in range(NT - 1):
                    last = nc.tensor.matmul(k.bank[4][:, c * P:(c + 1) * P],
                                            kd_t[:, c * P:(c + 1) * P],
                                            h.v[:, c, ds(u * P, P)], start=True, stop=True)
                last.then_inc(grown, 1)
                for n in range(LEVELS):
                    pe.wait_ge(lev_ready, u * LEVELS + n + 1)
                    if n >= 2:
                        pe.wait_ge(lev_done, u * LEVELS + n - 1)
                    for m in range(2):
                        for c in range(NT):
                            chunk = slice(c * P, (c + 1) * P)
                            last = nc.tensor.matmul(k.bank[2 * (n % 2) + m][:, chunk], left[n % 2][m][:, chunk],
                                                    lev[n % 2][:, chunk], start=True, stop=True)
                    last.then_inc(lev_ps, 1)
                pe.wait_ge(states_ready, u + 1)
                pe.wait_ge(lev_done, u * LEVELS + LEVELS)
                for c in range(NT):
                    chunk = slice(c * P, (c + 1) * P)
                    for m in range(2):
                        rows = slice(HD * m, HD * m + HD)
                        to = k.bank[5][:, c * P + HD * m:c * P + HD * m + HD]
                        last = nc.tensor.matmul(to, att[m][:, chunk], h.v[:, c, ds(u * P + HD * m, HD)],
                                                start=True, stop=c == 0)
                        if c:
                            last = nc.tensor.matmul(to, qe[:, chunk], states[:, c - 1, rows], start=False, stop=True)
                last.then_inc(o_ps, 1)

        @block.scalar
        def _(act):
            with act.Fori(0, HG_UNITS) as u:
                for n in range(LEVELS - 1):
                    act.wait_ge(diff_ready, u * (LEVELS - 1) + n + 1)
                    nc.scalar.activation(lev[n % 2][:, :], lev[n % 2][:, :], ACT.Exp).then_inc(lev_exp, 1)

        @block.vector
        def _(dve):
            nc.vector.memset(states[:, :, :], 0.0)
            for m in range(2):
                nc.vector.memset(att[m][:, :], 0.0)
                for x in range(2):
                    nc.vector.memset(left[x][m][:, :], 0.0)
            dve.drain().then_inc(o_sb, 1)
            with dve.Fori(0, HG_UNITS) as u:
                def unit(x):
                    return x[:, ds(u, 1), :].rearrange("p o n -> p (o n)")

                def halves(x, n):
                    v4 = x.rearrange("p (b s t) -> p b s t", s=2, t=1 << n)
                    return v4[:, :, 0, :], v4[:, :, 1, :]

                def exponents(n):
                    earlier, later = halves(unit(h.b), n)
                    middle = earlier[:, :, (1 << n) - 1:1 << n].to_broadcast([P, S >> (n + 1), 1 << n])
                    to_earlier, to_later = halves(lev[n % 2][:, :], n)
                    if n >= 2:
                        dve.wait_ge(lev_ps, u * LEVELS + n - 1)
                    nc.vector.tensor_tensor(to_earlier, middle, earlier, ALU.subtract)
                    nc.vector.tensor_tensor(to_later, later, middle, ALU.subtract)
                    dve.drain().then_inc(diff_ready, 1)

                def factors(n):
                    dve.wait_ge(lev_exp, u * (LEVELS - 1) + n + 1)
                    earlier, later = halves(lev[n % 2][:, :], n)
                    for m in range(2):
                        rows = slice(HD * m, HD * m + HD)
                        nc.vector.tensor_tensor(halves(left[n % 2][m][:, :], n)[0][rows], earlier[rows],
                                                halves(unit(h.key), n)[0][rows], ALU.mult)
                    nc.vector.tensor_tensor(later, later, halves(unit(h.q), n)[1], ALU.mult)
                    dve.drain().then_inc(lev_ready, 1)

                def itself():
                    dve.wait_ge(lev_ps, u * LEVELS + LEVELS - 2)
                    nc.vector.memset(carrier[:, :], 0.0)
                    for m in range(2):
                        rows = slice(HD * m, HD * m + HD)
                        nc.vector.tensor_copy(left[1][m][rows, :], unit(h.key)[rows])
                    nc.vector.tensor_copy(lev[1][:, :], unit(h.q))
                    dve.drain().then_inc(lev_ready, 1)

                def take(n):
                    dve.wait_ge(lev_ps, u * LEVELS + n + 1)
                    nc.vector.memset(carrier[:, :], 0.0)
                    mask = k.hg_mask[:, n * P:(n + 1) * P].unsqueeze(1).to_broadcast([P, NT, P])
                    for m in range(2):
                        nc.vector.copy_predicated(att[m][:, :].rearrange("p (c t) -> p c t", t=P), mask,
                                                  k.bank[2 * (n % 2) + m][:, :].rearrange("p (c t) -> p c t", t=P))
                    dve.drain().then_inc(lev_done, 1)

                exponents(0)
                exponents(1)
                dve.wait_ge(grown, u + 1)
                for c in range(NT - 1):
                    for m in range(2):
                        rows = slice(HD * m, HD * m + HD)
                        added = k.bank[4][rows, c * P + HD * m:c * P + HD * m + HD]
                        if c == 0:
                            nc.vector.tensor_copy(states[rows, c, rows], added)
                        else:
                            nc.vector.scalar_tensor_tensor(
                                out=states[rows, c, rows], in0=states[rows, c - 1, rows],
                                scalar=unit(h.eb)[rows, c * P + P - 1:c * P + P], in1=added,
                                op0=ALU.mult, op1=ALU.add)
                    dve.drain()
                dve.drain().then_inc(states_ready, 1)
                factors(0)
                for n in range(2, LEVELS + 1):
                    if n == LEVELS:
                        itself()
                    else:
                        factors(n - 1)
                        if n < LEVELS - 1:
                            exponents(n)
                    take(n - 2)
                take(LEVELS - 1)
                dve.wait_ge(o_ps, u + 1)
                nc.vector.memset(carrier[:, :], 0.0)
                nc.vector.tensor_copy(out[:, :, ds(u * P, P)], k.bank[5][:, :].rearrange("p (c e) -> p c e", e=P))
                dve.drain().then_inc(o_sb, 1)


def silu_stage(nc, k, A, m_t):
    w2, ahead_loads = A["w_in_2"][0], k.ahead_loads
    FIRST = [Z2 + P * c for c in range(3)] + [SBZ + P * c for c in range(2)] + [HGZ + P * c for c in range(3)]
    h0, l0, p0, w0, c0 = (k.split.done[x] for x in ("hi_ready", "lo_ready", "projected", "w_in", "copied"))
    with Stage(nc, "silu") as st:
        places = [(k.ahead[:, :, P * f:P * f + P], k.ahead_lower[:, :, P * f:P * f + P]) for f in range(3)]
        places += [tuple(x[:, :, :] for x in st.overlaid(f"raw{f}", [P, NK, P])) for f in range(3, NK)]
        raws, lowers = zip(*places)
        up = [st.sb(f"up{p}", [P, NK, P], F32R)[:, :, :] for p in range(4)]
        w = [Split(up[f % 4], lowers[f]) for f in range(NK)]
        sg = st.sb("sg", [P, 2, S])
        w_in = [k.split["w_in"], k.split["late_in"]]
        hi_ready, lo_ready = k.split["hi_ready"], k.split["lo_ready"]
        z_ps, sg_ready, gated = k.split["projected"], st.sem("sg_ready"), st.sem("gated")
        block = st.block()

        @block.sync
        def _(sp):
            for f in range(3, NK):
                sp.dma_start(raws[f], column_tiles(w2, FIRST[f])).then_inc(w_in[0 if f < 5 else 1], 16)
            sp.wait_ge(z_ps, p0 + 3)
            load_ahead(sp, k, column_tiles(A["w_out_2"][0], 0, 512))

        @block.gpsimd
        def _(pool):
            for f in range(NK):
                pool.wait_ge(hi_ready, h0 + f + 1)
                split_lower(nc.gpsimd, raws[f], up[f % 4], w[f].lo).then_inc(lo_ready, 1)

        @block.tensor
        def _(pe):
            for f in range(NK):
                pe.wait_ge(lo_ready, l0 + f + 1)
                if f >= 4:
                    pe.wait_ge(gated, f - 3)
                for c in range(NK):
                    last = split_product(nc, k.bank[f % 4][:, :], w[f][:, c, :], k.x_parts[:, c, :],
                                         c == 0, c == NK - 1)
                last.then_inc(z_ps, 1)

        @block.scalar
        def _(act):
            for f in range(NK + 4):
                if f < NK:
                    if f == 0:
                        act.wait_ge(k.ahead_in, ahead_loads)
                    elif f == 3:
                        act.wait_ge(w_in[0], w0 + 32)
                    elif f == 5:
                        act.wait_ge(w_in[1], 16 + 48)
                    if f >= 4:
                        act.wait_ge(z_ps, p0 + f - 3)
                    nc.scalar.copy(up[f % 4], raws[f]).then_inc(hi_ready, 1)
                if f >= 4:
                    g = f - 4
                    act.wait_ge(z_ps, p0 + g + 1)
                    if g >= 2:
                        act.wait_ge(gated, g - 1)
                    nc.scalar.activation(sg[:, g % 2, :], k.bank[g % 4][:, :], ACT.Sigmoid).then_inc(sg_ready, 1)

        @block.vector
        def _(dve):
            for f in range(NK):
                dve.wait_ge(sg_ready, f + 1)
                nc.vector.tensor_tensor(sg[:, f % 2, :], sg[:, f % 2, :], k.bank[f % 4][:, :], ALU.mult)
                dve.drain()
                nc.vector.tensor_tensor(m_t[:, f, :], m_t[:, f, :], sg[:, f % 2, :], ALU.mult).then_inc(gated, 1)

    k.split.counted(hi_ready=NK, lo_ready=NK, projected=NK, w_in=32, copied=0)


def store_stage(nc, k, out):
    with Stage(nc, "store") as st:
        stored = st.sem("stored")
        block = st.block()

        @block.sync
        def _(sp):
            sp.dma_start(out[0].rearrange("(i p) n -> p i n", p=P), k.x[:, :, :]).then_inc(stored, 16)
            sp.wait_ge(stored, 16)


class Kernel:
    pass


def program(nc, A, out):
    k = Kernel()
    with ExitStack() as stack:
        def sb(name, shape, dt=F32):
            return stack.enter_context(nc.sbuf_tensor(name, shape, dt))

        k.bank = [stack.enter_context(nc.psum_tensor(f"bank{n}", [P, 512], F32)) for n in range(8)]
        k.const = sb("const", [P, C_END])
        k.hg_mask = sb("hg_mask", [P, 8 * P], I32)
        k.ident = k.const[:, C_ID:C_ID + P]
        k.neg_lam = sb("neg_lam", [P, 1])
        k.x, k.stats = sb("xs", [P, NT, D]), sb("stats", [P, NT, 12])
        k.gain, k.shift = sb("gain", [P, D]), sb("shift", [P, D])
        k.x_parts = Split(sb("x_hi", [P, NK, S], F32R)[:, :, :], sb("x_lo", [P, NK, S], F32R)[:, :, :])
        k.ahead, k.ahead_lower = overlaid(nc, stack, "ahead", [P, NK, 512])
        k.ahead_tiles, k.ahead_lower_tiles = (x[:, :, :].rearrange("p k (a b) -> p (k a) b", b=P)
                                              for x in (k.ahead, k.ahead_lower))
        k.ahead_in, k.ahead_loads = stack.enter_context(nc.semaphore("ahead_in")), 0
        k.z_band_handle = nc.dram_tensor("z_band", (8, P, 640), F32, kind="Internal")
        k.z_t5_handle = nc.dram_tensor("z_t5", (6, P, 1024), F32, kind="Internal")
        k.z_band, k.z_t5 = k.z_band_handle.ap(), k.z_t5_handle.ap()
        k.band_stored, k.t5_stored = (stack.enter_context(nc.semaphore(n)) for n in ("band_stored", "t5_stored"))
        k.band_table_in = stack.enter_context(nc.semaphore("band_table_in"))
        k.h1 = nc.dram_tensor("h1", (S, D), F32, kind="Internal").ap()
        k.y_slots = nc.dram_tensor("y_slots", (SLOTS + P, D), F32, kind="Internal").ap()

        k.norm = SharedSemaphores(nc, stack, "norm", NORM_SEMS)
        k.attention = SharedSemaphores(nc, stack, "attention", ATTENTION_SEMS)
        k.units = SharedSemaphores(nc, stack, "units", UNIT_SEMS)
        k.split = SharedSemaphores(nc, stack, "split", ("hi_ready", "lo_ready", "projected", "w_in", "late_in", "copied"))
        k.heads = SharedSemaphores(nc, stack, "heads", HEADS_SEMS)
        k.output = SharedSemaphores(nc, stack, "output", OUTPUT_SEMS)

        def merge_ahead(sp):
            load_merge(sp, A["w_in"][0], (A["w_branch_a"][0], A["w_branch_b"][0]), k.ahead_tiles, 0, k.ahead_in)
            k.ahead_loads += 64

        setup_stage(nc, k, A)
        layer_norm_stage(nc, "ln0", k, k.x, A["ln_in_g"], A["ln_in_b"], x_t=k.x_parts,
                         following=(A["ln1_g"][0], A["ln1_b"][0]))
        with ExitStack() as mixer:
            def msb(name, shape, dt=F32):
                return mixer.enter_context(nc.sbuf_tensor(name, shape, dt))

            oa_t, ob_t = (Split(msb(f"{n}_upper", [P, 4, S], F32R)[:, :, :], lower[:, :, :], whole[:, :, :])
                          for n in ("oa_t", "ob_t") for whole, lower in [overlaid(nc, mixer, n, [P, 4, S])])
            band_table = nc.alloc_sbuf_tensor_at("band_table", [P, 8, S], F32, offset=nc.sbuf_base - 4 * 8 * S)
            k.band_row, k.t5_row = msb("band_row", [8, 640]), msb("t5_row", [6, 1024])
            def band_ahead(sp):
                load_ahead(sp, k, column_tiles(A["w_in"][0], 5 * WA, 512))
                load_band_table(sp, k, band_table)

            with ExitStack() as s2:
                table = s2.enter_context(nc.sbuf_tensor("alibi_table", [P, 4, S], F32))
                oa = s2.enter_context(nc.sbuf_tensor("oa", [P, NT, WA], F32))
                tables_stage(nc, k, A, table)
                first_attention_stage(
                    nc, "diff", k, A["w_in"][0], 0, WA,
                    lambda u, m, first, n: table[:, ds(u, 1), first:first + n].rearrange("p o n -> p (o n)"),
                    True, lambda m: k.neg_lam[:, :] if m else None, oa)
                transpose_heads_stage(nc, "diffnorm", k, oa[:, :, :], oa_t, 4,
                                      A["subln_w"].rearrange("o p -> p o"), LN_EPS, 1.0 - LAM_INIT,
                                      ahead=band_ahead)
            with ExitStack() as s2:
                ob = s2.enter_context(nc.sbuf_tensor("ob", [P, NT, WA], F32))
                band_bias_stage(nc, k, band_table)
                first_attention_stage(
                    nc, "band", k, A["w_in"][0], 3 * WA, 4 * WA,
                    lambda u, m, first, n: band_table[:, ds(u * 2 + m, 1), first:first + n].rearrange("p o n -> p (o n)"),
                    False, lambda m: None, ob)
                transpose_heads_stage(nc, "bandt", k, ob[:, :, :], ob_t, ahead=merge_ahead)
            m_t, m_lower = overlaid(nc, mixer, "m_t", [P, NK, S])
            merge_stage(nc, k, A, oa_t, ob_t, m_t)
            output_stage(nc, "out1", k, A["w_out"][0], m_t, m_lower[:, :, :], k.x)
        layer_norm_stage(nc, "ln1", k, k.x, A["ln1_g"][0], A["ln1_b"][0], x_t=k.x_parts, save=k.h1,
                         following=(A["ln2_g"][0], A["ln2_b"][0]))
        with ExitStack() as moe:
            def rsb(name, shape, dt=F32):
                return moe.enter_context(nc.sbuf_tensor(name, shape, dt))

            r = Kernel()
            r.weight, r.expert = rsb("weight", [P, NT, TOPK]), rsb("expert", [P, MAX_BLOCKS])
            r.expert_i = rsb("expert_i", [P, MAX_BLOCKS + 1], I32)
            r.row, r.token = rsb("row", [P, MAX_BLOCKS], U32), rsb("token", [P, MAX_BLOCKS + 2], U32)
            r.bias = rsb("bias", [96, 3 * FF], BF16)
            r.ring, r.lower = zip(*(overlaid(nc, moe, f"piece{s}", [P, 4, 512]) for s in range(LOADED)))
            r.piece_in = [moe.enter_context(nc.semaphore(f"piece{s}_in")) for s in range(LOADED)]
            route_stage(nc, k, A, r)
            experts_stage(nc, k, A, r)
            combine_stage(nc, k, r, k.x)
        w2 = A["w_in_2"][0]
        layer_norm_stage(nc, "ln2", k, k.x, A["ln2_g"][0], A["ln2_b"][0], x_t=k.x_parts,
                         ahead=column_tiles(w2, KC2, 3 * P), following=(A["ln_g_2"][0], A["ln_b_2"][0]))
        with ExitStack() as mixer:
            def msb(name, shape, dt=F32):
                return mixer.enter_context(nc.sbuf_tensor(name, shape, dt))

            m_t, m_lower = overlaid(nc, mixer, "mixed_t", [P, NK, S])
            with ExitStack() as s2:
                def nsb(name, shape, dt=F32):
                    return s2.enter_context(nc.sbuf_tensor(name, shape, dt))

                n = Kernel()
                n.table = nsb("t5_table", [P, 6, BW])
                n.ks_t, n.kw_t, n.kc_t = nsb("ks_t", [P, S]), nsb("kw_t", [P, S]), nsb("kc_t", [P, N_CMP])
                n.vs, n.vw, n.vc = nsb("vs", [P, NT, P]), nsb("vw", [P, NT, P]), nsb("vc", [N_CMP, P])
                n.gates = nsb("gates", [P, NT, 18])
                nsa_keys_stage(nc, k, A, n, m_t[:, :, :])
                o_nsa = nsb("o_nsa", [P, NT, 384])
                nsa_attention_stage(nc, k, A, n, o_nsa[:, :, :])
                transpose_heads_stage(nc, "nsat", k, o_nsa[:, :, :], m_t[:, 0:3, :],
                                      ahead=lambda sp: load_ahead(sp, k, column_tiles(w2, SBQ, 512)))
            stick_breaking_stage(nc, k, A, m_t[:, 3:5, :])
            with ExitStack() as s2:
                def hsb(name, shape):
                    return s2.enter_context(nc.sbuf_tensor(name, shape, F32))

                h = Kernel()
                h.q, h.key, h.b, h.eb, h.kd, h.kd_t, h.qe = (
                    hsb(f"hgrn_{x}", [P, HG_UNITS, S]) for x in ("q", "key", "b", "eb", "kd", "kd_t", "qe"))
                h.v = hsb("hg_v", [P, NT, HG_W])
                hgrn_gates_stage(nc, k, A, h)
                o_hg = hsb("o_hg", [P, NT, HG_W])
                hgrn_stage(nc, k, h, o_hg)
                transpose_heads_stage(nc, "hgt", k, o_hg[:, :, :], m_t[:, 5:8, :], 6,
                                      A["hg_norm_w_2"][0].rearrange("(c p) -> p c", p=P), RMS_EPS,
                                      ahead=lambda sp: load_ahead(sp, k, column_tiles(w2, Z2, HG_W)))
            silu_stage(nc, k, A, m_t)
            output_stage(nc, "out2", k, A["w_out_2"][0], m_t, m_lower[:, :, :], k.x)
        layer_norm_stage(nc, "ln3", k, k.x, A["ln_g_2"][0], A["ln_b_2"][0])
        store_stage(nc, k, out)


def constants():
    import numpy as np

    p, f = np.arange(P)[:, None], np.arange(P)[None, :]
    c = np.zeros((P, C_END), np.float32)
    c[:, C_ID:C_ID + P] = p == f
    c[:, C_GT:C_GT + P] = p > f
    c[:, C_LT:C_LT + P] = p < f
    c[:, C_ONE:C_ONE + P] = 1.0
    c[:, C_IOTA:C_IOTA + P] = f
    c[:, C_DIST:C_DIST + S] = -np.abs(p - np.arange(S)[None, :] + S - P)
    c[:, C_P] = np.arange(P)
    c[:, C_P + 1] = np.arange(P) % NE
    c[:, C_P + 2] = np.arange(P) + SLOTS + 1
    mask = np.zeros((P, 8, P), np.int32)
    mask[:, 7] = p == f
    for n in range(7):
        mask[:, n] = ((p ^ f) >> n == 1) & (f > p)
    n = 511 - np.arange(512)
    large = 16 + (np.log(np.maximum(n, 1).astype(np.float32) / np.float32(16.0))
                  / np.float32(np.log(8.0)) * np.float32(16.0)).astype(np.int32)
    bucket = np.where(n < 16, n, np.clip(large, 0, 31))
    onehot = (np.arange(32)[:, None] == bucket[None, :]).astype(np.float32)
    return {"c_f32": c, "c_mask": mask.reshape(P, 8 * P), "c_onehot": onehot}


def kernel(**inputs):
    import numpy as np
    import concourse.bacc as bacc
    from concourse import mybir
    from concourse.bass_utils import run_bass_kernel_spmd

    nc = bacc.Bacc("TRN2", target_bir_lowering=False, num_devices=1)
    arrays, A = {}, {}
    for name, value in {**inputs, **constants()}.items():
        a = np.ascontiguousarray(value)
        arrays[f"in_{name}_dram"] = a
        A[name] = nc.dram_tensor(f"in_{name}_dram", a.shape, mybir.dt.from_np(a.dtype), kind="ExternalInput").ap()
    out = nc.dram_tensor("out_0_dram", (1, S, D), mybir.dt.float32, kind="ExternalOutput").ap()
    program(nc, A, out)
    results = run_bass_kernel_spmd(nc, [arrays], core_ids=[0])
    return results.results[0]["out_0_dram"]
```
